# Optimizing a Trainium2 kernel written in Bass

```python
import math
import jax, jax.numpy as jnp
from jax import lax
import numpy as np

D_MODEL = 1024
BATCH = 1
SEQ = 256
DEPTH = 1
DEC_BATCH = 1
DEC_SEQ = 512
PAST_LEN = 128

GRID_W = 64
NA_WIDTH = D_MODEL // 2
NA_HEAD_DIM = 64
NA_HEADS = NA_WIDTH // NA_HEAD_DIM
NA_KH = 8
NA_KW = 16
NA_QB = 16
NA_KB = 32
RWKV_WIDTH = D_MODEL - NA_WIDTH
RWKV_HEAD_DIM = 64
RWKV_HEADS = RWKV_WIDTH // RWKV_HEAD_DIM
DECAY_LORA = 64
ICLR_LORA = 64
GATE_LORA = 128
RWKV_SPLITS = (RWKV_WIDTH, RWKV_WIDTH, RWKV_WIDTH, DECAY_LORA, DECAY_LORA, ICLR_LORA, ICLR_LORA, GATE_LORA)
RWKV_IN = sum(RWKV_SPLITS)
IN_WIDTH = 3 * NA_WIDTH + RWKV_IN
N_GROUPS = 4
EXPERTS_PER_GROUP = 8
N_EXPERTS = N_GROUPS * EXPERTS_PER_GROUP
EXPERT_HIDDEN = 512
TOP_K_IN_GROUP = 2
MOE_BLOCK = 256
NORM_EPS = 1e-6
LNX_EPS = 64e-5
MASK_VALUE = -1e30

kernel_name = 'hybrid_na_rwkv7_hmoe_encoder'

def rms_norm(x, g):
    xf = x.astype(jnp.float32)
    y = xf * lax.rsqrt(jnp.mean(xf * xf, axis=-1, keepdims=True) + NORM_EPS)
    return (y * g.astype(jnp.float32)).astype(x.dtype)

def _na_column_tables():
    nqb = GRID_W // NA_QB
    qcols = np.arange(GRID_W).reshape(nqb, NA_QB)
    band_start = np.clip(np.arange(nqb) * NA_QB - NA_KW // 2, 0, GRID_W - NA_KB)
    colidx = band_start[:, None] + np.arange(NA_KB)[None, :]
    win_start = np.clip(qcols - NA_KW // 2, 0, GRID_W - NA_KW)
    kc = colidx[:, None, :]
    valid = (kc >= win_start[..., None]) & (kc < win_start[..., None] + NA_KW)
    dxidx = np.clip(kc - qcols[..., None] + NA_KW - 1, 0, 2 * NA_KW - 2)
    return colidx.astype(np.int32), valid, dxidx.astype(np.int32)

def neighbourhood_attention(q, k, v, rpb):
    bsz, seq, _ = q.shape
    rows = seq // GRID_W
    kh = min(NA_KH, rows)
    nqb = GRID_W // NA_QB
    colidx, valid, dxidx = _na_column_tables()
    shp = (bsz, rows, GRID_W, NA_HEADS, NA_HEAD_DIM)
    q, k, v = q.reshape(shp), k.reshape(shp), v.reshape(shp)
    rpb_t = jnp.transpose(rpb[:, :, dxidx], (0, 2, 3, 1, 4)).astype(jnp.float32)
    col_mask = jnp.asarray(np.where(valid, 0.0, MASK_VALUE), jnp.float32)[:, :, None, :]
    colidx_j = jnp.asarray(colidx)
    scale = NA_HEAD_DIM ** -0.5

    def row_step(args):
        i, q_row = args
        rs = jnp.clip(i - kh // 2, 0, rows - kh)
        k_r = lax.dynamic_slice_in_dim(k, rs, kh, axis=1)[:, :, colidx_j]
        v_r = lax.dynamic_slice_in_dim(v, rs, kh, axis=1)[:, :, colidx_j]
        dy = rs + jnp.arange(kh) - i + (NA_KH - 1)
        bias = rpb_t[:, :, :, dy, :]
        qb = q_row.reshape(bsz, nqb, NA_QB, NA_HEADS, NA_HEAD_DIM)
        s = jnp.einsum('bnqhd,bmnkhd->bhnqmk', qb, k_r).astype(jnp.float32) * scale + bias + col_mask
        p = jax.nn.softmax(s.reshape(bsz, NA_HEADS, nqb, NA_QB, kh * NA_KB), axis=-1).reshape(s.shape)
        o = jnp.einsum('bhnqmk,bmnkhd->bnqhd', p.astype(v.dtype), v_r)
        return o.reshape(bsz, GRID_W, NA_WIDTH)

    out = lax.map(row_step, (jnp.arange(rows), jnp.moveaxis(q, 1, 0)))
    return jnp.moveaxis(out, 0, 1).reshape(bsz, seq, NA_WIDTH)

def token_shift(z, mu):
    prev = jnp.pad(z[:, :-1], ((0, 0), (1, 0), (0, 0)))
    nxt = jnp.pad(z[:, 1:], ((0, 0), (0, 1), (0, 0)))
    return z + mu[0] * (prev - z) + mu[1] * (nxt - z)

def wkv7_scan(r, w, k, v, a, b, reverse):
    bsz, seq, nh, n = r.shape

    def step(S, inp):
        r_t, w_t, k_t, v_t, a_t, b_t = inp
        sa = jnp.einsum('bhvk,bhk->bhv', S, a_t)
        S = S * w_t[:, :, None, :] + sa[..., None] * b_t[:, :, None, :] + v_t[..., None] * k_t[:, :, None, :]
        return S, jnp.einsum('bhvk,bhk->bhv', S, r_t)

    S0 = jnp.zeros((bsz, nh, n, n), jnp.float32)
    xs = tuple(jnp.moveaxis(t, 1, 0) for t in (r, w, k, v, a, b))
    _, ys = lax.scan(step, S0, xs, reverse=reverse)
    return jnp.moveaxis(ys, 0, 1)

def rwkv7_direction(rh, k, vh, kk, xw, xa, w0, w2, a0, a2, k_a, r_k, reverse):
    bsz, seq, _ = k.shape
    heads = lambda t: t.reshape(bsz, seq, RWKV_HEADS, RWKV_HEAD_DIM)
    logw = -jax.nn.softplus(-(w0 + jnp.tanh(xw) @ w2)) - 0.5
    decay = jnp.exp(-jnp.exp(logw))
    a = jax.nn.sigmoid(a0 + xa @ a2)
    kdh = heads(k * (1.0 + (a - 1.0) * k_a))
    wkv = wkv7_scan(rh, heads(decay), kdh, vh, -kk, kk * heads(a), reverse)
    bonus = jnp.sum(rh * kdh * r_k, axis=-1, keepdims=True) * vh
    return wkv, bonus

def rwkv7_bidirectional(z, mu, w0, w2, a0, a2, g2, k_k, k_a, r_k, lnx_g, lnx_b):
    bsz, seq, _ = z.shape
    heads = lambda t: t.reshape(bsz, seq, RWKV_HEADS, RWKV_HEAD_DIM)
    z = token_shift(z.astype(jnp.float32), mu.astype(jnp.float32))
    cuts = [int(c) for c in np.cumsum(RWKV_SPLITS)[:-1]]
    r, k, v, xw_f, xw_b, xa_f, xa_b, xg = jnp.split(z, cuts, axis=-1)
    g = jax.nn.sigmoid(xg) @ g2.astype(jnp.float32)
    kk = heads(k * k_k)
    kk = kk / jnp.maximum(jnp.sqrt(jnp.sum(kk * kk, axis=-1, keepdims=True)), 1e-12)
    rh, vh = heads(r), heads(v)
    wkv_f, bonus_f = rwkv7_direction(rh, k, vh, kk, xw_f, xa_f, w0[0], w2[0], a0[0], a2[0], k_a, r_k, False)
    wkv_b, bonus_b = rwkv7_direction(rh, k, vh, kk, xw_b, xa_b, w0[1], w2[1], a0[1], a2[1], k_a, r_k, True)
    wkv = wkv_f + wkv_b
    mean = jnp.mean(wkv, axis=-1, keepdims=True)
    var = jnp.mean(jnp.square(wkv - mean), axis=-1, keepdims=True)
    y = ((wkv - mean) * lax.rsqrt(var + LNX_EPS)).reshape(bsz, seq, RWKV_WIDTH) * lnx_g + lnx_b
    y = y + (bonus_f + bonus_b).reshape(bsz, seq, RWKV_WIDTH)
    return y * g

def hmoe(h, rg_w, rg_b, re_w, re_b, w1, w3, w2):
    bsz, seq, d = h.shape
    hf = h.reshape(-1, d)
    n_tok = hf.shape[0]
    pg = jax.nn.softmax((hf @ rg_w + rg_b).astype(jnp.float32), axis=-1)
    gsel = jnp.argmax(pg, axis=-1)
    gw = jnp.max(pg, axis=-1, keepdims=True)
    le = (hf @ re_w + re_b).astype(jnp.float32).reshape(n_tok, N_GROUPS, EXPERTS_PER_GROUP)
    le = jnp.take_along_axis(le, gsel[:, None, None], axis=1)[:, 0]
    top_p, top_i = lax.top_k(jax.nn.softmax(le, axis=-1), TOP_K_IN_GROUP)
    top_p = top_p / jnp.sum(top_p, axis=-1, keepdims=True)
    eid = (gsel[:, None] * EXPERTS_PER_GROUP + top_i).reshape(-1)
    wts = (gw * top_p).reshape(-1)
    tok = jnp.repeat(jnp.arange(n_tok, dtype=jnp.int32), TOP_K_IN_GROUP)
    n_slot = eid.shape[0]
    order = jnp.argsort(eid)
    se = eid[order]
    counts = jnp.bincount(eid, length=N_EXPERTS)
    start = jnp.cumsum(counts) - counts
    pcounts = (counts + MOE_BLOCK - 1) // MOE_BLOCK * MOE_BLOCK
    pend = jnp.cumsum(pcounts)
    pstart = pend - pcounts
    pos = pstart[se] + jnp.arange(n_slot) - start[se]
    n_blocks = -(-n_slot // MOE_BLOCK) + N_EXPERTS
    buf_tok = jnp.zeros((n_blocks * MOE_BLOCK,), jnp.int32).at[pos].set(tok[order])
    buf_w = jnp.zeros((n_blocks * MOE_BLOCK,), jnp.float32).at[pos].set(wts[order])
    block_exp = jnp.minimum(jnp.searchsorted(pend, jnp.arange(n_blocks) * MOE_BLOCK, side='right'), N_EXPERTS - 1)

    def block_step(args):
        t, e, wt = args
        xb = hf[t]
        hid = jax.nn.silu(xb @ w1[e]) * (xb @ w3[e])
        return (hid @ w2[e]) * wt[:, None].astype(hf.dtype)

    yb = lax.map(block_step, (buf_tok.reshape(n_blocks, MOE_BLOCK), block_exp, buf_w.reshape(n_blocks, MOE_BLOCK)))
    out = jnp.zeros_like(hf).at[buf_tok].add(yb.reshape(-1, d))
    return out.reshape(bsz, seq, d)

def encoder_layer(x, c, ada_w, ada_b, norm1_g, norm2_g, w_in, na_rpb, rwkv_mu, rwkv_w0, rwkv_w2,
                  rwkv_a0, rwkv_a2, rwkv_g2, rwkv_kk, rwkv_ka, rwkv_rk, rwkv_lnx_g, rwkv_lnx_b, w_out,
                  router_g_w, router_g_b, router_e_w, router_e_b, exp_w1, exp_w3, exp_w2):
    mod = (jax.nn.silu(c) @ ada_w + ada_b)[:, None, :]
    sh1, sc1, g1, sh2, sc2, g2 = jnp.split(mod, 6, axis=-1)
    h = rms_norm(x, norm1_g) * (1 + sc1) + sh1
    z = h @ w_in
    q_a, k_a, v_a, z_r = jnp.split(z, [NA_WIDTH, 2 * NA_WIDTH, 3 * NA_WIDTH], axis=-1)
    att = neighbourhood_attention(q_a, k_a, v_a, na_rpb)
    rec = rwkv7_bidirectional(z_r, rwkv_mu, rwkv_w0, rwkv_w2, rwkv_a0, rwkv_a2, rwkv_g2,
                              rwkv_kk, rwkv_ka, rwkv_rk, rwkv_lnx_g, rwkv_lnx_b).astype(x.dtype)
    x = x + g1 * (jnp.concatenate([att, rec], axis=-1) @ w_out)
    h = rms_norm(x, norm2_g) * (1 + sc2) + sh2
    x = x + g2 * hmoe(h, router_g_w, router_g_b, router_e_w, router_e_b, exp_w1, exp_w3, exp_w2)
    return x

def setup_inputs(seed: int = 0) -> dict:
    key = jax.random.key(seed)
    ks = jax.random.split(key, 32)
    nrm = lambda i, shape, s: jax.random.normal(ks[i], shape, jnp.float32) * s
    L, D = DEPTH, D_MODEL
    return {
        'x_prompt': nrm(0, (BATCH, SEQ, D), 1.0),
        'x_sample': nrm(1, (DEC_BATCH, DEC_SEQ, D), 1.0),
        'c_prompt': nrm(2, (BATCH, D), 1.0),
        'c_sample': nrm(3, (DEC_BATCH, D), 1.0),
        'ada_w': nrm(4, (L, D, 6 * D), 0.5 * D ** -0.5),
        'ada_b': nrm(5, (L, 6 * D), 0.02),
        'norm1_g': 1.0 + nrm(6, (L, D), 0.05),
        'norm2_g': 1.0 + nrm(7, (L, D), 0.05),
        'w_in': nrm(8, (L, D, IN_WIDTH), D ** -0.5),
        'na_rpb': nrm(9, (L, NA_HEADS, 2 * NA_KH - 1, 2 * NA_KW - 1), 0.1),
        'rwkv_mu': jax.random.uniform(ks[10], (L, 2, RWKV_IN), jnp.float32, 0.0, 0.5),
        'rwkv_w0': jax.random.uniform(ks[11], (L, 2, RWKV_WIDTH), jnp.float32, -6.5, -1.5),
        'rwkv_w2': nrm(12, (L, 2, DECAY_LORA, RWKV_WIDTH), 0.1 * DECAY_LORA ** -0.5),
        'rwkv_a0': nrm(13, (L, 2, RWKV_WIDTH), 0.1),
        'rwkv_a2': nrm(14, (L, 2, ICLR_LORA, RWKV_WIDTH), 0.1 * ICLR_LORA ** -0.5),
        'rwkv_g2': nrm(15, (L, GATE_LORA, RWKV_WIDTH), GATE_LORA ** -0.5),
        'rwkv_kk': 0.85 + nrm(16, (L, RWKV_WIDTH), 0.05),
        'rwkv_ka': 1.0 + nrm(17, (L, RWKV_WIDTH), 0.05),
        'rwkv_rk': nrm(18, (L, RWKV_HEADS, RWKV_HEAD_DIM), 0.1),
        'rwkv_lnx_g': 1.0 + nrm(19, (L, RWKV_WIDTH), 0.05),
        'rwkv_lnx_b': nrm(20, (L, RWKV_WIDTH), 0.02),
        'w_out': nrm(21, (L, D, D), D ** -0.5),
        'router_g_w': nrm(22, (L, D, N_GROUPS), D ** -0.5),
        'router_g_b': nrm(23, (L, N_GROUPS), 0.01),
        'router_e_w': nrm(24, (L, D, N_EXPERTS), D ** -0.5),
        'router_e_b': nrm(25, (L, N_EXPERTS), 0.01),
        'exp_w1': nrm(26, (L, N_EXPERTS, D, EXPERT_HIDDEN), D ** -0.5),
        'exp_w3': nrm(27, (L, N_EXPERTS, D, EXPERT_HIDDEN), D ** -0.5),
        'exp_w2': nrm(28, (L, N_EXPERTS, EXPERT_HIDDEN, D), EXPERT_HIDDEN ** -0.5),
        'final_g': 1.0 + nrm(29, (D,), 0.05),
    }

def reference(x_prompt, x_sample, c_prompt, c_sample, ada_w, ada_b, norm1_g, norm2_g, w_in, na_rpb,
              rwkv_mu, rwkv_w0, rwkv_w2, rwkv_a0, rwkv_a2, rwkv_g2, rwkv_kk, rwkv_ka, rwkv_rk,
              rwkv_lnx_g, rwkv_lnx_b, w_out, router_g_w, router_g_b, router_e_w, router_e_b,
              exp_w1, exp_w3, exp_w2, final_g):
    def trunk(x, c):
        for l in range(DEPTH):
            x = encoder_layer(x, c, ada_w[l], ada_b[l], norm1_g[l], norm2_g[l], w_in[l], na_rpb[l],
                              rwkv_mu[l], rwkv_w0[l], rwkv_w2[l], rwkv_a0[l], rwkv_a2[l], rwkv_g2[l],
                              rwkv_kk[l], rwkv_ka[l], rwkv_rk[l], rwkv_lnx_g[l], rwkv_lnx_b[l], w_out[l],
                              router_g_w[l], router_g_b[l], router_e_w[l], router_e_b[l],
                              exp_w1[l], exp_w3[l], exp_w2[l])
        return rms_norm(x, final_g)

    y_prompt = trunk(x_prompt, c_prompt)
    y_sample = trunk(x_sample, c_sample)
    return (y_prompt, y_sample)


_drawn_inputs = setup_inputs


def setup_inputs(seed=0):
    import zlib

    import numpy as np

    out = dict(_drawn_inputs(seed))
    spreads = {}
    factors = {'norm1_g': 3.697,
     'norm2_g': 2.914,
     'na_rpb': 8.0,
     'rwkv_w2': 8.0,
     'rwkv_a0': 7.772,
     'rwkv_a2': 7.573,
     'rwkv_kk': 3.478,
     'rwkv_ka': 3.449,
     'rwkv_lnx_g': 6.252,
     'rwkv_lnx_b': 24.076,
     'router_g_b': 8.0,
     'router_e_b': 6.728}
    for name, (base, spread) in spreads.items():
        noise = np.random.default_rng([zlib.crc32(name.encode()), seed]).standard_normal(out[name].shape)
        drawn = base * np.exp(spread * noise) if base else spread * noise
        out[name] = __import__('jax').numpy.asarray(drawn.astype(out[name].dtype))
    for name, factor in factors.items():
        out[name] = (out[name] * factor).astype(out[name].dtype)
    return out
```

```python
from contextlib import ExitStack

import numpy as np

import concourse.bass as bass
import concourse.mybir as mybir

f32 = mybir.dt.float32
f16 = mybir.dt.float16
i32 = mybir.dt.int32
u32 = mybir.dt.uint32
ALU = mybir.AluOpType
ACT = mybir.ActivationFunctionType
AX = mybir.AxisListType.X

P = 128
D = 1024
KD = D // P
T_S, T_P = 512, 256
NT_S, NT_P = T_S // P, T_P // P
NT = NT_S + NT_P
TOK = NT * P
W = 512
HD = 64
NH = W // HD
NPAIR = NH // 2
GW = 64
QB, KB = 16, 32
NQB = GW // QB
NZ = 15
ZLORA = 12
NE, EPG, NG = 32, 8, 4
HID = 512
KH = HID // P
BLK = 64
MAX_OVER = 2 * TOK // BLK
NBLK = NE + MAX_OVER
EPS = 1e-6
LNX_EPS = 64e-5
DECAY = float(np.exp(-0.5))
BIG = 3.0e38
U_SCALE = 2048.0
LEVELS = 7


class Own:

    def __init__(self, eng, sem):
        self.eng, self.sem, self.n = eng, sem, 0

    def done(self, ins):
        self.n += 1
        ins.then_inc(self.sem, 1)
        return self.n

    def wait(self, value):
        self.eng.wait_ge(self.sem, value)

    def link(self, ins):
        self.wait(self.done(ins))


def constants():
    j, t = np.arange(P)[:, None], np.arange(P)[None, :]
    half = (np.arange(P) < P // 2).astype(np.float32)
    c = {}
    c["c_ident"] = np.eye(P, dtype=np.float32)
    c["c_ident16"] = np.eye(P, dtype=np.float16)
    c["c_tri"] = np.stack([(j <= t) - half[:, None], (j >= t) - (1 - half)[:, None]]).astype(np.float32).transpose(1, 0, 2)
    c["c_mid"] = np.stack([np.stack([half, 1 - half], 1), np.stack([1 - half, half], 1)]).astype(np.float32).transpose(1, 0, 2)
    seen = [np.concatenate([j < t, j <= t], 1), np.concatenate([j > t, j >= t], 1)]
    c["c_seen"] = np.stack([np.concatenate([m, m], 1) for m in seen]).astype(np.float32).transpose(1, 0, 2)
    c["c_pair"] = np.kron(np.eye(2), np.ones((HD, HD))).astype(np.float32)
    sel = np.zeros((P, 3, P), np.float32)
    for g in range(2):
        sel[g::32, g] = 1
    sel[0, 2, 0:2] = 1
    c["c_sel"] = sel
    before = np.zeros((P, P), np.float32)
    before[j < t] = 1
    c["c_before"] = before
    c["c_eps"] = np.tile(np.array([EPS, LNX_EPS], np.float32), (P, 1))
    c["c_ones"] = np.ones((P, P), np.float32)
    qc = np.arange(QB)
    mask = np.zeros((3, P, KB), np.float32)
    for kind, n in enumerate((0, 1, 3)):
        cols = n * QB + qc
        start = np.clip(n * QB - QB // 2, 0, GW - KB)
        win = np.clip(cols - 8, 0, GW - 16)
        kc = start + np.arange(KB)
        ok = (kc >= win[:, None]) & (kc < win[:, None] + 16)
        mask[kind] = np.tile(np.where(ok, 0.0, -1e30), (8, 1))
    c["c_window"] = np.ascontiguousarray(mask.transpose(1, 0, 2))
    e = np.arange(NE, dtype=np.float32)
    c["c_expert"] = np.tile(e, (P, 1))
    c["c_fall8"] = np.tile(8.0 - np.arange(8, dtype=np.float32), (P, 1))
    c["c_first"] = np.tile(e * BLK, (P, 1))
    c["c_place"] = np.arange(P, dtype=np.float32)[:, None].copy()
    c["c_token"] = (np.arange(NT)[None, :] * P + np.arange(P)[:, None]).astype(np.int32)
    return {k: np.ascontiguousarray(v) for k, v in c.items()}


def group(t):
    return 0 if t < NT_S else 1


def band(n):
    return min(max(n * QB - QB // 2, 0), GW - KB)


def build(nc, A, O, upto=7):
    ctx = ExitStack()
    with ctx:
        sems = {}

        def sem(name):
            if name not in sems:
                sems[name] = nc.alloc_semaphore(name=name)
            return sems[name]

        def dram(name, shape, dt=f32):
            return nc.dram_tensor(name, shape, dt, kind="Internal").ap()

        ARENA = 53200
        arena = ctx.enter_context(nc.sbuf_tensor("arena", [P, ARENA], f32))
        top = [0]

        def take(n):
            at = top[0]
            top[0] += n
            assert top[0] <= ARENA, top[0]
            return arena[:, at:at + n]

        bank = [ctx.enter_context(nc.psum_tensor(f"bank{i}", [P, 512], f32))[:, :] for i in range(8)]

        v_dram = dram("v_scratch", [TOK, W])
        dir_dram = dram("direction_scratch", [2, 3, NT, P, W])
        h2_dram = dram("h2_scratch", [TOK, D])
        slot_dram = dram("slot_token", [NBLK * BLK, 1], i32)
        y_dram = dram("slot_out", [NBLK * BLK, D])
        over_dram = dram("overflow_list", [MAX_OVER, 2], i32)

        ident = take(P)
        eps = take(2)
        modp = take(6 * D)
        catT = take(KD * TOK).rearrange("p (c t) -> p c t", c=KD)
        hT = catT
        base5 = top[0]
        ident16 = take(P // 2).bitcast(f16)
        kk_row, ka_row, rk_row, lg_row, lb_row = (take(W) for _ in range(5))
        rkv = take(3 * NT * W).rearrange("p (q t c) -> p q t c", q=3, t=NT)
        kkn = take(NT * W).rearrange("p (t c) -> p t c", t=NT)
        gate = take(NT * W).rearrange("p (t c) -> p t c", t=NT)
        bonus = take(NT * NH).rearrange("p (t h) -> p t h", t=NT)
        base4 = top[0]
        qT = take(NPAIR * TOK).rearrange("p (c t) -> p c t", c=NPAIR)
        kT = take(NPAIR * TOK).rearrange("p (c t) -> p c t", c=NPAIR)
        base3 = top[0]

        top[0] = base3
        adaw = [take(KD * 512).rearrange("p (k n) -> p k n", k=KD) for _ in range(2)]
        NWIN = 3
        winb = [take(KD * P).rearrange("p (k n) -> p k n", k=KD) for _ in range(NWIN)]
        lz = take(3 * TOK).rearrange("p (c t) -> p c t", c=3)
        sel = take(3 * P).rearrange("p (g c) -> p g c", g=3)
        mu = take(NZ * 3).rearrange("p (c m) -> p c m", m=3)
        cT = take(KD * 2).rearrange("p (k g) -> p k g", g=2)
        siluT = take(KD * 32).rearrange("p (k m) -> p k m", k=KD)
        stat = take(NT * 4).rearrange("p (t m) -> p t m", t=NT)
        at_rkv = top[0]
        top[0] = base5 + P // 2 + 5 * W
        xb = [take(D) for _ in range(2)]
        hb = [take(D) for _ in range(2)]
        rows = take(4 * D).rearrange("p (g m d) -> p g m d", g=2, m=2)
        n1_row = take(D)
        sq1 = take(D)
        top[0] = base5 + P // 2 + 5 * W + 3 * NT * W
        adab = [take(512) for _ in range(2)]
        zs = [take(TOK) for _ in range(2)]
        top[0] = at_rkv

        x_tile = [A["x_sample"][0, t * P:(t + 1) * P, :] for t in range(NT_S)] + \
                 [A["x_prompt"][0, t * P:(t + 1) * P, :] for t in range(NT_P)]
        ada_v = A["ada_w"][0].rearrange("(k p) n -> p k n", p=P)
        win_v = A["w_in"][0].rearrange("(k p) n -> p k n", p=P)
        ZCOL = 3 * W
        order = [("z", ZLORA + i, ZCOL + (ZLORA + i) * P) for i in range(3)]
        order += [("z", i, ZCOL + i * P) for i in range(ZLORA)]
        order += [("q", i, i * P) for i in range(NPAIR)] + [("k", i, W + i * P) for i in range(NPAIR)]
        ring = [("ada", c) for c in range(4)] + [("wv", 0)] + [("ada", c) for c in range(4, 12)]

        def sp_phase1(sp):
            small = [(ident, A["c_ident"]), (eps, A["c_eps"]), (ident16, A["c_ident16"]),
                     (kk_row, A["rwkv_kk"][0].partition_broadcast(P)), (ka_row, A["rwkv_ka"][0].partition_broadcast(P)),
                     (rk_row, A["rwkv_rk"][0].partition_broadcast(P)), (lg_row, A["rwkv_lnx_g"][0].partition_broadcast(P)),
                     (lb_row, A["rwkv_lnx_b"][0].partition_broadcast(P)),
                     (n1_row, A["norm1_g"][0].partition_broadcast(P)), (sel, A["c_sel"]), (mu[:, :, 0:2], A["mu"]),
                     (cT, A["c_cols"])]
            sp.dma_start(small[-1][0], small[-1][1]).then_inc(sem("consts_in"), 16)

            def wide(i):
                kind, c = ring[i]
                if i >= 2 and ring[i - 2][0] == "ada":
                    sp.wait_ge(sem("mod_mm"), ring[i - 2][1] + 1)
                elif i >= 2:
                    sp.wait_ge(sem("v_mm"), NT)
                s = sem(f"wide_in{i % 2}")
                if kind == "ada":
                    sp.dma_start(adaw[i % 2], ada_v[:, :, c * 512:(c + 1) * 512]).then_inc(s, 16)
                    sp.dma_start(adab[i % 2][0:1, :], A["ada_b"][0:1, c * 512:(c + 1) * 512]).then_inc(s, 16)
                else:
                    sp.dma_start(adaw[i % 2], win_v[:, :, 2 * W:3 * W]).then_inc(s, 32)

            def win(i):
                if i >= NWIN:
                    sp.wait_ge(sem("proj_mm"), i - NWIN + 1)
                c = order[i][2]
                sp.dma_start(winb[i % NWIN], win_v[:, :, c:c + P]).then_inc(sem(f"win_in{i % NWIN}"), 16)

            def x(t):
                if t >= 2:
                    sp.wait_ge(sem("x_used"), t - 1)
                sp.dma_start(xb[t % 2], x_tile[t]).then_inc(sem(f"x_in{t % 2}"), 16)

            wide(0)
            for dst, src in small[:-1]:
                sp.dma_start(dst, src).then_inc(sem("consts_in"), 16)
            x(0)
            x(1)
            for i in range(1, 4):
                wide(i)
            for i in range(NWIN):
                win(i)
            for t in range(2, NT):
                x(t)
            wide(4)
            for i in range(NWIN, len(order)):
                win(i)
            for i in range(5, len(ring)):
                wide(i)

        def pool_phase1(pool):
            nc.gpsimd.memset(siluT, 0.0).then_inc(sem("silu_zero"), 1)

        def act_phase1(act):
            own = Own(act, sem("act_own"))
            act.wait_ge(sem("consts_in"), 16 * 12)
            act.wait_ge(sem("silu_zero"), 1)
            nc.scalar.activation(siluT[:, :, 0:2], cT, ACT.Silu).then_inc(sem("silu_ready"), 1)

            def mod(i, at):
                act.wait_ge(sem("mod_mm"), i + 1)
                nc.scalar.copy(modp[:, at * 512:(at + 1) * 512], bank[i % 2]).then_inc(sem("mod_ready"), 1)

            for i in range(4):
                mod(i, i)

            def rms(t):
                act.wait_ge(sem(f"x_in{t % 2}"), 16 * (t // 2 + 1))
                if t:
                    own.wait(own.n)
                own.link(nc.scalar.activation(sq1, xb[t % 2], ACT.Square, scale=1.0 / 32.0, accum_out=stat[:, t, 0:1]))
                own.done(nc.scalar.activation(stat[:, t, 1:2], stat[:, t, 0:1], ACT.Sqrt, bias=eps[:, 0:1]))

            rms(0)
            rms(1)
            for t in range(NT):
                act.wait_ge(sem("hT_mm"), 2 * t + 1)
                nc.scalar.copy(hT[:, 0:4, t * P:(t + 1) * P], bank[2].rearrange("p (k c) -> p k c", k=4)).then_inc(sem("hT_act"), 1)
                if t + 2 < NT:
                    rms(t + 2)
            for i, (kind, c, _) in enumerate(order):
                b0, b1 = bank[4 + i % 2], bank[6 + i % 2]
                act.wait_ge(sem("proj_mm"), i + 1)
                if kind in "qk":
                    dst = qT if kind == "q" else kT
                    s = float(HD) ** -0.5 if kind == "q" else 1.0
                    for lo, hi, src in ((0, T_S, b0), (T_S, TOK, b1[:, 0:T_P])):
                        to = dst[:, c, lo:hi]
                        if kind == "q":
                            to = to.rearrange("p (n r c) -> p r n c", n=NQB, c=QB)
                            src = src.rearrange("p (r n c) -> p r n c", n=NQB, c=QB)
                        nc.scalar.mul(to, src, s).then_inc(sem("proj_act"), 1)
                else:
                    if i == 0:
                        act.wait_ge(sem("mu_ready"), 1)
                    dst = lz[:, c - ZLORA, :] if c >= ZLORA else zs[i % 2]
                    if c < ZLORA and i >= 5:
                        act.wait_ge(sem("z_tr"), i - 4)
                    nc.scalar.mul(dst[:, 0:T_S], b0, mu[:, c, 2:3]).then_inc(sem("proj_act"), 1)
                    nc.scalar.mul(dst[:, T_S:TOK], b1[:, 0:T_P], mu[:, c, 2:3]).then_inc(sem("proj_act"), 1)
                    if c < ZLORA and i >= 4:
                        act_z_evac(act, i - 1)
                if i == 15:
                    act_z_evac(act, 14)
            for i, t in enumerate(range(NT)):
                act.wait_ge(sem("v_mm"), i + 1)
                if i >= 2:
                    act.wait_ge(sem(f"v_out{i % 2}"), 16 * (i // 2))
                nc.scalar.copy(zs[i % 2][:, 0:W], bank[2 + i % 2]).then_inc(sem("v_ready"), 1)
                act.wait_ge(sem("v_ready"), i + 1)
                act.dma_start(v_dram[t * P:(t + 1) * P, :], zs[i % 2][:, 0:W]).then_inc(sem(f"v_out{i % 2}"), 16)
            for i in range(4, 12):
                mod(i, i)
            act.wait_ge(sem("v_out0"), 48)
            act.wait_ge(sem("v_out1"), 48)

        def act_z_evac(act, i):
            c = order[i][1]
            act.wait_ge(sem("z_tr"), i - 2)
            nc.scalar.copy(rkv[:, c // 4, 0:NT_S, (c % 4) * P:(c % 4 + 1) * P],
                           bank[i % 2].rearrange("p (t c) -> p t c", t=4)).then_inc(sem("z_act"), 1)

        def dve_z_evac(dve, i):
            c = order[i][1]
            dve.wait_ge(sem("z_tr"), i - 2)
            nc.vector.tensor_copy(rkv[:, c // 4, NT_S:NT, (c % 4) * P:(c % 4 + 1) * P],
                                  bank[2 + i % 2][:, 0:256].rearrange("p (t c) -> p t c", t=2)).then_inc(sem("z_dve"), 1)

        def dve_phase1(dve):
            own = Own(dve, sem("dve_own"))
            dve.wait_ge(sem("consts_in"), 16 * 12)
            own.link(nc.vector.tensor_tensor(mu[:, :, 2], mu[:, :, 0], mu[:, :, 1], ALU.add))
            nc.vector.tensor_scalar(mu[:, :, 2], mu[:, :, 2], -1.0, 1.0, ALU.mult, ALU.add).then_inc(sem("mu_ready"), 1)
            n = 0
            for m in range(2):
                for g in range(2):
                    for hf in range(2):
                        dve.wait_ge(sem("row_mm"), n + 1)
                        dst = rows[:, g, m, hf * 512:(hf + 1) * 512]
                        if m == 0:
                            ins = nc.vector.tensor_copy(dst, bank[n % 2])
                        else:
                            ins = nc.vector.scalar_tensor_tensor(dst, bank[n % 2], 1.0, n1_row[:, hf * 512:(hf + 1) * 512],
                                                                 ALU.add, ALU.mult)
                        ins.then_inc(sem("row_ready"), 1)
                        n += 1
            dve.wait_ge(sem("row_ready"), 8)

            def hT_evac(t):
                dve.wait_ge(sem("hT_mm"), 2 * t + 2)
                nc.vector.tensor_copy(hT[:, 4:8, t * P:(t + 1) * P], bank[3].rearrange("p (k c) -> p k c", k=4)).then_inc(sem("hT_dve"), 1)

            for t in range(NT):
                if t >= 2:
                    dve.wait_ge(sem("hT_mm"), 2 * t - 2)
                dve.wait_ge(sem("act_own"), 2 * t + 2)
                own.link(nc.vector.reciprocal(stat[:, t, 2:3], stat[:, t, 1:2]))
                ins = nc.vector.scalar_tensor_tensor(hb[t % 2], xb[t % 2], stat[:, t, 2:3], rows[:, group(t), 1, :], ALU.mult, ALU.mult)
                ins.then_inc(sem("x_used"), 1)
                dve.wait_ge(sem("x_used"), t + 1)
                nc.vector.tensor_tensor(hb[t % 2], hb[t % 2], rows[:, group(t), 0, :], ALU.add).then_inc(sem("h_ready"), 1)
                if t:
                    hT_evac(t - 1)
            hT_evac(NT - 1)
            for i, (kind, c, _) in enumerate(order):
                if kind != "z":
                    if i == 15:
                        dve_z_evac(dve, 14)
                    continue
                b0, b1 = bank[4 + i % 2], bank[6 + i % 2]
                dst = lz[:, c - ZLORA, :] if c >= ZLORA else zs[i % 2]
                dve.wait_ge(sem("proj_act"), 2 * i + 2)
                own.done(nc.vector.scalar_tensor_tensor(dst[:, 1:T_S], b0[:, 0:T_S - 1], mu[:, c, 0:1], dst[:, 1:T_S], ALU.mult, ALU.add))
                k = own.done(nc.vector.scalar_tensor_tensor(dst[:, T_S + 1:TOK], b1[:, 0:T_P - 1], mu[:, c, 0:1], dst[:, T_S + 1:TOK], ALU.mult, ALU.add))
                own.wait(k)
                nc.vector.scalar_tensor_tensor(dst[:, 0:T_S - 1], b0[:, 1:T_S], mu[:, c, 1:2], dst[:, 0:T_S - 1], ALU.mult, ALU.add).then_inc(sem("z_ready"), 1)
                nc.vector.scalar_tensor_tensor(dst[:, T_S:TOK - 1], b1[:, 1:T_P], mu[:, c, 1:2], dst[:, T_S:TOK - 1], ALU.mult, ALU.add).then_inc(sem("z_ready"), 1)
                if c < ZLORA and i >= 4:
                    dve_z_evac(dve, i - 1)

        def pe_phase1(pe):
            def mod(i, r):
                pe.wait_ge(sem(f"wide_in{r % 2}"), 32 * (r // 2 + 1))
                if i >= 2:
                    pe.wait_ge(sem("mod_ready"), i - 1)
                for k in range(2):
                    for q in range(4):
                        nc.tensor.matmul(bank[i % 2][32 * q:32 * q + 32, :], siluT[:, 2 * q + k, :], adaw[r % 2][:, 2 * q + k, :],
                                         start=(k == 0), stop=(k == 1 and q > 0), tile_position=(0, 32 * q))
                nc.tensor.matmul(bank[i % 2][0:32, :], sel[0:1, 2, 0:32], adab[r % 2][0:1, :],
                                 start=False, stop=True).then_inc(sem("mod_mm"), 1)

            pe.wait_ge(sem("silu_ready"), 1)
            pe.wait_ge(sem("consts_in"), 16 * 12)
            for i in range(4):
                mod(i, i)
            pe.wait_ge(sem("mod_ready"), 4)
            n = 0
            for m in range(2):
                for g in range(2):
                    for hf in range(2):
                        if n >= 2:
                            pe.wait_ge(sem("row_ready"), n - 1)
                        c = m * 2 + hf
                        nc.tensor.matmul(bank[n % 2], sel[:, g, :], modp[:, c * 512:(c + 1) * 512], start=True, stop=True).then_inc(sem("row_mm"), 1)
                        n += 1
            for t in range(NT):
                pe.wait_ge(sem("h_ready"), t + 1)
                for hf in range(2):
                    if t:
                        pe.wait_ge(sem("hT_act" if hf == 0 else "hT_dve"), t)
                    for k in range(4):
                        ins = nc.tensor.transpose(bank[2 + hf][:, k * P:(k + 1) * P], hb[t % 2][:, (hf * 4 + k) * P:(hf * 4 + k + 1) * P], ident)
                    ins.then_inc(sem("hT_mm"), 1)
            pe.wait_ge(sem("hT_act"), NT)
            pe.wait_ge(sem("hT_dve"), NT)

            def z_transposes(i):
                pe.wait_ge(sem("z_ready"), 2 * i + 2)
                if i >= 5:
                    pe.wait_ge(sem("z_act"), i - 4)
                    pe.wait_ge(sem("z_dve"), i - 4)
                for t in range(NT):
                    dst = bank[i % 2][:, t * P:(t + 1) * P] if t < NT_S else bank[2 + i % 2][:, (t - NT_S) * P:(t - NT_S + 1) * P]
                    ins = nc.tensor.transpose(dst, zs[i % 2][:, t * P:(t + 1) * P], ident)
                ins.then_inc(sem("z_tr"), 1)

            for i, (kind, c, _) in enumerate(order):
                pe.wait_ge(sem(f"win_in{i % NWIN}"), 16 * (i // NWIN + 1))
                if i >= 2:
                    pe.wait_ge(sem("proj_act"), 2 * (i - 1))
                    if order[i - 2][0] == "z":
                        pe.wait_ge(sem("z_ready"), 2 * (i - 1))
                for k in range(KD):
                    nc.tensor.matmul(bank[4 + i % 2], winb[i % NWIN][:, k, :], hT[:, k, 0:T_S], start=(k == 0), stop=(k == KD - 1))
                    ins = nc.tensor.matmul(bank[6 + i % 2][:, 0:T_P], winb[i % NWIN][:, k, :], hT[:, k, T_S:TOK], start=(k == 0), stop=(k == KD - 1))
                ins.then_inc(sem("proj_mm"), 1)
                if 4 <= i <= 15:
                    z_transposes(i - 1)
            pe.wait_ge(sem("wide_in0"), 32 * 3)
            pe.wait_ge(sem("z_act"), 12)
            pe.wait_ge(sem("z_dve"), 12)
            for t in range(NT):
                if t >= 2:
                    pe.wait_ge(sem("v_ready"), t - 1)
                for k in range(KD):
                    ins = nc.tensor.matmul(bank[2 + t % 2], hT[:, k, t * P:(t + 1) * P], adaw[0][:, k, :], start=(k == 0), stop=(k == KD - 1))
                ins.then_inc(sem("v_mm"), 1)
            for i in range(4, 12):
                mod(i, i + 1)

        top[0] = base3
        w_lora = take(5 * W).rearrange("p (j c) -> p j c", j=5)
        lrow = take(4 * W).rearrange("p (j c) -> p j c", j=4)
        pre = take(4 * W).rearrange("p (j c) -> p j c", j=4)
        sg = take(6 * W).rearrange("p (d q c) -> p d q c", d=2, q=3)
        sq2 = take(W)
        bon = take(W)
        nrm = take(NT * NH)
        assert top[0] <= base3 + 2 * KD * 512 + NWIN * KD * P

        def sp_phase2(sp):
            sp.wait_ge(sem("lora_zero"), 1)
            for d in range(2):
                half = slice(d * 64, d * 64 + 64)
                sp.dma_start(w_lora[half, 2 * d, :], A["rwkv_w2"][0, d]).then_inc(sem("lora_in"), 16)
                sp.dma_start(w_lora[half, 2 * d + 1, :], A["rwkv_a2"][0, d]).then_inc(sem("lora_in"), 16)
                sp.dma_start(lrow[:, 2 * d, :], A["rwkv_w0"][0, d].partition_broadcast(P)).then_inc(sem("lora_in"), 16)
                sp.dma_start(lrow[:, 2 * d + 1, :], A["rwkv_a0"][0, d].partition_broadcast(P)).then_inc(sem("lora_in"), 16)
            sp.dma_start(w_lora[:, 4, :], A["rwkv_g2"][0]).then_inc(sem("lora_in"), 16)
            for t in range(NT):
                sp.wait_ge(sem("key_ready"), t + 1)
                sp.dma_start(dir_dram[:, :, t].rearrange("d q p c -> p (d q) c"), sg.rearrange("p d q c -> p (d q) c")).then_inc(sem("sig_out"), 16)
            sp.wait_ge(sem("sig_out"), 16 * NT)

        def pool_phase2(pool):
            nc.gpsimd.memset(w_lora[:, 0:4, :], 0.0).then_inc(sem("lora_zero"), 1)
            for t in range(NT):
                nc.gpsimd.tensor_tensor(kkn[:, t, :], rkv[:, 1, t, :], kk_row, ALU.mult).then_inc(sem("kk_raw"), 1)
                pool.wait_ge(sem("kk_raw"), t + 1)
                if t:
                    pool.wait_ge(sem("kk_sum"), t)
                nc.gpsimd.tensor_tensor(sq2, kkn[:, t, :], kkn[:, t, :], ALU.mult).then_inc(sem("kk_sq"), 1)

        def act_phase2(act):
            nc.scalar.activation(lz[:, 0, :], lz[:, 0, :], ACT.Tanh).then_inc(sem("lz_act"), 1)
            nc.scalar.activation(lz[:, 2, :], lz[:, 2, :], ACT.Sigmoid).then_inc(sem("lz_act"), 1)
            for t in range(NT):
                act.wait_ge(sem("pre_ready"), 4 * t + 4)
                if t:
                    act.wait_ge(sem("sig_out"), 16 * t)
                    act.wait_ge(sem("bonus_read"), t)
                nc.scalar.activation(sg[:, :, 0:2, :], pre.rearrange("p (d q) c -> p d q c", d=2), ACT.Sigmoid).then_inc(sem("sig_ready"), 1)
                act.wait_ge(sem("lora_mm"), 5 * t + 5)
                nc.scalar.copy(gate[:, t, :], bank[4]).then_inc(sem("gate_ready"), 1)
            act.wait_ge(sem("kk_sum"), NT)
            nc.scalar.activation(nrm, nrm, ACT.Sqrt).then_inc(sem("kk_root"), 1)

        def pe_phase2(pe):
            pe.wait_ge(sem("lora_in"), 16 * 9)
            pe.wait_ge(sem("lz_act"), 2)
            for t in range(NT):
                for j in range(5):
                    if t:
                        if j < 4:
                            pe.wait_ge(sem("pre_ready"), 4 * (t - 1) + j + 1)
                        else:
                            pe.wait_ge(sem("gate_ready"), t)
                    c = 2 if j == 4 else j % 2
                    nc.tensor.matmul(bank[j], lz[:, c, t * P:(t + 1) * P], w_lora[:, j, :], start=True, stop=True).then_inc(sem("lora_mm"), 1)

        def dve_phase2(dve):
            own = Own(dve, sem("dve_own2"))
            dve.wait_ge(sem("lora_in"), 16 * 9)

            def key_sum(t):
                dve.wait_ge(sem("kk_sq"), t + 1)
                nc.vector.reduce_sum(nrm[:, t * NH:(t + 1) * NH], sq2.rearrange("p (h c) -> p h c", h=NH), AX).then_inc(sem("kk_sum"), 1)

            for t in range(NT):
                if t:
                    dve.wait_ge(sem("sig_ready"), t)
                for j in range(4):
                    dve.wait_ge(sem("lora_mm"), 5 * t + j + 1)
                    nc.vector.tensor_tensor(pre[:, j, :], bank[j], lrow[:, j, :], ALU.add).then_inc(sem("pre_ready"), 1)
                key_sum(t)
                dve.wait_ge(sem("sig_ready"), t + 1)
                for d in range(2):
                    own.done(nc.vector.scalar_tensor_tensor(sg[:, d, 2, :], sg[:, d, 1, :], -1.0, ka_row, ALU.add, ALU.mult))
                own.wait(own.n - 1)
                own.done(nc.vector.scalar_tensor_tensor(sg[:, 0, 2, :], sg[:, 0, 2, :], 1.0, rkv[:, 1, t, :], ALU.add, ALU.mult))
                own.wait(own.n)
                nc.vector.scalar_tensor_tensor(sg[:, 1, 2, :], sg[:, 1, 2, :], 1.0, rkv[:, 1, t, :], ALU.add, ALU.mult).then_inc(sem("key_ready"), 1)
                dve.wait_ge(sem("key_ready"), t + 1)
                own.link(nc.vector.tensor_tensor(bon, sg[:, 0, 2, :], sg[:, 1, 2, :], ALU.add))
                own.link(nc.vector.tensor_tensor(bon, bon, rkv[:, 0, t, :], ALU.mult))
                own.link(nc.vector.tensor_tensor(bon, bon, rk_row, ALU.mult))
                nc.vector.reduce_sum(bonus[:, t, :], bon.rearrange("p (h c) -> p h c", h=NH), AX).then_inc(sem("bonus_read"), 1)
                dve.wait_ge(sem("bonus_read"), t + 1)
            dve.wait_ge(sem("kk_root"), 1)
            own.link(nc.vector.tensor_scalar(nrm, nrm, 1e-12, None, ALU.max))
            own.link(nc.vector.reciprocal(nrm, nrm))
            for t in range(NT):
                k3 = kkn[:, t, :].rearrange("p (h c) -> p h c", h=NH)
                s3 = nrm[:, t * NH:(t + 1) * NH].unsqueeze(2).to_broadcast([P, NH, HD])
                nc.vector.tensor_tensor(k3, k3, s3, ALU.mult)

        top[0] = base3
        bias = take(3 * NH * 8 * KB).rearrange("p (k h c) -> p k h c", k=3, h=NH)
        window = take(3 * KB).rearrange("p (k c) -> p k c", k=3)
        vband = take(NQB * 3 * W).rearrange("p (n s c) -> p n s c", n=NQB, s=3)
        sc = [take(8 * KB) for _ in range(3)]
        pT = [take(8 * KB) for _ in range(2)]
        items = [(g, n, h) for g in range(2) for n in range(NQB) for h in range(NH)]
        NI = len(items)
        nmax, psum_row, pinv = (take(NI) for _ in range(3))
        GR = [T_S // GW, T_P // GW]
        TOFF = [0, T_S]
        KIND = [0, 1, 1, 2]

        def grid(ap, g, col, cols):
            return ap[:, TOFF[g]:TOFF[g] + GR[g] * GW].rearrange("p (r c) -> p r c", c=GW)[:, :, col:col + cols]

        def sp_phase3(sp):
            sp.dma_start(window, A["c_window"]).then_inc(sem("bias_in"), 16)
            for k in range(3):
                sp.dma_start(bias[:, k], A["bias"][k]).then_inc(sem("bias_in"), 16)
            for g in range(2):
                for n in range(NQB):
                    for m in range(GR[g]):
                        r0 = TOFF[g] + m * GW + band(n)
                        s = m // 4 if g == 0 else 2
                        sp.dma_start(vband[32 * (m % 4):32 * (m % 4) + 32, n, s, :], v_dram[r0:r0 + KB, :]).then_inc(sem("band_in"), 16)

        def pool_phase3(pool):
            for i, (g, n, h) in enumerate(items):
                nq, nk = GR[g] * QB, GR[g] * KB
                pool.wait_ge(sem("p_inv"), i + 1)
                nc.gpsimd.tensor_scalar(sc[i % 3][0:nq, 0:nk], sc[i % 3][0:nq, 0:nk], pinv[0:nq, i:i + 1], None, ALU.mult).then_inc(sem("p_ready"), 1)

        def act_phase3(act):
            for i in range(NI + 3):
                if i < NI:
                    g, n, h = items[i]
                    nq, nk = GR[g] * QB, GR[g] * KB
                    act.wait_ge(sem("s_max"), i + 1)
                    nc.scalar.activation(sc[i % 3][0:nq, 0:nk], sc[i % 3][0:nq, 0:nk], ACT.Exp, bias=nmax[0:nq, i:i + 1],
                                         accum_out=psum_row[0:nq, i:i + 1]).then_inc(sem("p_exp"), 1)
                if 2 <= i < NI + 2:
                    j = i - 2
                    n_t = 256 if items[j][0] == 0 else 64
                    act.wait_ge(sem("pT_mm"), j + 1)
                    if j >= 2:
                        act.wait_ge(sem("o_mm"), j - 1)
                    nc.scalar.copy(pT[j % 2][:, 0:n_t], bank[3 + j % 2][:, 0:n_t]).then_inc(sem("pT_ready"), 1)
                if i >= 3 and i % 2 == 0:
                    j = i - 3
                    g, n, h = items[j]
                    act.wait_ge(sem("o_mm"), j + 1)
                    nc.scalar.copy(grid(catT[:, h // 2, :], g, n * QB, QB),
                                   bank[5 + (j // 2) % 2][:, 0:GR[g] * QB].rearrange("p (r c) -> p r c", c=QB)).then_inc(sem("o_ready"), 1)

        def dve_phase3(dve):
            own = Own(dve, sem("dve_own3"))
            dve.wait_ge(sem("bias_in"), 16 * 4)
            for k in range(3):
                b3 = bias[:, k].rearrange("p h (m c) -> p (h m) c", c=KB)
                last = own.done(nc.vector.tensor_tensor(b3, b3, window[:, k, :].unsqueeze(1).to_broadcast([P, NH * 8, KB]), ALU.add))
            own.wait(last)

            def inverse(i):
                nq = GR[items[i][0]] * QB
                dve.wait_ge(sem("p_exp"), i + 1)
                nc.vector.reciprocal(pinv[0:nq, i:i + 1], psum_row[0:nq, i:i + 1]).then_inc(sem("p_inv"), 1)

            for i, (g, n, h) in enumerate(items):
                nq, nk = GR[g] * QB, GR[g] * KB
                dve.wait_ge(sem("s_mm"), i + 1)
                if i >= 3:
                    dve.wait_ge(sem("pT_mm"), i - 2)
                own.link(nc.vector.tensor_tensor(sc[i % 3][0:nq, 0:nk], bank[i % 3][0:nq, 0:nk], bias[0:nq, KIND[n], h, 0:nk], ALU.add))
                nc.vector.tensor_reduce(nmax[0:nq, i:i + 1], sc[i % 3][0:nq, 0:nk], AX, ALU.max, negate=True).then_inc(sem("s_max"), 1)
                if i:
                    inverse(i - 1)
            inverse(NI - 1)

        def pe_phase3(pe):
            pe.wait_ge(sem("band_in"), 16 * NQB * sum(GR))
            for i in range(NI + 3):
                if i < NI:
                    g, n, h = items[i]
                    nq, nk = GR[g] * QB, GR[g] * KB
                    hp = slice(64 * (h % 2), 64 * (h % 2) + 64)
                    if i >= 3:
                        pe.wait_ge(sem("s_max"), i - 2)
                    nc.tensor.matmul(bank[i % 3][0:nq, 0:nk], qT[hp, h // 2, TOFF[g] + n * nq:TOFF[g] + (n + 1) * nq], grid(kT[hp, h // 2, :], g, band(n), KB),
                                     start=True, stop=True).then_inc(sem("s_mm"), 1)
                if 2 <= i < NI + 2:
                    j = i - 2
                    g = items[j][0]
                    nq = GR[g] * QB
                    pe.wait_ge(sem("p_ready"), j + 1)
                    if j >= 2:
                        pe.wait_ge(sem("pT_ready"), j - 1)
                    for s in range(2 - g):
                        ins = nc.tensor.transpose(bank[3 + j % 2][:, s * P:s * P + nq], sc[j % 3][0:nq, s * P:(s + 1) * P], ident[0:nq, 0:nq])
                    ins.then_inc(sem("pT_mm"), 1)
                if i >= 3:
                    j = i - 3
                    g, n, h = items[j]
                    nq = GR[g] * QB
                    hp = slice(64 * (h % 2), 64 * (h % 2) + 64)
                    pe.wait_ge(sem("pT_ready"), j + 1)
                    if j >= 4 and h % 2 == 0:
                        pe.wait_ge(sem("o_ready"), j // 2 - 1)
                    for s in range(2 - g):
                        ins = nc.tensor.matmul(bank[5 + (j // 2) % 2][hp, 0:nq], vband[:, n, 2 if g else s, h * HD:(h + 1) * HD],
                                               pT[j % 2][:, s * P:s * P + nq], start=(s == 0), stop=(s == 1 - g))
                    ins.then_inc(sem("o_mm"), 1)

        top[0] = base4
        tri = take(2 * P).rearrange("p (d c) -> p d c", d=2)
        midc = take(4).rearrange("p (d c) -> p d c", d=2)
        seen = take(2 * 512).rearrange("p (d c) -> p d c", d=2)
        pairm = take(P)
        sgw = [take(3 * W).rearrange("p (q c) -> p q c", q=3) for _ in range(2)]
        cin, cinv, cex = take(W), take(W), take(W)
        tok4 = take(4 * W).rearrange("p (q c) -> p q c", q=4)
        chT = take(4 * W).rearrange("p (q j c) -> p q j c", q=4, j=NPAIR)
        ar4 = take(NPAIR * 512).rearrange("p (j c) -> p j c", j=NPAIR)
        Lb = take(NPAIR * 512).rearrange("p (j c) -> p j c", j=NPAIR)
        Lk = take(NPAIR * 512).rearrange("p (j c) -> p j c", j=NPAIR)
        inv = take(NH * 192).bitcast(f16).rearrange("p (h c) -> p h c", h=NH)
        cme = take(8).rearrange("p (j m) -> p j m", m=2)
        cend = take(W).rearrange("p (j c) -> p j c", j=NPAIR)
        state = [take(W) for _ in range(2)]
        stp = take(W).rearrange("p (j c) -> p j c", j=NPAIR)
        rhs, u0, res, u1 = take(W), take(W), take(W), take(W)
        rhs16, res16 = take(W // 2).bitcast(f16), take(W // 2).bitcast(f16)
        yacc = catT[:, 4:8, :].rearrange("p c t -> p (c t)").rearrange("p (t c) -> p t c", t=NT)
        IA, IR, IB, IK = range(4)
        steps = [(d, t) for i in range(NT_S) for d, t in ((0, i), (1, NT_S - 1 - i))] + \
                [(d, t) for i in range(NT_P) for d, t in ((0, NT_S + i), (1, NT - 1 - i))]
        fresh = (0, 1, 2 * NT_S, 2 * NT_S + 1)

        def hcol(h):
            return slice(h * HD, (h + 1) * HD)

        def lcol(h, r):
            return slice((h % 2) * 256 + r * P, (h % 2) * 256 + (r + 1) * P)

        def evac_of(l, h):
            return l * (NH // 2) + h // 2 + 1

        EVACS = LEVELS * NH // 2

        def sp_phase4(sp):
            for dst, src in ((tri, A["c_tri"]), (midc, A["c_mid"]), (seen, A["c_seen"]), (pairm, A["c_pair"])):
                sp.dma_start(dst, src).then_inc(sem("consts4_in"), 16)
            for n, (d, t) in enumerate(steps):
                if n >= 2:
                    sp.wait_ge(sem("mid_mm"), n - 1)
                    sp.wait_ge(sem("tok_ready"), 3 * (n - 1))
                    sp.wait_ge(sem("ktok_ready"), n - 1)
                sp.dma_start(sgw[n % 2], dir_dram[d, :, t].rearrange("q p c -> p q c")).then_inc(sem(f"sig_in{n % 2}"), 16)

        def pool_phase4(pool):
            nc.gpsimd.memset(ar4, 0.0).then_inc(sem("zero4"), 1)
            nc.gpsimd.memset(yacc, 0.0).then_inc(sem("zero4"), 1)
            pool.wait_ge(sem("consts4_in"), 64)
            for n, (d, t) in enumerate(steps):
                pool.wait_ge(sem(f"sig_in{n % 2}"), 16 * (n // 2 + 1))
                if n:
                    pool.wait_ge(sem("st_mm"), n)
                pool.wait_ge(sem("exps"), 3 * n + 2)
                nc.gpsimd.tensor_tensor(tok4[:, IK, :], sgw[n % 2][:, 2, :], cinv, ALU.mult).then_inc(sem("ktok_ready"), 1)
                pool.wait_ge(sem("cme_ready"), n + 1)
                if n:
                    pool.wait_ge(sem("st_ready"), n)
                nc.gpsimd.tensor_tensor(cend, pairm.unsqueeze(1).to_broadcast([P, NPAIR, P]),
                                        cme[:, :, 1:2].to_broadcast([P, NPAIR, P]), ALU.mult).then_inc(sem("cend_ready"), 1)

        def act_phase4(act):
            for n, (d, t) in enumerate(steps):
                act.wait_ge(sem("cum_mm"), n + 1)
                if n:
                    act.wait_ge(sem("tok_ready"), 3 * n)
                    act.wait_ge(sem("ktok_ready"), n)
                    act.wait_ge(sem("cend_ready"), n)
                    act.wait_ge(sem("stp_ready"), n)
                nc.scalar.activation(cin, bank[3], ACT.Exp, scale=-DECAY).then_inc(sem("exps"), 1)
                nc.scalar.activation(cinv, bank[3], ACT.Exp, scale=DECAY).then_inc(sem("exps"), 1)
                act.wait_ge(sem("mid_mm"), n + 1)
                nc.scalar.activation(cme, bank[2][:, 0:8].rearrange("p (j m) -> p j m", m=2), ACT.Exp, scale=-DECAY).then_inc(sem("cme_ready"), 1)
                act.wait_ge(sem("cex_ready"), n + 1)
                nc.scalar.activation(cex, cex, ACT.Exp, scale=-DECAY).then_inc(sem("exps"), 1)
                for q, j in ((IB, 2), (IK, 3)):
                    act.wait_ge(sem("tr_mm"), 4 * n + j)
                    nc.scalar.copy(chT[:, q], bank[4 + q].rearrange("p (j c) -> p j c", j=NPAIR)).then_inc(sem("chT_act"), 1)
                for j in range(NPAIR):
                    act.wait_ge(sem("L_ready"), 8 * n + 2 * j + 1)
                    nc.scalar.copy(inv[:, 2 * j:2 * j + 2, 0:P], Lb[:, j, :].rearrange("p (h r c) -> p h r c", h=2, r=2)[:, :, 0, :]).then_inc(sem("Nt_ready"), 1)
                act.wait_ge(sem("rhs_mm"), n + 1)
                nc.scalar.copy(rhs, bank[0]).then_inc(sem("rhs_ready"), 1)
                for l in range(LEVELS):
                    for h in range(0, NH, 2):
                        act.wait_ge(sem("inv_mm"), NH * (LEVELS * n + l) + h + 1)
                        if l < LEVELS - 1:
                            ins = nc.scalar.copy(inv[:, h, :], bank[4 + h % 4][:, 0:3 * P])
                        else:
                            ins = nc.scalar.copy(inv[:, h, P:2 * P], bank[4 + h % 4][:, P:2 * P])
                        ins.then_inc(sem("inv_act"), 1)
                act.wait_ge(sem("u0_mm"), n + 1)
                nc.scalar.copy(u0, bank[1]).then_inc(sem("u0_ready"), 1)
            act.wait_ge(sem("y_centred"), 1)
            nc.scalar.activation(rkv[:, 0], yacc, ACT.Square).then_inc(sem("y_squared"), 1)
            act.wait_ge(sem("y_var"), 1)
            nc.scalar.activation(nrm4, nrm4, ACT.Sqrt, scale=1.0 / HD, bias=eps[:, 1:2]).then_inc(sem("y_root"), 1)
            for t in range(NT):
                act.wait_ge(sem("rec_tr"), t + 1)
                nc.scalar.copy(catT[:, 4:8, t * P:(t + 1) * P], bank[t % 2].rearrange("p (j c) -> p j c", j=NPAIR)).then_inc(sem("rec_ready"), 1)

        def dve_phase4(dve):
            own = Own(dve, sem("dve_own4"))
            dve.wait_ge(sem("zero4"), 2)
            dve.wait_ge(sem("consts4_in"), 64)
            for n, (d, t) in enumerate(steps):
                dve.wait_ge(sem(f"sig_in{n % 2}"), 16 * (n // 2 + 1))
                last = own.done(nc.vector.tensor_tensor(tok4[:, IB, :], kkn[:, t, :], sgw[n % 2][:, 1, :], ALU.mult))
                if n in fresh:
                    own.wait(own.done(nc.vector.memset(state[d], 0.0)))
                dve.wait_ge(sem("exps"), 3 * n + 2)
                nc.vector.tensor_tensor(cex, bank[3], sgw[n % 2][:, 0, :], ALU.subtract).then_inc(sem("cex_ready"), 1)
                nc.vector.tensor_tensor(tok4[:, IR, :], rkv[:, 0, t, :], cin, ALU.mult).then_inc(sem("tok_ready"), 1)
                own.wait(last)
                nc.vector.tensor_tensor(tok4[:, IB, :], tok4[:, IB, :], cinv, ALU.mult).then_inc(sem("tok_ready"), 1)
                dve.wait_ge(sem("exps"), 3 * n + 3)
                nc.vector.scalar_tensor_tensor(tok4[:, IA, :], kkn[:, t, :], -1.0, cex, ALU.mult, ALU.mult).then_inc(sem("tok_ready"), 1)
                dve.wait_ge(sem("cme_ready"), n + 1)
                s3 = state[d].rearrange("p (j c) -> p j c", j=NPAIR)
                nc.vector.tensor_tensor(stp, s3, cme[:, :, 0:1].to_broadcast([P, NPAIR, P]), ALU.mult).then_inc(sem("stp_ready"), 1)
                for q, j in ((IR, 1), (IA, 4)):
                    dve.wait_ge(sem("tr_mm"), 4 * n + j)
                    own.link(nc.vector.tensor_copy(chT[:, q], bank[4 + q].rearrange("p (j c) -> p j c", j=NPAIR)))
                    r = 0 if q == IA else P
                    for hh in range(2):
                        hp = slice(64 * hh, 64 * hh + 64)
                        nc.vector.tensor_copy(ar4[hp, :, hh * 256 + r:hh * 256 + r + P], chT[hp, q]).then_inc(sem("chT_dve"), 1)
                for j in range(NPAIR):
                    for k, L in ((0, Lb), (1, Lk)):
                        dve.wait_ge(sem("L_mm"), 8 * n + 2 * j + k + 1)
                        nc.vector.scalar_tensor_tensor(L[:, j, :], bank[4 + 2 * (j % 2) + k], BIG, seen[:, d, :], ALU.min, ALU.mult).then_inc(sem("L_ready"), 1)
                dve.wait_ge(sem("N_mm"), n + 1)
                nc.vector.tensor_copy(inv[:, :, 2 * P:3 * P], bank[3].bitcast(f16).rearrange("p (h c) -> p h c", h=NH)).then_inc(sem("N_ready"), 1)
                dve.wait_ge(sem("rhs_ready"), n + 1)
                nc.vector.tensor_copy(rhs16, rhs).then_inc(sem("rhs16_ready"), 1)
                for l in range(LEVELS):
                    for h in range(1, NH, 2):
                        dve.wait_ge(sem("inv_mm"), NH * (LEVELS * n + l) + h + 1)
                        if l < LEVELS - 1:
                            ins = nc.vector.tensor_copy(inv[:, h, :], bank[4 + h % 4][:, 0:3 * P])
                        else:
                            ins = nc.vector.tensor_copy(inv[:, h, P:2 * P], bank[4 + h % 4][:, P:2 * P])
                        ins.then_inc(sem("inv_dve"), 1)
                dve.wait_ge(sem("u0_ready"), n + 1)
                own.link(nc.vector.tensor_tensor(res, rhs, u0, ALU.subtract))
                own.link(nc.vector.tensor_scalar(res, res, U_SCALE, None, ALU.mult))
                dve.wait_ge(sem("nu_mm"), n + 1)
                nc.vector.scalar_tensor_tensor(res16, bank[0], U_SCALE, res, ALU.mult, ALU.add).then_inc(sem("res16_ready"), 1)
                dve.wait_ge(sem("du_mm"), n + 1)
                nc.vector.scalar_tensor_tensor(u1, bank[1], 1.0 / U_SCALE, u0, ALU.mult, ALU.add).then_inc(sem("u1_ready"), 1)
                dve.wait_ge(sem("y_mm"), n + 1)
                nc.vector.tensor_tensor(yacc[:, t, :], bank[2], yacc[:, t, :], ALU.add).then_inc(sem("y_ready"), 1)
                dve.wait_ge(sem("st_mm"), n + 1)
                own.link(nc.vector.tensor_tensor(state[d], bank[3], stp.rearrange("p j c -> p (j c)"), ALU.add))
                dve.wait_ge(sem("cend_ready"), n + 1)
                nc.vector.tensor_tensor(s3, s3, cend, ALU.mult).then_inc(sem("st_ready"), 1)
                dve.wait_ge(sem("st_ready"), n + 1)
            dve.wait_ge(sem("y_ready"), len(steps))
            y4 = yacc.rearrange("p t (h c) -> p (t h) c", c=HD)
            own.link(nc.vector.reduce_sum(nrm4, y4, AX))
            own.link(nc.vector.tensor_scalar(nrm4, nrm4, 1.0 / HD, None, ALU.mult))
            nc.vector.tensor_tensor(y4, y4, nrm4.unsqueeze(2).to_broadcast([P, NT * NH, HD]), ALU.subtract).then_inc(sem("y_centred"), 1)
            dve.wait_ge(sem("y_squared"), 1)
            nc.vector.reduce_sum(nrm4, rkv[:, 0].rearrange("p t (h c) -> p (t h) c", c=HD), AX).then_inc(sem("y_var"), 1)
            dve.wait_ge(sem("y_root"), 1)
            own.link(nc.vector.reciprocal(nrm4, nrm4))
            own.link(nc.vector.tensor_tensor(y4, y4, nrm4.unsqueeze(2).to_broadcast([P, NT * NH, HD]), ALU.mult))
            own.link(nc.vector.tensor_tensor(yacc, yacc, lg_row.unsqueeze(1).to_broadcast([P, NT, W]), ALU.mult))
            own.link(nc.vector.tensor_tensor(yacc, yacc, lb_row.unsqueeze(1).to_broadcast([P, NT, W]), ALU.add))
            v4 = rkv[:, 2].rearrange("p t (h c) -> p (t h) c", c=HD)
            own.link(nc.vector.tensor_tensor(v4, v4, bonus.rearrange("p t h -> p (t h)").unsqueeze(2).to_broadcast([P, NT * NH, HD]), ALU.mult))
            own.link(nc.vector.tensor_tensor(yacc, yacc, rkv[:, 2], ALU.add))
            nc.vector.tensor_tensor(gate, gate, yacc, ALU.mult).then_inc(sem("rec_tok"), 1)

        nrm4 = take(NT * NH)

        def pe_phase4(pe):
            pe.wait_ge(sem("consts4_in"), 64)

            def mm(out, lhsT, r, start=False):
                return nc.tensor.matmul(out, lhsT, r, start=start, stop=True, skip_group_check=True)

            for n, (d, t) in enumerate(steps):
                v = rkv[:, 2, t, :]
                pe.wait_ge(sem(f"sig_in{n % 2}"), 16 * (n // 2 + 1))
                if n:
                    pe.wait_ge(sem("st_ready"), n)
                    pe.wait_ge(sem("y_ready"), n)
                mm(bank[3], tri[:, d, :], sgw[n % 2][:, 0, :], True).then_inc(sem("cum_mm"), 1)
                for j in range(NPAIR):
                    ins = mm(bank[2][:, 2 * j:2 * j + 2], sgw[n % 2][:, 0, j * P:(j + 1) * P], midc[:, d, :], True)
                ins.then_inc(sem("mid_mm"), 1)
                for q, s, v0 in ((IR, "tok_ready", 3 * n + 1), (IB, "tok_ready", 3 * n + 2), (IK, "ktok_ready", n + 1), (IA, "tok_ready", 3 * n + 3)):
                    pe.wait_ge(sem(s), v0)
                    for j in range(NPAIR):
                        ins = nc.tensor.transpose(bank[4 + q][:, j * P:(j + 1) * P], tok4[:, q, j * P:(j + 1) * P], ident)
                    ins.then_inc(sem("tr_mm"), 1)
                pe.wait_ge(sem("chT_act"), 2 * n + 2)
                pe.wait_ge(sem("chT_dve"), 4 * n + 4)
                for j in range(NPAIR):
                    for k, q in ((0, IB), (1, IK)):
                        if j >= 2:
                            pe.wait_ge(sem("L_ready"), 8 * n + 2 * (j - 2) + k + 1)
                        mm(bank[4 + 2 * (j % 2) + k], chT[:, q, j, :], ar4[:, j, :], True).then_inc(sem("L_mm"), 1)
                pe.wait_ge(sem("Nt_ready"), 4 * n + 4)
                pe.wait_ge(sem("cex_ready"), n + 1)
                b16 = bank[3].bitcast(f16)
                for h in range(NH):
                    ins = nc.tensor.transpose(b16[:, h * P:(h + 1) * P], inv[:, h, 0:P], ident16)
                ins.then_inc(sem("N_mm"), 1)
                pe.wait_ge(sem("L_ready"), 8 * n + 8)
                pe.wait_ge(sem("stp_ready"), n + 1)
                pe.wait_ge(sem("cme_ready"), n + 1)
                for j in range(NPAIR):
                    mm(bank[0][:, j * P:(j + 1) * P], chT[:, IA, j, :], stp[:, j, :], j == 0)
                for h in range(NH):
                    ins = mm(bank[0][:, hcol(h)], Lk[:, h // 2, lcol(h, 0)], v[:, hcol(h)])
                ins.then_inc(sem("rhs_mm"), 1)
                for j in range(NPAIR):
                    mm(bank[2][:, j * P:(j + 1) * P], chT[:, IR, j, :], stp[:, j, :], j == 0)
                for h in range(NH):
                    mm(bank[2][:, hcol(h)], Lk[:, h // 2, lcol(h, 1)], v[:, hcol(h)])
                pe.wait_ge(sem("N_ready"), n + 1)
                for l in range(LEVELS):
                    for h in range(NH):
                        own = sem("inv_act" if h % 2 == 0 else "inv_dve")
                        need = evac_of(l, h - 4) if h >= 4 else evac_of(l - 1, h + 4)
                        if need > 0 and (l or h >= 4):
                            pe.wait_ge(own, EVACS * n + need)
                        b = bank[4 + h % 4]
                        nt, x, m = inv[:, h, 0:P], inv[:, h, P:2 * P], inv[:, h, 2 * P:3 * P]
                        if l == 0:
                            mm(b[:, 0:P], m, nt, True)
                            mm(b[:, P:2 * P], m, ident16)
                            mm(b[:, P:2 * P], ident16, ident16)
                            ins = mm(b[:, 2 * P:3 * P], nt, m)
                        elif l < LEVELS - 1:
                            mm(b[:, 0:2 * P], m, inv[:, h, 0:2 * P], True)
                            mm(b[:, P:2 * P], ident16, x)
                            ins = mm(b[:, 2 * P:3 * P], nt, m)
                        else:
                            mm(b[:, P:2 * P], m, x, True)
                            ins = mm(b[:, P:2 * P], ident16, x)
                        ins.then_inc(sem("inv_mm"), 1)
                pe.wait_ge(sem("rhs16_ready"), n + 1)
                pe.wait_ge(sem("inv_act"), EVACS * (n + 1))
                pe.wait_ge(sem("inv_dve"), EVACS * (n + 1))
                for h in range(NH):
                    ins = mm(bank[1][:, hcol(h)], inv[:, h, P:2 * P], rhs16[:, hcol(h)], h == 0)
                ins.then_inc(sem("u0_mm"), 1)
                pe.wait_ge(sem("u0_ready"), n + 1)
                for h in range(NH):
                    ins = mm(bank[0][:, hcol(h)], Lb[:, h // 2, lcol(h, 0)], u0[:, hcol(h)], h == 0)
                ins.then_inc(sem("nu_mm"), 1)
                pe.wait_ge(sem("res16_ready"), n + 1)
                for h in range(NH):
                    ins = mm(bank[1][:, hcol(h)], inv[:, h, P:2 * P], res16[:, hcol(h)], h == 0)
                ins.then_inc(sem("du_mm"), 1)
                pe.wait_ge(sem("u1_ready"), n + 1)
                for j in range(NPAIR):
                    mm(bank[3][:, j * P:(j + 1) * P], tok4[:, IB, j * P:(j + 1) * P], u1[:, j * P:(j + 1) * P], j == 0)
                    ins = mm(bank[3][:, j * P:(j + 1) * P], tok4[:, IK, j * P:(j + 1) * P], v[:, j * P:(j + 1) * P])
                ins.then_inc(sem("st_mm"), 1)
                for h in range(NH):
                    ins = mm(bank[2][:, hcol(h)], Lb[:, h // 2, lcol(h, 1)], u1[:, hcol(h)])
                ins.then_inc(sem("y_mm"), 1)
            pe.wait_ge(sem("rec_tok"), 1)
            for t in range(NT):
                if t >= 2:
                    pe.wait_ge(sem("rec_ready"), t - 1)
                for j in range(NPAIR):
                    ins = nc.tensor.transpose(bank[t % 2][:, j * P:(j + 1) * P], gate[:, t, j * P:(j + 1) * P], ident)
                ins.then_inc(sem("rec_tr"), 1)

        top[0] = base5
        x2 = take(NT * D).rearrange("p (t d) -> p t d", t=NT)
        g2_row = take(2 * D).rearrange("p (g d) -> p g d", g=2)
        wts = take(NT * 2).rearrange("p (t k) -> p t k", k=2)
        pos_i = take(NT * 2).bitcast(i32).rearrange("p (t k) -> p t k", k=2)
        base6 = top[0]
        wout = take(KD * D).rearrange("p (k n) -> p k n", k=KD)
        g1_row = take(2 * D).rearrange("p (g d) -> p g d", g=2)
        ss_row = take(4 * D).rearrange("p (g m d) -> p g m d", g=2, m=2)
        n2_row = take(D)
        h2 = [take(D) for _ in range(2)]
        sq5 = take(D)
        h2T = [take(D).rearrange("p (k c) -> p k c", k=KD) for _ in range(2)]
        sel5 = take(3 * P).rearrange("p (g c) -> p g c", g=3)
        before, ones = take(P), take(P)
        rw = take(KD * 36).rearrange("p (k e) -> p k e", k=KD)
        rb = take(36)
        stat5 = take(NT * 4).rearrange("p (t m) -> p t m", t=NT)
        logit = take(NT * 36).rearrange("p (t e) -> p t e", t=NT)
        expert_row, first_row, fall_row, place = take(NE), take(NE), take(8), take(1)
        token_i = take(NT).bitcast(i32)
        zero = take(512)
        gm, gsum, m1, m2, pk = (take(NT) for _ in range(5))
        og, tg = (take(NT * NG).rearrange("p (t g) -> p t g", g=NG) for _ in range(2))
        s8, t8, o1, o2 = (take(NT * 8).rearrange("p (t e) -> p t e", e=8) for _ in range(4))
        e1, e2, both, slot_f, lsel = (take(NT * NE).rearrange("p (t e) -> p t e", e=NE) for _ in range(5))
        tilebase = take((NT + 1) * NE).rearrange("p (t e) -> p t e", e=NE)
        over, incl, incl2, o32, excl = (take(NE) for _ in range(5))
        lst = take(2)
        lst_i = take(2).bitcast(i32)
        top5 = top[0]
        WEXP = 2 * KD * HID + KH * D
        assert top5 <= ARENA - 2 * KD * HID

        def sp_phase5(sp):
            sp.wait_ge(sem("zero5"), 1)
            sp.dma_start(slot_dram.rearrange("(p n) o -> p (n o)", p=P), zero.bitcast(i32)[:, 0:NBLK * BLK // P]).then_inc(sem("slots_zero"), 16)
            unused = y_dram[NE * BLK:, :].rearrange("(p s) (j n) -> p (s j) n", p=P, n=512)
            sp.dma_start(unused, zero.unsqueeze(1).to_broadcast([P, MAX_OVER * BLK // P * 2, 512])).then_inc(sem("unused_zero"), 16)
            for dst, src in ((sel5, A["c_sel"]), (n2_row, A["norm2_g"][0].partition_broadcast(P)), (before, A["c_before"]),
                             (ones, A["c_ones"]), (rw, A["router_w"]), (rb, A["router_b"].partition_broadcast(P)),
                             (expert_row, A["c_expert"]), (first_row, A["c_first"]), (fall_row, A["c_fall8"]),
                             (place, A["c_place"]), (token_i, A["c_token"])):
                sp.dma_start(dst, src).then_inc(sem("consts5_in"), 16)
            sp.dma_start(wout, A["w_out"][0].rearrange("(k p) n -> p k n", p=P)).then_inc(sem("wout_in"), 16)
            for t in range(NT):
                sp.dma_start(x2[:, t, :], x_tile[t]).then_inc(sem("x5_in"), 16)
            for t in range(NT):
                sp.wait_ge(sem("h2_ready"), t + 1)
                sp.dma_start(h2_dram[t * P:(t + 1) * P, :], h2[t % 2]).then_inc(sem(f"h2_out{t % 2}"), 16)
            sp.wait_ge(sem("list_ready"), 1)
            sp.dma_start(over_dram, lst_i[0:MAX_OVER, :]).then_inc(sem("list_out"), 16)
            sp.wait_ge(sem("list_out"), 16)
            sp.wait_ge(sem("unused_zero"), 16)
            sp.wait_ge(sem("h2_out0"), 48)
            sp.wait_ge(sem("h2_out1"), 48)

        def pool_phase5(pool):
            nc.gpsimd.memset(zero, 0.0).then_inc(sem("zero5"), 1)
            pool.wait_ge(sem("slots_zero"), 16)
            pool.wait_ge(sem("consts5_in"), 16 * 11)
            pool.wait_ge(sem("pos_ready"), 1)
            for t in range(NT):
                for k in range(2):
                    nc.gpsimd.indirect_dma_start(slot_dram, bass.IndirectOffsetOnAxis(ap=pos_i.bitcast(u32)[:, t, k:k + 1], axis=0),
                                                 token_i[:, t:t + 1], None).then_inc(sem("slot_out"), 16)
            pool.wait_ge(sem("slot_out"), 16 * 2 * NT)

        def act_phase5(act):
            own = Own(act, sem("act_own5"))
            for t in range(NT):
                act.wait_ge(sem("x2_ready"), t + 1)
                if t:
                    own.wait(own.n)
                own.link(nc.scalar.activation(sq5, x2[:, t, :], ACT.Square, scale=1.0 / 32.0, accum_out=stat5[:, t, 0:1]))
                own.done(nc.scalar.activation(stat5[:, t, 1:2], stat5[:, t, 0:1], ACT.Sqrt, bias=eps[:, 0:1]))
                if t:
                    h2T_evac(act, t - 1)
            h2T_evac(act, NT - 1)
            act.wait_ge(sem("g_centred"), 1)
            nc.scalar.activation(tg, tg, ACT.Exp).then_inc(sem("g_exp"), 1)
            act.wait_ge(sem("m_diff"), 1)
            nc.scalar.activation(m2, m2, ACT.Exp).then_inc(sem("m_exp"), 1)

        def h2T_evac(act, t):
            for hf in range(2):
                act.wait_ge(sem("h2T_mm"), 2 * t + hf + 1)
                if t >= 2:
                    act.wait_ge(sem("router_mm"), t - 1)
                nc.scalar.copy(h2T[t % 2][:, 4 * hf:4 * hf + 4, :], bank[6 + hf].rearrange("p (k c) -> p k c", k=4)).then_inc(sem("h2T_ready"), 1)

        MODS = [(2, g1_row, None), (3, ss_row, 0), (4, ss_row, 1), (5, g2_row, None)]

        def dve_phase5(dve):
            own = Own(dve, sem("dve_own5"))
            dve.wait_ge(sem("consts5_in"), 16 * 11)
            n = 0
            for m, to, which in MODS:
                for g in range(2):
                    for hf in range(2):
                        dve.wait_ge(sem("row5_mm"), n + 1)
                        cols = slice(hf * 512, hf * 512 + 512)
                        dst = to[:, g, cols] if which is None else to[:, g, which, cols]
                        if which == 1:
                            ins = nc.vector.scalar_tensor_tensor(dst, bank[n % 2], 1.0, n2_row[:, cols], ALU.add, ALU.mult)
                        else:
                            ins = nc.vector.tensor_copy(dst, bank[n % 2])
                        ins.then_inc(sem("row5_ready"), 1)
                        n += 1
            dve.wait_ge(sem("row5_ready"), 16)
            dve.wait_ge(sem("x5_in"), 16 * NT)

            def residual(t):
                tmp = h2[t % 2]
                if t >= 2:
                    dve.wait_ge(sem(f"h2_out{t % 2}"), 16 * (t // 2))
                    dve.wait_ge(sem("h2T_mm"), 2 * (t - 1))
                for hf in range(2):
                    cols = slice(hf * 512, hf * 512 + 512)
                    dve.wait_ge(sem("o5_mm"), 2 * t + hf + 1)
                    k = own.done(nc.vector.tensor_tensor(tmp[:, cols], bank[2 + 2 * (t % 2) + hf], g1_row[:, group(t), cols], ALU.mult))
                own.wait(k)
                nc.vector.tensor_tensor(x2[:, t, :], x2[:, t, :], tmp, ALU.add).then_inc(sem("x2_ready"), 1)

            def norm(t):
                dve.wait_ge(sem("act_own5"), 2 * t + 2)
                own.link(nc.vector.reciprocal(stat5[:, t, 2:3], stat5[:, t, 1:2]))
                own.link(nc.vector.scalar_tensor_tensor(h2[t % 2], x2[:, t, :], stat5[:, t, 2:3], ss_row[:, group(t), 1, :], ALU.mult, ALU.mult))
                nc.vector.tensor_tensor(h2[t % 2], h2[t % 2], ss_row[:, group(t), 0, :], ALU.add).then_inc(sem("h2_ready"), 1)

            def scores(t):
                dve.wait_ge(sem("router_mm"), t + 1)
                nc.vector.tensor_tensor(logit[:, t, :], bank[t % 2][:, 0:36], rb, ALU.add).then_inc(sem("logit_ready"), 1)

            residual(0)
            for t in range(NT):
                if t + 1 < NT:
                    residual(t + 1)
                norm(t)
                if t:
                    scores(t - 1)
            scores(NT - 1)
            dve.wait_ge(sem("logit_ready"), NT)

            def b(ap, shape):
                return ap.unsqueeze(len(ap.shape)).to_broadcast(shape)

            def first_max(one_hot, top_v, values, tmp, width):
                shape = [P, NT, width]
                own.link(nc.vector.tensor_reduce(top_v, values, AX, ALU.max))
                own.link(nc.vector.tensor_tensor(tmp, values, b(top_v, shape), ALU.is_equal))
                own.link(nc.vector.tensor_tensor(tmp, tmp, fall_row[:, 0:width].unsqueeze(1).to_broadcast(shape), ALU.mult))
                own.link(nc.vector.tensor_reduce(pk, tmp, AX, ALU.max))
                own.link(nc.vector.tensor_tensor(one_hot, tmp, b(pk, shape), ALU.is_equal))

            pg = logit[:, :, 0:NG]
            first_max(og, gm, pg, tg, NG)
            nc.vector.tensor_tensor(tg, pg, b(gm, [P, NT, NG]), ALU.subtract).then_inc(sem("g_centred"), 1)
            le = logit[:, :, NG:].rearrange("p t (g e) -> p t g e", g=NG)
            own.link(nc.vector.tensor_tensor(lsel.rearrange("p t (g e) -> p t g e", g=NG), le, b(og, [P, NT, NG, EPG]), ALU.mult))
            own.link(nc.vector.tensor_reduce(s8, lsel.rearrange("p t (g e) -> p t e g", g=NG), AX, ALU.add))
            first_max(o1, m1, s8, t8, EPG)
            own.link(nc.vector.scalar_tensor_tensor(s8, o1, -1e30, s8, ALU.mult, ALU.add))
            first_max(o2, m2, s8, t8, EPG)
            own.link(nc.vector.tensor_tensor(m2, m2, m1, ALU.subtract))
            dve.wait_ge(sem("g_exp"), 1)
            nc.vector.tensor_reduce(gsum, tg, AX, ALU.add).then_inc(sem("m_diff"), 1)
            dve.wait_ge(sem("m_exp"), 1)
            own.link(nc.vector.tensor_scalar(m1, m2, 1.0, None, ALU.add))
            own.link(nc.vector.tensor_tensor(m1, m1, gsum, ALU.mult))
            own.link(nc.vector.reciprocal(wts[:, :, 0], m1))
            own.link(nc.vector.tensor_tensor(wts[:, :, 1], wts[:, :, 0], m2, ALU.mult))
            for one, o8 in ((e1, o1), (e2, o2)):
                own.link(nc.vector.tensor_tensor(one.rearrange("p t (g e) -> p t g e", g=NG), b(og, [P, NT, NG, EPG]),
                                                 o8.unsqueeze(2).to_broadcast([P, NT, NG, EPG]), ALU.mult))
            nc.vector.tensor_tensor(both, e1, e2, ALU.add).then_inc(sem("hits_ready"), 1)
            own.link(nc.vector.memset(tilebase[:, 0, :], 0.0))
            dve.wait_ge(sem("rank_mm"), 2)
            tot = bank[3][:, 0:NT * NE].rearrange("p (t e) -> p t e", e=NE)
            for t in range(NT):
                own.link(nc.vector.tensor_tensor(tilebase[:, t + 1, :], tot[:, t, :], tilebase[:, t, :], ALU.add))
            cnt = tilebase[:, NT, :]
            own.link(nc.vector.tensor_scalar(over, cnt, float(BLK), None, ALU.is_gt))
            for k in range(2, TOK // BLK):
                own.link(nc.vector.scalar_tensor_tensor(over, cnt, float(BLK * k), over, ALU.is_gt, ALU.add))
            own.link(nc.vector.tensor_copy(incl, over))
            a, c = incl, incl2
            for s in (1, 2, 4, 8, 16):
                own.done(nc.vector.tensor_copy(c[:, 0:s], a[:, 0:s]))
                own.link(nc.vector.tensor_tensor(c[:, s:NE], a[:, s:NE], a[:, 0:NE - s], ALU.add))
                a, c = c, a
            own.link(nc.vector.tensor_tensor(excl, a, over, ALU.subtract))
            own.link(nc.vector.tensor_scalar(over, excl, float(NE - 1), float(BLK), ALU.add, ALU.mult))
            own.link(nc.vector.tensor_tensor(over, over, first_row, ALU.subtract))
            own.link(nc.vector.tensor_tensor(slot_f, bank[2][:, 0:NT * NE].rearrange("p (t e) -> p t e", e=NE), tilebase[:, 0:NT, :], ALU.add))
            own.link(nc.vector.scalar_tensor_tensor(lsel, slot_f, float(BLK), over.unsqueeze(1).to_broadcast([P, NT, NE]), ALU.is_ge, ALU.mult))
            own.link(nc.vector.tensor_tensor(slot_f, slot_f, lsel, ALU.add))
            own.link(nc.vector.tensor_tensor(slot_f, slot_f, first_row.unsqueeze(1).to_broadcast([P, NT, NE]), ALU.add))
            for k, one in enumerate((e1, e2)):
                own.link(nc.vector.tensor_tensor(one, one, slot_f, ALU.mult))
                own.link(nc.vector.tensor_reduce(pk, one, AX, ALU.add))
                ins = nc.vector.tensor_copy(pos_i[:, :, k], pk)
                if k == 0:
                    own.link(ins)
            ins.then_inc(sem("pos_ready"), 1)
            own.link(nc.vector.tensor_scalar(o32, a, place, None, ALU.is_gt))
            own.link(nc.vector.scalar_tensor_tensor(o32, excl, place, o32, ALU.is_le, ALU.mult))
            own.link(nc.vector.tensor_tensor(o32, o32, expert_row, ALU.mult))
            own.link(nc.vector.tensor_reduce(lst[:, 0:1], o32, AX, ALU.add))
            own.link(nc.vector.tensor_copy(lst[:, 1:2], a[:, NE - 1:NE]))
            nc.vector.tensor_copy(lst_i, lst).then_inc(sem("list_ready"), 1)

        def pe_phase5(pe):
            pe.wait_ge(sem("consts5_in"), 16 * 11)
            n = 0
            for m, _, _ in MODS:
                for g in range(2):
                    for hf in range(2):
                        if n >= 2:
                            pe.wait_ge(sem("row5_ready"), n - 1)
                        nc.tensor.matmul(bank[n % 2], sel5[:, g, :], modp[:, (2 * m + hf) * 512:(2 * m + hf + 1) * 512],
                                         start=True, stop=True).then_inc(sem("row5_mm"), 1)
                        n += 1
            pe.wait_ge(sem("wout_in"), 16)
            for t in range(NT + 2):
                if t < NT:
                    if t >= 2:
                        pe.wait_ge(sem("x2_ready"), t - 1)
                    for hf in range(2):
                        for k in range(KD):
                            ins = nc.tensor.matmul(bank[2 + 2 * (t % 2) + hf], catT[:, k, t * P:(t + 1) * P], wout[:, k, hf * 512:hf * 512 + 512],
                                                   start=(k == 0), stop=(k == KD - 1))
                        ins.then_inc(sem("o5_mm"), 1)
                if t >= 2:
                    j = t - 2
                    pe.wait_ge(sem("h2_ready"), j + 1)
                    for hf in range(2):
                        if j:
                            pe.wait_ge(sem("h2T_ready"), 2 * (j - 1) + hf + 1)
                        for k in range(4):
                            kk = 4 * hf + k
                            ins = nc.tensor.transpose(bank[6 + hf][:, k * P:(k + 1) * P], h2[j % 2][:, kk * P:(kk + 1) * P], ident)
                        ins.then_inc(sem("h2T_mm"), 1)
                    pe.wait_ge(sem("h2T_ready"), 2 * j + 2)
                    if j >= 2:
                        pe.wait_ge(sem("logit_ready"), j - 1)
                    for k in range(KD):
                        ins = nc.tensor.matmul(bank[j % 2][:, 0:36], h2T[j % 2][:, k, :], rw[:, k, :], start=(k == 0), stop=(k == KD - 1))
                    ins.then_inc(sem("router_mm"), 1)
            pe.wait_ge(sem("hits_ready"), 1)
            hits = both.rearrange("p t e -> p (t e)")
            nc.tensor.matmul(bank[2][:, 0:NT * NE], before, hits, start=True, stop=True).then_inc(sem("rank_mm"), 1)
            nc.tensor.matmul(bank[3][:, 0:NT * NE], ones, hits, start=True, stop=True).then_inc(sem("rank_mm"), 1)

        top[0] = base6
        NSLOT = 2
        HALF = HID // 2
        idx_o = take(1).bitcast(i32)
        idx_c = [take(1).bitcast(i32) for _ in range(2)]
        xg = [take(D) for _ in range(2)]
        xT = [take(KD * BLK).rearrange("p (k c) -> p k c", k=KD) for _ in range(2)]
        sil, hid = take(HALF), take(HALF)
        hidT = take(HALF).rearrange("p (c n t) -> p c n t", c=2, n=2)
        yb = [take(HID) for _ in range(2)]
        top6 = top[0]
        w1_s, w3_s, w2_s = [], [], []
        for k in range(NSLOT):
            top[0] = ARENA - (k + 1) * WEXP
            assert top[0] >= top6, (top[0], top6)
            w2_s.append(take(KH * D).rearrange("p (k n) -> p k n", k=KH))
            w1_s.append(take(KD * HID).rearrange("p (k n) -> p k n", k=KD))
            w3_s.append(take(KD * HID).rearrange("p (k n) -> p k n", k=KD))
        w1_v = A["exp_w1"][0].rearrange("e (k p) n -> e p k n", p=P)
        w3_v = A["exp_w3"][0].rearrange("e (k p) n -> e p k n", p=P)
        w2_v = A["exp_w2"][0].rearrange("e (k p) n -> e p k n", p=P)
        y_v = y_dram.rearrange("s (j n) -> s j n", j=2)

        def one(ap, e):
            return ap[bass.ds(e, 1)].rearrange("o p k n -> p (o k) n")

        CREDIT = 3
        LOOP = 4
        TURNS = NE // LOOP

        class Main:
            over = ""
            credit = CREDIT

            def __init__(self, e, u, n, wn, sn):
                self.e, self.n, self.w, self.wn, self.s, self.sn = e, n, u % NSLOT, wn, u % 2, sn
                self.first_slot = e * BLK

            def sem(self, name):
                return sem(name)

        class Over:
            over = "over_"
            credit = 0

            def __init__(self, m, e=None):
                self.e, self.n, self.w, self.wn, self.s, self.sn = e, m, 0, m, 0, m
                self.first_slot = m * BLK + NE * BLK

            def sem(self, name):
                return sem("over_" + name)

        def turns(eng, body):
            with eng.Fori(0, TURNS) as i:
                for u in range(LOOP):
                    body(Main(i * LOOP + u, u, i * LOOP + u, i * (LOOP // NSLOT) + u // NSLOT, i * (LOOP // 2) + u // 2))
            for u in range(NE - TURNS * LOOP):
                e = TURNS * LOOP + u
                body(Main(e, u, e, e // NSLOT, e // 2))

        def overflow(eng, body, with_expert=False):
            count = eng.value_load(over_dram[0:1, 1:2], min_val=0, max_val=MAX_OVER)
            with eng.If(count > 0):
                with eng.Fori(0, count) as m:
                    e = eng.value_load(over_dram[bass.ds(m, 1), 0:1], min_val=0, max_val=NE - 1) if with_expert else None
                    body(Over(m, e))
            with eng.Else():
                pass

        def sp_phase6(sp):
            def load(c):
                idx = idx_o if c.over else idx_c[c.s]
                if not c.over:
                    sp.wait_ge(sem("xT_mm"), CREDIT + c.n - 1)
                sp.dma_start(idx[0:BLK, :], slot_dram[bass.ds(c.first_slot, BLK), :]).then_inc(c.sem(f"idx_in{c.s}"), 16)
                for name, slot, view in (("h1_mm", w1_s, w1_v), ("h3_mm", w3_s, w3_v), ("y_mm6", w2_s, w2_v)):
                    if not c.over:
                        sp.wait_ge(sem(name), CREDIT + c.n - NSLOT + 1)
                    sp.dma_start(slot[c.w], one(view, c.e)).then_inc(c.sem(f"{name}_w{c.w}"), 16)

            turns(sp, load)

            def over(c):
                sp.wait_ge(sem("over_y_out0"), 32 * c.n + 16)
                load(c)

            sp.wait_ge(sem("y_mm6"), CREDIT + NE)
            overflow(sp, over, with_expert=True)

        def pool_phase6(pool):
            def gather(c):
                pool.wait_ge(c.sem(f"idx_in{c.s}"), 16 * c.sn + 16)
                if not c.over:
                    pool.wait_ge(sem("xT_mm"), CREDIT + c.n - 1)
                pool.sem_inc(sem("pool_turn"), 1)
                idx = idx_o if c.over else idx_c[c.s]
                nc.gpsimd.indirect_dma_start(xg[c.s][0:BLK, :], None, h2_dram,
                                             bass.IndirectOffsetOnAxis(ap=idx.bitcast(u32)[0:BLK, :], axis=0)).then_inc(c.sem(f"xg_in{c.s}"), 16)

            turns(pool, gather)
            overflow(pool, gather)

        def act_phase6(act):
            for name in ("y_out0", "y_out1", "over_y_out0"):
                act.sem_inc(sem(name), 16)
            for name in ("xT_ready", "sil_ready", "hidT_ready"):
                act.sem_inc(sem(name), CREDIT)

            def body(c):
                k = c.credit + c.n + 1
                act.wait_ge(c.sem("xT_mm"), k)
                if not c.over:
                    act.wait_ge(sem("h3_mm"), k - 2)
                nc.scalar.copy(xT[c.s], bank[0].rearrange("p (k c) -> p k c", k=KD)).then_inc(c.sem("xT_ready"), 1)
                act.wait_ge(c.sem("h1_mm"), k)
                if not c.over:
                    act.wait_ge(sem("hid_ready"), k - 1)
                nc.scalar.activation(sil, bank[1 + 2 * c.s][:, 0:HALF], ACT.Silu).then_inc(c.sem("sil_ready"), 1)
                act.wait_ge(c.sem("hidT_mm"), k)
                if not c.over:
                    act.wait_ge(sem("y_mm6"), k - 1)
                nc.scalar.copy(hidT, bank[5][:, 0:HALF].rearrange("p (c n t) -> p c n t", c=2, n=2)).then_inc(c.sem("hidT_ready"), 1)
                act.wait_ge(c.sem("y_ready6"), k)
                for j in range(2):
                    act.dma_start(y_v[bass.ds(c.first_slot, BLK), j, :], yb[c.s][j * BLK:(j + 1) * BLK, :]).then_inc(c.sem(f"y_out{c.s}"), 16)

            turns(act, body)
            act.wait_ge(sem("y_out0"), 16 + 32 * NE // 2)
            act.wait_ge(sem("y_out1"), 16 + 32 * NE // 2)

            def over(c):
                body(c)
                act.wait_ge(sem("over_y_out0"), 32 * c.n + 48)

            overflow(act, over)

        def dve_phase6(dve):
            for name in ("hid_ready", "y_ready6"):
                dve.sem_inc(sem(name), CREDIT)

            def body(c):
                k = c.credit + c.n + 1
                dve.wait_ge(c.sem("sil_ready"), k)
                dve.wait_ge(c.sem("h3_mm"), k)
                if not c.over:
                    dve.wait_ge(sem("hidT_mm"), k - 1)
                nc.vector.tensor_tensor(hid, bank[2 + 2 * c.s][:, 0:HALF], sil, ALU.mult).then_inc(c.sem("hid_ready"), 1)
                dve.wait_ge(c.sem("y_mm6"), k)
                if not c.over:
                    dve.wait_ge(sem(f"y_out{c.s}"), 32 * c.sn + 16)
                nc.vector.tensor_copy(yb[c.s], bank[6 + c.s]).then_inc(c.sem("y_ready6"), 1)

            turns(dve, body)
            overflow(dve, body)

        def pe_phase6(pe):
            for name in ("xT_mm", "h1_mm", "h3_mm", "hidT_mm", "y_mm6"):
                pe.sem_inc(sem(name), CREDIT)

            def body(c):
                k = c.credit + c.n + 1
                pe.wait_ge(c.sem(f"xg_in{c.s}"), 16 * c.sn + 16)
                if not c.over:
                    pe.wait_ge(sem("xT_ready"), k - 1)
                pe.sem_inc(sem("pe_turn"), 1)
                for j in range(KD):
                    ins = nc.tensor.transpose(bank[0][:, j * BLK:(j + 1) * BLK], xg[c.s][0:BLK, j * P:(j + 1) * P], ident[0:BLK, 0:BLK])
                ins.then_inc(c.sem("xT_mm"), 1)
                pe.wait_ge(c.sem("xT_ready"), k)
                for name, slot, b, free in (("h1_mm", w1_s, 1, "sil_ready"), ("h3_mm", w3_s, 2, "hid_ready")):
                    pe.wait_ge(c.sem(f"{name}_w{c.w}"), 16 * c.wn + 16)
                    if not c.over:
                        pe.wait_ge(sem(free), k - 2)
                    for j in range(KD):
                        for n in range(2):
                            ins = nc.tensor.matmul(bank[b + 2 * c.s][BLK * n:BLK * n + BLK, 0:HALF], xT[c.s][:, j, :],
                                                   slot[c.w][:, j, n * HALF:(n + 1) * HALF], start=(j == 0), stop=(j == KD - 1))
                    ins.then_inc(c.sem(name), 1)
                pe.wait_ge(c.sem("hid_ready"), k)
                if not c.over:
                    pe.wait_ge(sem("hidT_ready"), k - 1)
                for j in range(2):
                    ins = nc.tensor.transpose(bank[5][:, j * P:(j + 1) * P], hid[:, j * P:(j + 1) * P], ident)
                ins.then_inc(c.sem("hidT_mm"), 1)
                pe.wait_ge(c.sem("hidT_ready"), k)
                pe.wait_ge(c.sem(f"y_mm6_w{c.w}"), 16 * c.wn + 16)
                if not c.over:
                    pe.wait_ge(sem("y_ready6"), k - 2)
                for j in range(KH):
                    for n in range(2):
                        ins = nc.tensor.matmul(bank[6 + c.s][BLK * n:BLK * n + BLK, :], hidT[:, j % 2, j // 2, :],
                                               w2_s[c.w][:, j, n * 512:(n + 1) * 512], start=(j == 0), stop=(j == KH - 1))
                ins.then_inc(c.sem("y_mm6"), 1)

            turns(pe, body)
            overflow(pe, body)

        top[0] = base6
        ya = [[take(D) for _ in range(2)] for _ in range(2)]
        sq7 = take(D)
        yo = [take(D) for _ in range(2)]
        f_row = take(D)
        stat7 = take(NT * 4).rearrange("p (t m) -> p t m", t=NT)
        y_out_v = [O[1][0, t * P:(t + 1) * P, :] for t in range(NT_S)] + [O[0][0, t * P:(t + 1) * P, :] for t in range(NT_P)]

        def sp_phase7(sp):
            sp.dma_start(f_row, A["final_row"].partition_broadcast(P)).then_inc(sem("final_in"), 16)
            for t in range(NT):
                sp.wait_ge(sem("final_ready"), t + 1)
                sp.dma_start(y_out_v[t], yo[t % 2]).then_inc(sem(f"final_out{t % 2}"), 16)
            sp.wait_ge(sem("final_out0"), 16 * NT // 2)
            sp.wait_ge(sem("final_out1"), 16 * NT // 2)

        def pool_phase7(pool):
            for t in range(NT):
                if t >= 2:
                    pool.wait_ge(sem("joined"), t - 1)
                for k in range(2):
                    nc.gpsimd.indirect_dma_start(ya[t % 2][k], None, y_dram,
                                                 bass.IndirectOffsetOnAxis(ap=pos_i.bitcast(u32)[:, t, k:k + 1], axis=0)).then_inc(sem(f"rows_in{t % 2}"), 16)

        def act_phase7(act):
            own = Own(act, sem("act_own7"))
            for t in range(NT):
                act.wait_ge(sem("joined"), t + 1)
                if t:
                    own.wait(own.n)
                own.link(nc.scalar.activation(sq7, x2[:, t, :], ACT.Square, scale=1.0 / 32.0, accum_out=stat7[:, t, 0:1]))
                own.done(nc.scalar.activation(stat7[:, t, 1:2], stat7[:, t, 0:1], ACT.Sqrt, bias=eps[:, 0:1]))

        def dve_phase7(dve):
            own = Own(dve, sem("dve_own7"))
            dve.wait_ge(sem("final_in"), 16)

            def join(t):
                a, b = ya[t % 2]
                dve.wait_ge(sem(f"rows_in{t % 2}"), 32 * (t // 2 + 1))
                own.link(nc.vector.tensor_scalar(a, a, wts[:, t, 0:1], None, ALU.mult))
                own.link(nc.vector.scalar_tensor_tensor(a, b, wts[:, t, 1:2], a, ALU.mult, ALU.add))
                nc.vector.tensor_tensor(a, a, g2_row[:, group(t), :], ALU.mult).then_inc(sem("joined0"), 1)
                dve.wait_ge(sem("joined0"), t + 1)
                nc.vector.tensor_tensor(x2[:, t, :], x2[:, t, :], a, ALU.add).then_inc(sem("joined"), 1)

            def norm(t):
                dve.wait_ge(sem("act_own7"), 2 * t + 2)
                if t >= 2:
                    dve.wait_ge(sem(f"final_out{t % 2}"), 16 * (t // 2))
                own.link(nc.vector.reciprocal(stat7[:, t, 2:3], stat7[:, t, 1:2]))
                nc.vector.scalar_tensor_tensor(yo[t % 2], x2[:, t, :], stat7[:, t, 2:3], f_row, ALU.mult, ALU.mult).then_inc(sem("final_ready"), 1)

            for t in range(NT):
                join(t)
                if t:
                    norm(t - 1)
            norm(NT - 1)

        def run_phase(sp=None, pool=None, act=None, dve=None, pe=None):
            with nc.Block() as block:
                for engine, own_program in ((block.sync, sp), (block.gpsimd, pool), (block.scalar, act), (block.vector, dve), (block.tensor, pe)):
                    if own_program is not None:
                        engine(own_program)
            nc.clear_and_free_semaphores(list(sems.values()))
            sems.clear()
            nc.all_engine_barrier()

        for programs in ((sp_phase1, pool_phase1, act_phase1, dve_phase1, pe_phase1),
                         (sp_phase2, pool_phase2, act_phase2, dve_phase2, pe_phase2),
                         (sp_phase3, pool_phase3, act_phase3, dve_phase3, pe_phase3),
                         (sp_phase4, pool_phase4, act_phase4, dve_phase4, pe_phase4),
                         (sp_phase5, pool_phase5, act_phase5, dve_phase5, pe_phase5),
                         (sp_phase6, pool_phase6, act_phase6, dve_phase6, pe_phase6),
                         (sp_phase7, pool_phase7, act_phase7, dve_phase7, None))[:upto]:
            run_phase(*programs)


def layout(inputs):
    a = {k: np.ascontiguousarray(np.asarray(v)) for k, v in inputs.items()}
    a["c_cols"] = np.ascontiguousarray(np.stack([a.pop("c_sample")[0], a.pop("c_prompt")[0]], -1)
                                       .reshape(KD, P, 2).transpose(1, 0, 2))
    a["mu"] = np.ascontiguousarray(a.pop("rwkv_mu")[0].reshape(2, NZ, P).transpose(2, 1, 0))
    rpb = a.pop("na_rpb")[0]
    pad = np.pad(rpb, ((0, 0), (0, 0), (16, 16)))
    i, m = np.arange(8)[:, None, None, None], np.arange(8)[None, None, :, None]
    qc, kc = np.arange(QB)[None, :, None, None], np.arange(KB)[None, None, None, :]
    bias = np.stack([pad[:, m - i + 7, kc + off - qc + 15 + 16] for off in (0, -8, -16)])
    a["bias"] = np.ascontiguousarray(bias.reshape(3, NH, P, 8 * KB).transpose(0, 2, 1, 3))
    a["router_w"] = np.ascontiguousarray(np.concatenate([a.pop("router_g_w")[0], a.pop("router_e_w")[0]], 1)
                                         .reshape(KD, P, NG + NE).transpose(1, 0, 2))
    a["router_b"] = np.concatenate([a.pop("router_g_b")[0], a.pop("router_e_b")[0]])
    a["final_row"] = a.pop("final_g")
    a.update(constants())
    return a


def program(nc, inputs, upto=7):
    arrays = {f"in_{k}": v for k, v in layout(inputs).items()}
    A = {k[3:]: nc.dram_tensor(k, v.shape, mybir.dt.from_np(v.dtype), kind="ExternalInput").ap() for k, v in arrays.items()}
    O = [nc.dram_tensor("y_prompt", (1, T_P, D), f32, kind="ExternalOutput").ap(),
         nc.dram_tensor("y_sample", (1, T_S, D), f32, kind="ExternalOutput").ap()]
    build(nc, A, O, upto)
    return arrays


def kernel(**inputs):
    import concourse.bacc as bacc
    from concourse.bass_utils import run_bass_kernel_spmd

    nc = bacc.Bacc("TRN2", target_bir_lowering=False, num_devices=1)
    arrays = program(nc, inputs)
    r = run_bass_kernel_spmd(nc, [arrays], core_ids=[0])
    return r.results[0]["y_prompt"], r.results[0]["y_sample"]
```

```python
from contextlib import ExitStack

import numpy as np

import concourse.bass as bass
import concourse.mybir as mybir

f32 = mybir.dt.float32
f16 = mybir.dt.float16
i32 = mybir.dt.int32
u32 = mybir.dt.uint32
ALU = mybir.AluOpType
ACT = mybir.ActivationFunctionType
AX = mybir.AxisListType.X

P = 128
D = 1024
KD = D // P
T_S, T_P = 512, 256
NT_S, NT_P = T_S // P, T_P // P
NT = NT_S + NT_P
TOK = NT * P
W = 512
HD = 64
NH = W // HD
NPAIR = NH // 2
GW = 64
QB, KB = 16, 32
NQB = GW // QB
NZ = 15
ZLORA = 12
NE, EPG, NG = 32, 8, 4
HID = 512
KH = HID // P
BLK = 64
MAX_OVER = 2 * TOK // BLK
NBLK = NE + MAX_OVER
EPS = 1e-6
LNX_EPS = 64e-5
DECAY = float(np.exp(-0.5))
BIG = 3.0e38
U_SCALE = 2048.0
LEVELS = 7


class Own:

    def __init__(self, eng, sem):
        self.eng, self.sem, self.n = eng, sem, 0

    def done(self, ins):
        self.n += 1
        ins.then_inc(self.sem, 1)
        return self.n

    def wait(self, value):
        self.eng.wait_ge(self.sem, value)

    def link(self, ins):
        self.wait(self.done(ins))


def constants():
    j, t = np.arange(P)[:, None], np.arange(P)[None, :]
    half = (np.arange(P) < P // 2).astype(np.float32)
    c = {}
    c["c_ident"] = np.eye(P, dtype=np.float32)
    c["c_ident16"] = np.eye(P, dtype=np.float16)
    c["c_tri"] = np.stack([(j <= t) - half[:, None], (j >= t) - (1 - half)[:, None]]).astype(np.float32).transpose(1, 0, 2)
    c["c_mid"] = np.stack([np.stack([half, 1 - half], 1), np.stack([1 - half, half], 1)]).astype(np.float32).transpose(1, 0, 2)
    seen = [np.concatenate([j < t, j <= t], 1), np.concatenate([j >= t, j > t], 1)]
    c["c_seen"] = np.stack([np.concatenate([m, m], 1) for m in seen]).astype(np.float32).transpose(1, 0, 2)
    c["c_pair"] = np.kron(np.eye(2), np.ones((HD, HD))).astype(np.float32)
    sel = np.zeros((P, 3, P), np.float32)
    for g in range(2):
        sel[g::32, g] = 1
    sel[0, 2, 0:2] = 1
    c["c_sel"] = sel
    before = np.zeros((P, P), np.float32)
    before[j < t] = 1
    c["c_before"] = before
    c["c_eps"] = np.tile(np.array([EPS, LNX_EPS], np.float32), (P, 1))
    c["c_ones"] = np.ones((P, P), np.float32)
    qc = np.arange(QB)
    mask = np.zeros((3, P, KB), np.float32)
    for kind, n in enumerate((0, 1, 3)):
        cols = n * QB + qc
        start = np.clip(n * QB - QB // 2, 0, GW - KB)
        win = np.clip(cols - 8, 0, GW - 16)
        kc = start + np.arange(KB)
        ok = (kc >= win[:, None]) & (kc < win[:, None] + 16)
        mask[kind] = np.tile(np.where(ok, 0.0, -1e30), (8, 1))
    c["c_window"] = np.ascontiguousarray(mask.transpose(1, 0, 2))
    e = np.arange(NE, dtype=np.float32)
    c["c_expert"] = np.tile(e, (P, 1))
    c["c_fall8"] = np.tile(8.0 - np.arange(8, dtype=np.float32), (P, 1))
    c["c_first"] = np.tile(e * BLK, (P, 1))
    c["c_place"] = np.arange(P, dtype=np.float32)[:, None].copy()
    c["c_token"] = (np.arange(NT)[None, :] * P + np.arange(P)[:, None]).astype(np.int32)
    return {k: np.ascontiguousarray(v) for k, v in c.items()}


def group(t):
    return 0 if t < NT_S else 1


def band(n):
    return min(max(n * QB - QB // 2, 0), GW - KB)


def build(nc, A, O, upto=7):
    ctx = ExitStack()
    with ctx:
        sems = {}

        def sem(name):
            if name not in sems:
                sems[name] = nc.alloc_semaphore(name=name)
            return sems[name]

        def dram(name, shape, dt=f32):
            return nc.dram_tensor(name, shape, dt, kind="Internal").ap()

        ARENA = 53200
        arena = ctx.enter_context(nc.sbuf_tensor("arena", [P, ARENA], f32))
        top = [0]

        def take(n):
            at = top[0]
            top[0] += n
            assert top[0] <= ARENA, top[0]
            return arena[:, at:at + n]

        bank = [ctx.enter_context(nc.psum_tensor(f"bank{i}", [P, 512], f32))[:, :] for i in range(8)]

        v_dram = dram("v_scratch", [TOK, W])
        dir_dram = dram("direction_scratch", [2, 3, NT, P, W])
        h2_dram = dram("h2_scratch", [TOK, D])
        slot_dram = dram("slot_token", [NBLK * BLK, 1], i32)
        y_dram = dram("slot_out", [NBLK * BLK, D])
        over_dram = dram("overflow_list", [MAX_OVER, 2], i32)

        ident = take(P)
        eps = take(2)
        modp = take(6 * D)
        catT = take(KD * TOK).rearrange("p (c t) -> p c t", c=KD)
        hT = catT
        base5 = top[0]
        ident16 = take(P // 2).bitcast(f16)
        kk_row, ka_row, rk_row, lg_row, lb_row = (take(W) for _ in range(5))
        rkv = take(3 * NT * W).rearrange("p (q t c) -> p q t c", q=3, t=NT)
        kkn = take(NT * W).rearrange("p (t c) -> p t c", t=NT)
        gate = take(NT * W).rearrange("p (t c) -> p t c", t=NT)
        bonus = take(NT * NH).rearrange("p (t h) -> p t h", t=NT)
        base4 = top[0]
        qT = take(NPAIR * TOK).rearrange("p (c t) -> p c t", c=NPAIR)
        kT = take(NPAIR * TOK).rearrange("p (c t) -> p c t", c=NPAIR)
        base3 = top[0]

        top[0] = base3
        adaw = [take(KD * 512).rearrange("p (k n) -> p k n", k=KD) for _ in range(2)]
        NWIN = 3
        winb = [take(KD * P).rearrange("p (k n) -> p k n", k=KD) for _ in range(NWIN)]
        lz = take(3 * TOK).rearrange("p (c t) -> p c t", c=3)
        sel = take(3 * P).rearrange("p (g c) -> p g c", g=3)
        mu = take(NZ * 3).rearrange("p (c m) -> p c m", m=3)
        cT = take(KD * 2).rearrange("p (k g) -> p k g", g=2)
        siluT = take(KD * 32).rearrange("p (k m) -> p k m", k=KD)
        stat = take(NT * 4).rearrange("p (t m) -> p t m", t=NT)
        at_rkv = top[0]
        top[0] = base5 + P // 2 + 5 * W
        xb = [take(D) for _ in range(2)]
        hb = [take(D) for _ in range(2)]
        rows = take(4 * D).rearrange("p (g m d) -> p g m d", g=2, m=2)
        n1_row = take(D)
        sq1 = take(D)
        adab = [take(512) for _ in range(2)]
        zs = [take(TOK) for _ in range(2)]
        top[0] = at_rkv

        x_tile = [A["x_sample"][0, t * P:(t + 1) * P, :] for t in range(NT_S)] + \
                 [A["x_prompt"][0, t * P:(t + 1) * P, :] for t in range(NT_P)]
        ada_v = A["ada_w"][0].rearrange("(k p) n -> p k n", p=P)
        win_v = A["w_in"][0].rearrange("(k p) n -> p k n", p=P)
        ZCOL = 3 * W
        order = [("z", ZLORA + i, ZCOL + (ZLORA + i) * P) for i in range(3)]
        order += [("z", i, ZCOL + i * P) for i in range(ZLORA)]
        order += [("q", i, i * P) for i in range(NPAIR)] + [("k", i, W + i * P) for i in range(NPAIR)]
        NCHUNK = 6 * D // 512
        ring = [("ada", c) for c in range(NCHUNK)] + [("wv", 0)]
        TMOD = len(order) - (NCHUNK - 4)

        def sp_phase1(sp):
            small = [(ident, A["c_ident"]), (eps, A["c_eps"]), (ident16, A["c_ident16"]),
                     (kk_row, A["rwkv_kk"][0].partition_broadcast(P)), (ka_row, A["rwkv_ka"][0].partition_broadcast(P)),
                     (rk_row, A["rwkv_rk"][0].partition_broadcast(P)), (lg_row, A["rwkv_lnx_g"][0].partition_broadcast(P)),
                     (lb_row, A["rwkv_lnx_b"][0].partition_broadcast(P)),
                     (n1_row, A["norm1_g"][0].partition_broadcast(P)), (sel, A["c_sel"]), (mu[:, :, 0:2], A["mu"]),
                     (cT, A["c_cols"])]
            sp.dma_start(small[-1][0], small[-1][1]).then_inc(sem("consts_in"), 16)

            def wide(i):
                kind, c = ring[i]
                if i >= 2:
                    sp.wait_ge(sem("mod_mm"), i - 1)
                s = sem(f"wide_in{i % 2}")
                if kind == "ada":
                    sp.dma_start(adaw[i % 2], ada_v[:, :, c * 512:(c + 1) * 512]).then_inc(s, 16)
                    sp.dma_start(adab[i % 2][0:1, :], A["ada_b"][0:1, c * 512:(c + 1) * 512]).then_inc(s, 16)
                else:
                    sp.dma_start(adaw[i % 2], win_v[:, :, 2 * W:3 * W]).then_inc(s, 32)

            def win(i):
                if i >= NWIN:
                    sp.wait_ge(sem("proj_mm"), i - NWIN + 1)
                c = order[i][2]
                sp.dma_start(winb[i % NWIN], win_v[:, :, c:c + P]).then_inc(sem(f"win_in{i % NWIN}"), 16)

            def x(t):
                if t >= 2:
                    sp.wait_ge(sem("x_used"), t - 1)
                sp.dma_start(xb[t % 2], x_tile[t]).then_inc(sem(f"x_in{t % 2}"), 16)

            wide(0)
            for dst, src in small[:-1]:
                sp.dma_start(dst, src).then_inc(sem("consts_in"), 16)
            x(0)
            x(1)
            for i in range(1, 4):
                wide(i)
            for i in range(NWIN):
                win(i)
            for t in range(2, NT):
                x(t)
            wide(4)
            wide(5)
            for i in range(NWIN, len(order)):
                win(i)
                if i >= TMOD + NWIN:
                    wide(6 + i - TMOD - NWIN)
            for i in range(6 + len(order) - TMOD - NWIN, len(ring)):
                wide(i)

        def pool_phase1(pool):
            nc.gpsimd.memset(siluT, 0.0).then_inc(sem("silu_zero"), 1)

        def act_phase1(act):
            own = Own(act, sem("act_own"))
            act.wait_ge(sem("consts_in"), 16 * 12)
            act.wait_ge(sem("silu_zero"), 1)
            nc.scalar.activation(siluT[:, :, 0:2], cT, ACT.Silu).then_inc(sem("silu_ready"), 1)

            def mod(i, at):
                act.wait_ge(sem("mod_mm"), i + 1)
                nc.scalar.copy(modp[:, at * 512:(at + 1) * 512], bank[i % 2]).then_inc(sem("mod_ready"), 1)

            for i in range(4):
                mod(i, i)

            def rms(t):
                act.wait_ge(sem(f"x_in{t % 2}"), 16 * (t // 2 + 1))
                if t:
                    own.wait(own.n)
                own.link(nc.scalar.activation(sq1, xb[t % 2], ACT.Square, scale=1.0 / 32.0, accum_out=stat[:, t, 0:1]))
                own.done(nc.scalar.activation(stat[:, t, 1:2], stat[:, t, 0:1], ACT.Sqrt, bias=eps[:, 0:1]))

            rms(0)
            rms(1)
            for t in range(NT):
                act.wait_ge(sem("hT_mm"), 2 * t + 1)
                nc.scalar.copy(hT[:, 0:4, t * P:(t + 1) * P], bank[2].rearrange("p (k c) -> p k c", k=4)).then_inc(sem("hT_act"), 1)
                if t + 2 < NT:
                    rms(t + 2)
            for i, (kind, c, _) in enumerate(order):
                b0, b1 = bank[4 + i % 2], bank[6 + i % 2]
                act.wait_ge(sem("proj_mm"), i + 1)
                if kind in "qk":
                    dst = qT if kind == "q" else kT
                    s = float(HD) ** -0.5 if kind == "q" else 1.0
                    for lo, hi, src in ((0, T_S, b0), (T_S, TOK, b1[:, 0:T_P])):
                        to = dst[:, c, lo:hi]
                        if kind == "q":
                            to = to.rearrange("p (n r c) -> p r n c", n=NQB, c=QB)
                            src = src.rearrange("p (r n c) -> p r n c", n=NQB, c=QB)
                        nc.scalar.mul(to, src, s).then_inc(sem("proj_act"), 1)
                else:
                    if i == 0:
                        act.wait_ge(sem("mu_ready"), 1)
                    dst = lz[:, c - ZLORA, :] if c >= ZLORA else zs[i % 2]
                    if c < ZLORA and i >= 5:
                        act.wait_ge(sem("z_tr"), i - 4)
                    nc.scalar.mul(dst[:, 0:T_S], b0, mu[:, c, 2:3]).then_inc(sem("proj_act"), 1)
                    nc.scalar.mul(dst[:, T_S:TOK], b1[:, 0:T_P], mu[:, c, 2:3]).then_inc(sem("proj_act"), 1)
                    if c < ZLORA and i >= 4:
                        act_z_evac(act, i - 1)
                if i == 15:
                    act_z_evac(act, 14)
                if i >= TMOD:
                    mod(i - TMOD + 4, i - TMOD + 4)
            for i, t in enumerate(range(NT)):
                act.wait_ge(sem("v_mm"), i + 1)
                if i >= 2:
                    act.wait_ge(sem(f"v_out{i % 2}"), 16 * (i // 2))
                nc.scalar.copy(zs[i % 2][:, 0:W], bank[2 + i % 2]).then_inc(sem("v_ready"), 1)
                act.wait_ge(sem("v_ready"), i + 1)
                act.dma_start(v_dram[t * P:(t + 1) * P, :], zs[i % 2][:, 0:W]).then_inc(sem(f"v_out{i % 2}"), 16)
            act.wait_ge(sem("v_out0"), 48)
            act.wait_ge(sem("v_out1"), 48)

        def act_z_evac(act, i):
            c = order[i][1]
            act.wait_ge(sem("z_tr"), i - 2)
            nc.scalar.copy(rkv[:, c // 4, 0:NT_S, (c % 4) * P:(c % 4 + 1) * P],
                           bank[i % 2].rearrange("p (t c) -> p t c", t=4)).then_inc(sem("z_act"), 1)

        def dve_z_evac(dve, i):
            c = order[i][1]
            dve.wait_ge(sem("z_tr"), i - 2)
            nc.vector.tensor_copy(rkv[:, c // 4, NT_S:NT, (c % 4) * P:(c % 4 + 1) * P],
                                  bank[2 + i % 2][:, 0:256].rearrange("p (t c) -> p t c", t=2)).then_inc(sem("z_dve"), 1)

        def dve_phase1(dve):
            own = Own(dve, sem("dve_own"))
            dve.wait_ge(sem("consts_in"), 16 * 12)
            own.link(nc.vector.tensor_tensor(mu[:, :, 2], mu[:, :, 0], mu[:, :, 1], ALU.add))
            nc.vector.tensor_scalar(mu[:, :, 2], mu[:, :, 2], -1.0, 1.0, ALU.mult, ALU.add).then_inc(sem("mu_ready"), 1)
            n = 0
            for m in range(2):
                for g in range(2):
                    for hf in range(2):
                        dve.wait_ge(sem("row_mm"), n + 1)
                        dst = rows[:, g, m, hf * 512:(hf + 1) * 512]
                        if m == 0:
                            ins = nc.vector.tensor_copy(dst, bank[n % 2])
                        else:
                            ins = nc.vector.scalar_tensor_tensor(dst, bank[n % 2], 1.0, n1_row[:, hf * 512:(hf + 1) * 512],
                                                                 ALU.add, ALU.mult)
                        ins.then_inc(sem("row_ready"), 1)
                        n += 1
            dve.wait_ge(sem("row_ready"), 8)

            def hT_evac(t):
                dve.wait_ge(sem("hT_mm"), 2 * t + 2)
                nc.vector.tensor_copy(hT[:, 4:8, t * P:(t + 1) * P], bank[3].rearrange("p (k c) -> p k c", k=4)).then_inc(sem("hT_dve"), 1)

            for t in range(NT):
                if t >= 2:
                    dve.wait_ge(sem("hT_mm"), 2 * t - 2)
                dve.wait_ge(sem("act_own"), 2 * t + 2)
                own.link(nc.vector.reciprocal(stat[:, t, 2:3], stat[:, t, 1:2]))
                ins = nc.vector.scalar_tensor_tensor(hb[t % 2], xb[t % 2], stat[:, t, 2:3], rows[:, group(t), 1, :], ALU.mult, ALU.mult)
                ins.then_inc(sem("x_used"), 1)
                dve.wait_ge(sem("x_used"), t + 1)
                nc.vector.tensor_tensor(hb[t % 2], hb[t % 2], rows[:, group(t), 0, :], ALU.add).then_inc(sem("h_ready"), 1)
                if t:
                    hT_evac(t - 1)
            hT_evac(NT - 1)
            for i, (kind, c, _) in enumerate(order):
                if kind != "z":
                    if i == 15:
                        dve_z_evac(dve, 14)
                    continue
                b0, b1 = bank[4 + i % 2], bank[6 + i % 2]
                dst = lz[:, c - ZLORA, :] if c >= ZLORA else zs[i % 2]
                dve.wait_ge(sem("proj_act"), 2 * i + 2)
                own.done(nc.vector.scalar_tensor_tensor(dst[:, 1:T_S], b0[:, 0:T_S - 1], mu[:, c, 0:1], dst[:, 1:T_S], ALU.mult, ALU.add))
                k = own.done(nc.vector.scalar_tensor_tensor(dst[:, T_S + 1:TOK], b1[:, 0:T_P - 1], mu[:, c, 0:1], dst[:, T_S + 1:TOK], ALU.mult, ALU.add))
                own.wait(k)
                nc.vector.scalar_tensor_tensor(dst[:, 0:T_S - 1], b0[:, 1:T_S], mu[:, c, 1:2], dst[:, 0:T_S - 1], ALU.mult, ALU.add).then_inc(sem("z_ready"), 1)
                nc.vector.scalar_tensor_tensor(dst[:, T_S:TOK - 1], b1[:, 1:T_P], mu[:, c, 1:2], dst[:, T_S:TOK - 1], ALU.mult, ALU.add).then_inc(sem("z_ready"), 1)
                if c < ZLORA and i >= 4:
                    dve_z_evac(dve, i - 1)

        def pe_phase1(pe):
            def mod(i, r):
                pe.wait_ge(sem(f"wide_in{r % 2}"), 32 * (r // 2 + 1))
                if i >= 2:
                    pe.wait_ge(sem("mod_ready"), i - 1)
                for k in range(2):
                    for q in range(4):
                        nc.tensor.matmul(bank[i % 2][32 * q:32 * q + 32, :], siluT[:, 2 * q + k, :], adaw[r % 2][:, 2 * q + k, :],
                                         start=(k == 0), stop=(k == 1 and q > 0), tile_position=(0, 32 * q))
                nc.tensor.matmul(bank[i % 2][0:32, :], sel[0:1, 2, 0:32], adab[r % 2][0:1, :],
                                 start=False, stop=True).then_inc(sem("mod_mm"), 1)

            pe.wait_ge(sem("silu_ready"), 1)
            pe.wait_ge(sem("consts_in"), 16 * 12)
            for i in range(4):
                mod(i, i)
            pe.wait_ge(sem("mod_ready"), 4)
            n = 0
            for m in range(2):
                for g in range(2):
                    for hf in range(2):
                        if n >= 2:
                            pe.wait_ge(sem("row_ready"), n - 1)
                        c = m * 2 + hf
                        nc.tensor.matmul(bank[n % 2], sel[:, g, :], modp[:, c * 512:(c + 1) * 512], start=True, stop=True).then_inc(sem("row_mm"), 1)
                        n += 1
            for t in range(NT):
                pe.wait_ge(sem("h_ready"), t + 1)
                for hf in range(2):
                    if t:
                        pe.wait_ge(sem("hT_act" if hf == 0 else "hT_dve"), t)
                    for k in range(4):
                        ins = nc.tensor.transpose(bank[2 + hf][:, k * P:(k + 1) * P], hb[t % 2][:, (hf * 4 + k) * P:(hf * 4 + k + 1) * P], ident)
                    ins.then_inc(sem("hT_mm"), 1)
            pe.wait_ge(sem("hT_act"), NT)
            pe.wait_ge(sem("hT_dve"), NT)

            def z_transposes(i):
                pe.wait_ge(sem("z_ready"), 2 * i + 2)
                if i >= 5:
                    pe.wait_ge(sem("z_act"), i - 4)
                    pe.wait_ge(sem("z_dve"), i - 4)
                for t in range(NT):
                    dst = bank[i % 2][:, t * P:(t + 1) * P] if t < NT_S else bank[2 + i % 2][:, (t - NT_S) * P:(t - NT_S + 1) * P]
                    ins = nc.tensor.transpose(dst, zs[i % 2][:, t * P:(t + 1) * P], ident)
                ins.then_inc(sem("z_tr"), 1)

            for i, (kind, c, _) in enumerate(order):
                pe.wait_ge(sem(f"win_in{i % NWIN}"), 16 * (i // NWIN + 1))
                if i >= 2:
                    pe.wait_ge(sem("proj_act"), 2 * (i - 1))
                    if order[i - 2][0] == "z":
                        pe.wait_ge(sem("z_ready"), 2 * (i - 1))
                for k in range(KD):
                    nc.tensor.matmul(bank[4 + i % 2], winb[i % NWIN][:, k, :], hT[:, k, 0:T_S], start=(k == 0), stop=(k == KD - 1))
                    ins = nc.tensor.matmul(bank[6 + i % 2][:, 0:T_P], winb[i % NWIN][:, k, :], hT[:, k, T_S:TOK], start=(k == 0), stop=(k == KD - 1))
                ins.then_inc(sem("proj_mm"), 1)
                if 4 <= i <= 15:
                    z_transposes(i - 1)
                if i >= TMOD:
                    if i == TMOD:
                        pe.wait_ge(sem("z_act"), 12)
                        pe.wait_ge(sem("z_dve"), 12)
                    mod(i - TMOD + 4, i - TMOD + 4)
            pe.wait_ge(sem("wide_in0"), 32 * (NCHUNK // 2 + 1))
            pe.wait_ge(sem("mod_ready"), NCHUNK)
            pe.wait_ge(sem("z_act"), 12)
            pe.wait_ge(sem("z_dve"), 12)
            for t in range(NT):
                if t >= 2:
                    pe.wait_ge(sem("v_ready"), t - 1)
                for k in range(KD):
                    ins = nc.tensor.matmul(bank[2 + t % 2], hT[:, k, t * P:(t + 1) * P], adaw[0][:, k, :], start=(k == 0), stop=(k == KD - 1))
                ins.then_inc(sem("v_mm"), 1)

        top[0] = base3
        w_lora = take(5 * W).rearrange("p (j c) -> p j c", j=5)
        lrow = take(4 * W).rearrange("p (j c) -> p j c", j=4)
        pre = take(4 * W).rearrange("p (j c) -> p j c", j=4)
        sg = take(6 * W).rearrange("p (d q c) -> p d q c", d=2, q=3)
        sq2 = take(W)
        bon = take(W)
        nrm = take(NT * NH)
        assert top[0] <= base3 + 2 * KD * 512 + NWIN * KD * P

        def sp_phase2(sp):
            sp.wait_ge(sem("lora_zero"), 1)
            for d in range(2):
                half = slice(d * 64, d * 64 + 64)
                sp.dma_start(w_lora[half, 2 * d, :], A["rwkv_w2"][0, d]).then_inc(sem("lora_in"), 16)
                sp.dma_start(w_lora[half, 2 * d + 1, :], A["rwkv_a2"][0, d]).then_inc(sem("lora_in"), 16)
                sp.dma_start(lrow[:, 2 * d, :], A["rwkv_w0"][0, d].partition_broadcast(P)).then_inc(sem("lora_in"), 16)
                sp.dma_start(lrow[:, 2 * d + 1, :], A["rwkv_a0"][0, d].partition_broadcast(P)).then_inc(sem("lora_in"), 16)
            sp.dma_start(w_lora[:, 4, :], A["rwkv_g2"][0]).then_inc(sem("lora_in"), 16)
            for t in range(NT):
                sp.wait_ge(sem("key_ready"), t + 1)
                sp.dma_start(dir_dram[:, :, t].rearrange("d q p c -> p (d q) c"), sg.rearrange("p d q c -> p (d q) c")).then_inc(sem("sig_out"), 16)
            sp.wait_ge(sem("sig_out"), 16 * NT)

        def pool_phase2(pool):
            nc.gpsimd.memset(w_lora[:, 0:4, :], 0.0).then_inc(sem("lora_zero"), 1)
            for t in range(NT):
                nc.gpsimd.tensor_tensor(kkn[:, t, :], rkv[:, 1, t, :], kk_row, ALU.mult).then_inc(sem("kk_raw"), 1)
                pool.wait_ge(sem("kk_raw"), t + 1)
                if t:
                    pool.wait_ge(sem("kk_sum"), t)
                nc.gpsimd.tensor_tensor(sq2, kkn[:, t, :], kkn[:, t, :], ALU.mult).then_inc(sem("kk_sq"), 1)

        def act_phase2(act):
            nc.scalar.activation(lz[:, 0, :], lz[:, 0, :], ACT.Tanh).then_inc(sem("lz_act"), 1)
            nc.scalar.activation(lz[:, 2, :], lz[:, 2, :], ACT.Sigmoid).then_inc(sem("lz_act"), 1)
            for t in range(NT):
                act.wait_ge(sem("pre_ready"), 4 * t + 4)
                if t:
                    act.wait_ge(sem("sig_out"), 16 * t)
                    act.wait_ge(sem("bonus_read"), t)
                nc.scalar.activation(sg[:, :, 0:2, :], pre.rearrange("p (d q) c -> p d q c", d=2), ACT.Sigmoid).then_inc(sem("sig_ready"), 1)
                act.wait_ge(sem("lora_mm"), 5 * t + 5)
                nc.scalar.copy(gate[:, t, :], bank[4]).then_inc(sem("gate_ready"), 1)
            act.wait_ge(sem("kk_sum"), NT)
            nc.scalar.activation(nrm, nrm, ACT.Sqrt).then_inc(sem("kk_root"), 1)

        def pe_phase2(pe):
            pe.wait_ge(sem("lora_in"), 16 * 9)
            pe.wait_ge(sem("lz_act"), 2)
            for t in range(NT):
                for j in range(5):
                    if t:
                        if j < 4:
                            pe.wait_ge(sem("pre_ready"), 4 * (t - 1) + j + 1)
                        else:
                            pe.wait_ge(sem("gate_ready"), t)
                    c = 2 if j == 4 else j % 2
                    nc.tensor.matmul(bank[j], lz[:, c, t * P:(t + 1) * P], w_lora[:, j, :], start=True, stop=True).then_inc(sem("lora_mm"), 1)

        def dve_phase2(dve):
            own = Own(dve, sem("dve_own2"))
            dve.wait_ge(sem("lora_in"), 16 * 9)

            def key_sum(t):
                dve.wait_ge(sem("kk_sq"), t + 1)
                nc.vector.reduce_sum(nrm[:, t * NH:(t + 1) * NH], sq2.rearrange("p (h c) -> p h c", h=NH), AX).then_inc(sem("kk_sum"), 1)

            for t in range(NT):
                if t:
                    dve.wait_ge(sem("sig_ready"), t)
                for j in range(4):
                    dve.wait_ge(sem("lora_mm"), 5 * t + j + 1)
                    nc.vector.tensor_tensor(pre[:, j, :], bank[j], lrow[:, j, :], ALU.add).then_inc(sem("pre_ready"), 1)
                key_sum(t)
                dve.wait_ge(sem("sig_ready"), t + 1)
                for d in range(2):
                    own.done(nc.vector.scalar_tensor_tensor(sg[:, d, 2, :], sg[:, d, 1, :], -1.0, ka_row, ALU.add, ALU.mult))
                own.wait(own.n - 1)
                own.done(nc.vector.scalar_tensor_tensor(sg[:, 0, 2, :], sg[:, 0, 2, :], 1.0, rkv[:, 1, t, :], ALU.add, ALU.mult))
                own.wait(own.n)
                nc.vector.scalar_tensor_tensor(sg[:, 1, 2, :], sg[:, 1, 2, :], 1.0, rkv[:, 1, t, :], ALU.add, ALU.mult).then_inc(sem("key_ready"), 1)
                dve.wait_ge(sem("key_ready"), t + 1)
                own.link(nc.vector.tensor_tensor(bon, sg[:, 0, 2, :], sg[:, 1, 2, :], ALU.add))
                own.link(nc.vector.tensor_tensor(bon, bon, rkv[:, 0, t, :], ALU.mult))
                own.link(nc.vector.tensor_tensor(bon, bon, rk_row, ALU.mult))
                nc.vector.reduce_sum(bonus[:, t, :], bon.rearrange("p (h c) -> p h c", h=NH), AX).then_inc(sem("bonus_read"), 1)
                dve.wait_ge(sem("bonus_read"), t + 1)
            dve.wait_ge(sem("kk_root"), 1)
            own.link(nc.vector.tensor_scalar(nrm, nrm, 1e-12, None, ALU.max))
            own.link(nc.vector.reciprocal(nrm, nrm))
            for t in range(NT):
                k3 = kkn[:, t, :].rearrange("p (h c) -> p h c", h=NH)
                s3 = nrm[:, t * NH:(t + 1) * NH].unsqueeze(2).to_broadcast([P, NH, HD])
                nc.vector.tensor_tensor(k3, k3, s3, ALU.mult)

        top[0] = base3
        bias = take(3 * NH * 8 * KB).rearrange("p (k h c) -> p k h c", k=3, h=NH)
        window = take(3 * KB).rearrange("p (k c) -> p k c", k=3)
        vband = take(NQB * 3 * W).rearrange("p (n s c) -> p n s c", n=NQB, s=3)
        sc = [take(8 * KB) for _ in range(3)]
        pT = [take(8 * KB) for _ in range(2)]
        items = [(g, n, h) for g in range(2) for n in range(NQB) for h in range(NH)]
        NI = len(items)
        nmax, psum_row, pinv = (take(NI) for _ in range(3))
        GR = [T_S // GW, T_P // GW]
        TOFF = [0, T_S]
        KIND = [0, 1, 1, 2]

        def grid(ap, g, col, cols):
            return ap[:, TOFF[g]:TOFF[g] + GR[g] * GW].rearrange("p (r c) -> p r c", c=GW)[:, :, col:col + cols]

        def sp_phase3(sp):
            sp.dma_start(window, A["c_window"]).then_inc(sem("bias_in"), 16)
            for k in range(3):
                sp.dma_start(bias[:, k], A["bias"][k]).then_inc(sem("bias_in"), 16)
            for g in range(2):
                for n in range(NQB):
                    for m in range(GR[g]):
                        r0 = TOFF[g] + m * GW + band(n)
                        s = m // 4 if g == 0 else 2
                        sp.dma_start(vband[32 * (m % 4):32 * (m % 4) + 32, n, s, :], v_dram[r0:r0 + KB, :]).then_inc(sem("band_in"), 16)

        def pool_phase3(pool):
            for i, (g, n, h) in enumerate(items):
                nq, nk = GR[g] * QB, GR[g] * KB
                pool.wait_ge(sem("p_inv"), i + 1)
                nc.gpsimd.tensor_scalar(sc[i % 3][0:nq, 0:nk], sc[i % 3][0:nq, 0:nk], pinv[0:nq, i:i + 1], None, ALU.mult).then_inc(sem("p_ready"), 1)

        def act_phase3(act):
            for i in range(NI + 3):
                if i < NI:
                    g, n, h = items[i]
                    nq, nk = GR[g] * QB, GR[g] * KB
                    act.wait_ge(sem("s_max"), i + 1)
                    nc.scalar.activation(sc[i % 3][0:nq, 0:nk], sc[i % 3][0:nq, 0:nk], ACT.Exp, bias=nmax[0:nq, i:i + 1],
                                         accum_out=psum_row[0:nq, i:i + 1]).then_inc(sem("p_exp"), 1)
                if 2 <= i < NI + 2:
                    j = i - 2
                    n_t = 256 if items[j][0] == 0 else 64
                    act.wait_ge(sem("pT_mm"), j + 1)
                    if j >= 2:
                        act.wait_ge(sem("o_mm"), j - 1)
                    nc.scalar.copy(pT[j % 2][:, 0:n_t], bank[3 + j % 2][:, 0:n_t]).then_inc(sem("pT_ready"), 1)
                if i >= 3 and i % 2 == 0:
                    j = i - 3
                    g, n, h = items[j]
                    act.wait_ge(sem("o_mm"), j + 1)
                    nc.scalar.copy(grid(catT[:, h // 2, :], g, n * QB, QB),
                                   bank[5 + (j // 2) % 2][:, 0:GR[g] * QB].rearrange("p (r c) -> p r c", c=QB)).then_inc(sem("o_ready"), 1)

        def dve_phase3(dve):
            own = Own(dve, sem("dve_own3"))
            dve.wait_ge(sem("bias_in"), 16 * 4)
            for k in range(3):
                b3 = bias[:, k].rearrange("p h (m c) -> p (h m) c", c=KB)
                last = own.done(nc.vector.tensor_tensor(b3, b3, window[:, k, :].unsqueeze(1).to_broadcast([P, NH * 8, KB]), ALU.add))
            own.wait(last)

            def inverse(i):
                nq = GR[items[i][0]] * QB
                dve.wait_ge(sem("p_exp"), i + 1)
                nc.vector.reciprocal(pinv[0:nq, i:i + 1], psum_row[0:nq, i:i + 1]).then_inc(sem("p_inv"), 1)

            for i, (g, n, h) in enumerate(items):
                nq, nk = GR[g] * QB, GR[g] * KB
                dve.wait_ge(sem("s_mm"), i + 1)
                if i >= 3:
                    dve.wait_ge(sem("pT_mm"), i - 2)
                own.link(nc.vector.tensor_tensor(sc[i % 3][0:nq, 0:nk], bank[i % 3][0:nq, 0:nk], bias[0:nq, KIND[n], h, 0:nk], ALU.add))
                nc.vector.tensor_reduce(nmax[0:nq, i:i + 1], sc[i % 3][0:nq, 0:nk], AX, ALU.max, negate=True).then_inc(sem("s_max"), 1)
                if i:
                    inverse(i - 1)
            inverse(NI - 1)

        def pe_phase3(pe):
            pe.wait_ge(sem("band_in"), 16 * NQB * sum(GR))
            for i in range(NI + 3):
                if i < NI:
                    g, n, h = items[i]
                    nq, nk = GR[g] * QB, GR[g] * KB
                    hp = slice(64 * (h % 2), 64 * (h % 2) + 64)
                    if i >= 3:
                        pe.wait_ge(sem("s_max"), i - 2)
                    nc.tensor.matmul(bank[i % 3][0:nq, 0:nk], qT[hp, h // 2, TOFF[g] + n * nq:TOFF[g] + (n + 1) * nq], grid(kT[hp, h // 2, :], g, band(n), KB),
                                     start=True, stop=True).then_inc(sem("s_mm"), 1)
                if 2 <= i < NI + 2:
                    j = i - 2
                    g = items[j][0]
                    nq = GR[g] * QB
                    pe.wait_ge(sem("p_ready"), j + 1)
                    if j >= 2:
                        pe.wait_ge(sem("pT_ready"), j - 1)
                    for s in range(2 - g):
                        ins = nc.tensor.transpose(bank[3 + j % 2][:, s * P:s * P + nq], sc[j % 3][0:nq, s * P:(s + 1) * P], ident[0:nq, 0:nq])
                    ins.then_inc(sem("pT_mm"), 1)
                if i >= 3:
                    j = i - 3
                    g, n, h = items[j]
                    nq = GR[g] * QB
                    hp = slice(64 * (h % 2), 64 * (h % 2) + 64)
                    pe.wait_ge(sem("pT_ready"), j + 1)
                    if j >= 4 and h % 2 == 0:
                        pe.wait_ge(sem("o_ready"), j // 2 - 1)
                    for s in range(2 - g):
                        ins = nc.tensor.matmul(bank[5 + (j // 2) % 2][hp, 0:nq], vband[:, n, 2 if g else s, h * HD:(h + 1) * HD],
                                               pT[j % 2][:, s * P:s * P + nq], start=(s == 0), stop=(s == 1 - g))
                    ins.then_inc(sem("o_mm"), 1)

        top[0] = base4
        tri = take(2 * P).rearrange("p (d c) -> p d c", d=2)
        midc = take(4).rearrange("p (d c) -> p d c", d=2)
        seen = take(2 * 512).rearrange("p (d c) -> p d c", d=2)
        pairm = take(P)
        sgw = [take(3 * W).rearrange("p (q c) -> p q c", q=3) for _ in range(2)]
        cin, cinv = take(W), take(W)
        tok_ar = take(2 * W).rearrange("p (q c) -> p q c", q=2)
        tok_bk = [take(2 * W).rearrange("p (q c) -> p q c", q=2) for _ in range(2)]
        bkT = take(2 * W).rearrange("p (q j c) -> p q j c", q=2, j=NPAIR)
        ar4 = take(NPAIR * 512).rearrange("p (j c) -> p j c", j=NPAIR)
        Lb = take(NH * 3 * P).rearrange("p (h r c) -> p h r c", h=NH, r=3)
        Lk = take(NPAIR * 512).rearrange("p (j c) -> p j c", j=NPAIR)
        inv = take(NH * 192).bitcast(f16).rearrange("p (h c) -> p h c", h=NH)
        cme = take(8).rearrange("p (j m) -> p j m", m=2)
        cend = take(W).rearrange("p (j c) -> p j c", j=NPAIR)
        state = [take(W) for _ in range(2)]
        stp = [take(W).rearrange("p (j c) -> p j c", j=NPAIR) for _ in range(2)]
        rhs, u0, res = kk_row, ka_row, rk_row
        u1 = res
        rhs16, res16 = take(W // 2).bitcast(f16), take(W // 2).bitcast(f16)
        yacc = catT[:, 4:8, :].rearrange("p c t -> p (c t)").rearrange("p (t c) -> p t c", t=NT)
        IA, IR, IB, IK = range(4)
        steps = [(d, t) for i in range(NT_S) for d, t in ((0, i), (1, NT_S - 1 - i))] + \
                [(d, t) for i in range(NT_P) for d, t in ((0, NT_S + i), (1, NT - 1 - i))]
        fresh = (0, 1, 2 * NT_S, 2 * NT_S + 1)

        def tok(n, q):
            return tok_ar[:, q, :] if q in (IA, IR) else tok_bk[n % 2][:, q - IB, :]

        def hcol(h):
            return slice(h * HD, (h + 1) * HD)

        def lcol(h, r, d):
            at = (h % 2) * 256 + (r ^ d) * P
            return slice(at, at + P)

        ACT_HEADS, DVE_HEADS = (0, 2, 3, 5, 7), (1, 4, 6)

        def wait_level(eng, n, l, h):
            name, heads = ("inv_act", ACT_HEADS) if h in ACT_HEADS else ("inv_dve", DVE_HEADS)
            eng.wait_ge(sem(name), (LEVELS * n + l) * len(heads) + heads.index(h) + 1)

        def levels_out(eng, n):
            wait_level(eng, n, LEVELS - 1, ACT_HEADS[-1])
            wait_level(eng, n, LEVELS - 1, DVE_HEADS[-1])

        STEPS = len(steps)

        def sp_phase4(sp):
            for dst, src in ((tri, A["c_tri"]), (midc, A["c_mid"]), (seen, A["c_seen"]), (pairm, A["c_pair"])):
                sp.dma_start(dst, src).then_inc(sem("consts4_in"), 16)
            for n, (d, t) in enumerate(steps):
                if n >= 2:
                    sp.wait_ge(sem("mid_mm"), n - 1)
                    sp.wait_ge(sem("atok_ready"), n - 1)
                    sp.wait_ge(sem("ktok_ready"), n - 1)
                sp.dma_start(sgw[n % 2], dir_dram[d, :, t].rearrange("q p c -> p q c")).then_inc(sem(f"sig_in{n % 2}"), 16)

        def pool_phase4(pool):
            own = Own(pool, sem("pool_own4"))
            nc.gpsimd.memset(ar4, 0.0).then_inc(sem("zero4"), 1)
            nc.gpsimd.memset(yacc, 0.0).then_inc(sem("zero4"), 1)
            pool.wait_ge(sem("consts4_in"), 64)

            def rows(n):
                t = steps[n][1]
                pool.wait_ge(sem(f"sig_in{n % 2}"), 16 * (n // 2 + 1))
                if n >= 2:
                    pool.wait_ge(sem("st_mm"), n - 1)
                last = own.done(nc.gpsimd.tensor_tensor(tok(n, IB), kkn[:, t, :], sgw[n % 2][:, 1, :], ALU.mult))
                if n:
                    pool.wait_ge(sem("tr_mm"), 4 * n)
                pool.wait_ge(sem("exps"), 3 * n + 2)
                own.wait(last)
                nc.gpsimd.tensor_tensor(tok(n, IB), tok(n, IB), cinv, ALU.mult).then_inc(sem("btok_ready"), 1)
                nc.gpsimd.tensor_tensor(tok(n, IR), rkv[:, 0, t, :], cin, ALU.mult).then_inc(sem("rtok_ready"), 1)
                nc.gpsimd.tensor_tensor(tok(n, IK), sgw[n % 2][:, 2, :], cinv, ALU.mult).then_inc(sem("ktok_ready"), 1)

            rows(0)
            for n in range(STEPS):
                pool.wait_ge(sem("cme_ready"), n + 1)
                if n:
                    pool.wait_ge(sem("st_ready"), n)
                nc.gpsimd.tensor_tensor(cend, pairm.unsqueeze(1).to_broadcast([P, NPAIR, P]),
                                        cme[:, :, 1:2].to_broadcast([P, NPAIR, P]), ALU.mult).then_inc(sem("cend_ready"), 1)
                if n + 1 < STEPS:
                    rows(n + 1)

        def act_phase4(act):
            def u0_out(n):
                act.wait_ge(sem("u0_mm"), n + 1)
                nc.scalar.copy(u0, bank[1]).then_inc(sem("u0_ready"), 1)

            def decays(n, part):
                if part == 0:
                    act.wait_ge(sem("cum_mm"), n + 1)
                    if n:
                        for name in ("rtok_ready", "btok_ready", "ktok_ready", "cend_ready", "stp_ready"):
                            act.wait_ge(sem(name), n)
                    nc.scalar.activation(cinv, bank[1], ACT.Exp, scale=DECAY).then_inc(sem("exps"), 1)
                elif part == 1:
                    nc.scalar.activation(cin, bank[1], ACT.Exp, scale=-DECAY).then_inc(sem("exps"), 1)
                elif part == 2:
                    act.wait_ge(sem("cex_ready"), n + 1)
                    nc.scalar.activation(sgw[n % 2][:, 0, :], sgw[n % 2][:, 0, :], ACT.Exp, scale=-DECAY).then_inc(sem("exps"), 1)
                elif part == 3:
                    act.wait_ge(sem("mid_mm"), n + 1)
                    nc.scalar.activation(cme, bank[3][:, 0:8].rearrange("p (j m) -> p j m", m=2), ACT.Exp, scale=-DECAY).then_inc(sem("cme_ready"), 1)

            for part in range(4):
                decays(0, part)
            for n, (d, t) in enumerate(steps):
                act.wait_ge(sem("tr_mm"), 4 * n + 1)
                nc.scalar.copy(bkT[:, 0], bank[4 + IB].rearrange("p (j c) -> p j c", j=NPAIR)).then_inc(sem("chT_act"), 1)
                if n:
                    u0_out(n - 1)
                else:
                    act.wait_ge(sem("zero4"), 1)
                for q, j in ((IR, 2), (IA, 4)):
                    act.wait_ge(sem("tr_mm"), 4 * n + j)
                    nc.scalar.copy(ar4[0:64, :, lcol(0, int(q == IR), d)],
                                   bank[4 + q][0:64, :].rearrange("p (j c) -> p j c", j=NPAIR)).then_inc(sem("chT_act"), 1)
                for j in range(NPAIR):
                    act.wait_ge(sem("L_ready"), 8 * n + 2 * j + 1)
                    nc.scalar.copy(inv[:, 2 * j:2 * j + 2, 0:P], Lb[:, 2 * j:2 * j + 2, 1, :]).then_inc(sem("Nt_ready"), 1)
                act.wait_ge(sem("rhs_mm"), n + 1)
                nc.scalar.copy(rhs, bank[0]).then_inc(sem("rhs_ready"), 1)
                for l in range(LEVELS):
                    if n + 1 < STEPS and l < 4:
                        decays(n + 1, l)
                    for h in ACT_HEADS:
                        act.wait_ge(sem("inv_mm"), NH * (LEVELS * n + l) + h + 1)
                        if l < LEVELS - 1:
                            ins = nc.scalar.copy(inv[:, h, :], bank[4 + h % 4][:, 0:3 * P])
                        else:
                            ins = nc.scalar.copy(inv[:, h, P:2 * P], bank[4 + h % 4][:, P:2 * P])
                        ins.then_inc(sem("inv_act"), 1)
            u0_out(STEPS - 1)
            act.wait_ge(sem("y_centred"), 1)
            nc.scalar.activation(rkv[:, 0], yacc, ACT.Square).then_inc(sem("y_squared"), 1)
            act.wait_ge(sem("y_var"), 1)
            nc.scalar.activation(nrm4, nrm4, ACT.Sqrt, scale=1.0 / HD, bias=eps[:, 1:2]).then_inc(sem("y_root"), 1)
            for t in range(NT):
                act.wait_ge(sem("rec_tr"), t + 1)
                nc.scalar.copy(catT[:, 4:8, t * P:(t + 1) * P], bank[t % 2].rearrange("p (j c) -> p j c", j=NPAIR)).then_inc(sem("rec_ready"), 1)

        def dve_phase4(dve):
            own = Own(dve, sem("dve_own4"))
            dve.wait_ge(sem("zero4"), 2)
            dve.wait_ge(sem("consts4_in"), 64)

            def residual(n):
                dve.wait_ge(sem("u0_ready"), n + 1)
                own.link(nc.vector.tensor_tensor(res, rhs, u0, ALU.subtract))
                own.done(nc.vector.tensor_scalar(res, res, U_SCALE, None, ALU.mult))

            def residual16(n):
                own.wait(own.n)
                dve.wait_ge(sem("nu_mm"), n + 1)
                nc.vector.scalar_tensor_tensor(res16, bank[0], U_SCALE, res, ALU.mult, ALU.add).then_inc(sem("res16_ready"), 1)

            def solution(n):
                dve.wait_ge(sem("du_mm"), n + 1)
                nc.vector.scalar_tensor_tensor(u1, bank[1], 1.0 / U_SCALE, u0, ALU.mult, ALU.add).then_inc(sem("u1_ready"), 1)

            def advance(n):
                d, t = steps[n]
                dve.wait_ge(sem("st_mm"), n + 1)
                own.link(nc.vector.tensor_tensor(state[d], bank[3], stp[n % 2].rearrange("p j c -> p (j c)"), ALU.add))
                dve.wait_ge(sem("cend_ready"), n + 1)
                s3 = state[d].rearrange("p (j c) -> p j c", j=NPAIR)
                nc.vector.tensor_tensor(s3, s3, cend, ALU.mult).then_inc(sem("st_ready"), 1)
                dve.wait_ge(sem("y_mm"), n + 1)
                nc.vector.tensor_tensor(yacc[:, t, :], bank[2], yacc[:, t, :], ALU.add).then_inc(sem("y_ready"), 1)

            def without(n):
                dve.wait_ge(sem(f"sig_in{n % 2}"), 16 * (n // 2 + 1))
                dve.wait_ge(sem("mid_mm"), n + 1)
                dve.wait_ge(sem("exps"), 3 * n + 2)
                nc.vector.tensor_tensor(sgw[n % 2][:, 0, :], bank[1], sgw[n % 2][:, 0, :], ALU.subtract).then_inc(sem("cex_ready"), 1)

            def a_row(n):
                dve.wait_ge(sem("exps"), 3 * n + 3)
                if n:
                    dve.wait_ge(sem("tr_mm"), 4 * n)
                nc.vector.scalar_tensor_tensor(tok(n, IA), kkn[:, steps[n][1], :], -1.0, sgw[n % 2][:, 0, :], ALU.mult, ALU.mult).then_inc(sem("atok_ready"), 1)

            without(0)
            a_row(0)
            for n, (d, t) in enumerate(steps):
                if n in fresh:
                    own.wait(own.done(nc.vector.memset(state[d], 0.0)))
                dve.wait_ge(sem("cme_ready"), n + 1)
                s3 = state[d].rearrange("p (j c) -> p j c", j=NPAIR)
                nc.vector.tensor_tensor(stp[n % 2], s3, cme[:, :, 0:1].to_broadcast([P, NPAIR, P]), ALU.mult).then_inc(sem("stp_ready"), 1)
                for q, j in ((IR, 2), (IK, 3), (IA, 4)):
                    dve.wait_ge(sem("tr_mm"), 4 * n + j)
                    src = bank[4 + q].rearrange("p (j c) -> p j c", j=NPAIR)
                    if q == IK:
                        ins = nc.vector.tensor_copy(bkT[:, 1], src)
                    else:
                        ins = nc.vector.tensor_copy(ar4[64:128, :, lcol(1, int(q == IR), d)], src[64:128])
                    ins.then_inc(sem("chT_dve"), 1)
                    if n and q == IK:
                        residual(n - 1)
                if n:
                    residual16(n - 1)
                for j in range(NPAIR):
                    for k, L in ((0, Lb[:, 2 * j:2 * j + 2, 1 - d:3 - d, :].rearrange("p h r c -> p h (r c)")),
                                 (1, Lk[:, j, :].rearrange("p (h c) -> p h c", h=2))):
                        dve.wait_ge(sem("L_mm"), 8 * n + 2 * j + k + 1)
                        nc.vector.scalar_tensor_tensor(L, bank[4 + 2 * (j % 2) + k].rearrange("p (h c) -> p h c", h=2), BIG,
                                                       seen[:, d, :].rearrange("p (h c) -> p h c", h=2), ALU.min, ALU.mult).then_inc(sem("L_ready"), 1)
                    if n and j == 0:
                        solution(n - 1)
                    if n and j == 2:
                        advance(n - 1)
                dve.wait_ge(sem("N_mm"), n + 1)
                nc.vector.tensor_copy(inv[:, :, 2 * P:3 * P], bank[4].bitcast(f16).rearrange("p (h c) -> p h c", h=NH)).then_inc(sem("N_ready"), 1)
                for l in range(LEVELS):
                    if n + 1 < STEPS and l == 2:
                        without(n + 1)
                    if n + 1 < STEPS and l == 4:
                        a_row(n + 1)
                    if l == 6:
                        dve.wait_ge(sem("rhs_ready"), n + 1)
                        nc.vector.tensor_copy(rhs16, rhs).then_inc(sem("rhs16_ready"), 1)
                    for h in DVE_HEADS:
                        dve.wait_ge(sem("inv_mm"), NH * (LEVELS * n + l) + h + 1)
                        if l < LEVELS - 1:
                            ins = nc.vector.tensor_copy(inv[:, h, :], bank[4 + h % 4][:, 0:3 * P])
                        else:
                            ins = nc.vector.tensor_copy(inv[:, h, P:2 * P], bank[4 + h % 4][:, P:2 * P])
                        ins.then_inc(sem("inv_dve"), 1)
            n = len(steps) - 1
            residual(n)
            residual16(n)
            solution(n)
            advance(n)
            dve.wait_ge(sem("y_ready"), len(steps))
            y4 = yacc.rearrange("p t (h c) -> p (t h) c", c=HD)
            own.link(nc.vector.reduce_sum(nrm4, y4, AX))
            own.link(nc.vector.tensor_scalar(nrm4, nrm4, 1.0 / HD, None, ALU.mult))
            nc.vector.tensor_tensor(y4, y4, nrm4.unsqueeze(2).to_broadcast([P, NT * NH, HD]), ALU.subtract).then_inc(sem("y_centred"), 1)
            dve.wait_ge(sem("y_squared"), 1)
            nc.vector.reduce_sum(nrm4, rkv[:, 0].rearrange("p t (h c) -> p (t h) c", c=HD), AX).then_inc(sem("y_var"), 1)
            dve.wait_ge(sem("y_root"), 1)
            own.link(nc.vector.reciprocal(nrm4, nrm4))
            own.link(nc.vector.tensor_tensor(y4, y4, nrm4.unsqueeze(2).to_broadcast([P, NT * NH, HD]), ALU.mult))
            own.link(nc.vector.tensor_tensor(yacc, yacc, lg_row.unsqueeze(1).to_broadcast([P, NT, W]), ALU.mult))
            own.link(nc.vector.tensor_tensor(yacc, yacc, lb_row.unsqueeze(1).to_broadcast([P, NT, W]), ALU.add))
            v4 = rkv[:, 2].rearrange("p t (h c) -> p (t h) c", c=HD)
            own.link(nc.vector.tensor_tensor(v4, v4, bonus.rearrange("p t h -> p (t h)").unsqueeze(2).to_broadcast([P, NT * NH, HD]), ALU.mult))
            own.link(nc.vector.tensor_tensor(yacc, yacc, rkv[:, 2], ALU.add))
            nc.vector.tensor_tensor(gate, gate, yacc, ALU.mult).then_inc(sem("rec_tok"), 1)

        nrm4 = take(NT * NH)

        def pe_phase4(pe):
            pe.wait_ge(sem("consts4_in"), 64)

            def mm(out, lhsT, r, start=False):
                return nc.tensor.matmul(out, lhsT, r, start=start, stop=True, skip_group_check=True)

            def first_solution(n):
                pe.wait_ge(sem("rhs16_ready"), n + 1)
                levels_out(pe, n)
                if n + 1 < STEPS:
                    pe.wait_ge(sem("cex_ready"), n + 2)
                    pe.wait_ge(sem("exps"), 3 * n + 5)
                for h in range(NH):
                    ins = mm(bank[1][:, hcol(h)], inv[:, h, P:2 * P], rhs16[:, hcol(h)], h == 0)
                ins.then_inc(sem("u0_mm"), 1)

            def times_n(n):
                pe.wait_ge(sem("u0_ready"), n + 1)
                for h in range(NH):
                    ins = mm(bank[0][:, hcol(h)], Lb[:, h, 1, :], u0[:, hcol(h)], h == 0)
                ins.then_inc(sem("nu_mm"), 1)

            def correction(n):
                pe.wait_ge(sem("res16_ready"), n + 1)
                for h in range(NH):
                    ins = mm(bank[1][:, hcol(h)], inv[:, h, P:2 * P], res16[:, hcol(h)], h == 0)
                ins.then_inc(sem("du_mm"), 1)

            def advance(n):
                v = rkv[:, 2, steps[n][1], :]
                pe.wait_ge(sem("u1_ready"), n + 1)
                if n + 1 < STEPS:
                    pe.wait_ge(sem("cme_ready"), n + 2)
                if n:
                    pe.wait_ge(sem("st_ready"), n)
                for j in range(NPAIR):
                    mm(bank[3][:, j * P:(j + 1) * P], tok(n, IB)[:, j * P:(j + 1) * P], u1[:, j * P:(j + 1) * P], j == 0)
                    ins = mm(bank[3][:, j * P:(j + 1) * P], tok(n, IK)[:, j * P:(j + 1) * P], v[:, j * P:(j + 1) * P])
                ins.then_inc(sem("st_mm"), 1)
                for h in range(NH):
                    ins = mm(bank[2][:, hcol(h)], Lb[:, h, 2 - 2 * steps[n][0], :], u1[:, hcol(h)])
                ins.then_inc(sem("y_mm"), 1)

            def decay_sums(n):
                d = steps[n][0]
                pe.wait_ge(sem(f"sig_in{n % 2}"), 16 * (n // 2 + 1))
                if n >= 2:
                    pe.wait_ge(sem("u1_ready"), n - 1)
                    pe.wait_ge(sem("st_ready"), n - 1)
                mm(bank[1], tri[:, d, :], sgw[n % 2][:, 0, :], True).then_inc(sem("cum_mm"), 1)
                for j in range(NPAIR):
                    ins = mm(bank[3][:, 2 * j:2 * j + 2], sgw[n % 2][:, 0, j * P:(j + 1) * P], midc[:, d, :], True)
                ins.then_inc(sem("mid_mm"), 1)

            def head_of(q, h):
                return ar4[:, h // 2, lcol(h, int(q == IR), d)]

            decay_sums(0)
            for n, (d, t) in enumerate(steps):
                v = rkv[:, 2, t, :]
                if n:
                    levels_out(pe, n - 1)
                for q, s in ((IB, "btok_ready"), (IR, "rtok_ready"), (IK, "ktok_ready"), (IA, "atok_ready")):
                    pe.wait_ge(sem(s), n + 1)
                    for j in range(NPAIR):
                        ins = nc.tensor.transpose(bank[4 + q][:, j * P:(j + 1) * P], tok(n, q)[:, j * P:(j + 1) * P], ident)
                    ins.then_inc(sem("tr_mm"), 1)
                    if n and q == IB:
                        first_solution(n - 1)
                if n:
                    times_n(n - 1)
                pe.wait_ge(sem("chT_act"), 3 * n + 3)
                pe.wait_ge(sem("chT_dve"), 3 * n + 3)
                for j in range(NPAIR):
                    for k in range(2):
                        if j >= 2:
                            pe.wait_ge(sem("L_ready"), 8 * n + 2 * (j - 2) + k + 1)
                        mm(bank[4 + 2 * (j % 2) + k], bkT[:, k, j, :], ar4[:, j, :], True).then_inc(sem("L_mm"), 1)
                    if n and j == 0:
                        correction(n - 1)
                    if n and j == 1:
                        advance(n - 1)
                pe.wait_ge(sem("stp_ready"), n + 1)
                for h in range(NH):
                    mm(bank[0][:, hcol(h)], head_of(IA, h), stp[n % 2][:, h // 2, (h % 2) * HD:(h % 2 + 1) * HD], h == 0)
                for h in range(NH):
                    pe.wait_ge(sem("L_ready"), 8 * n + 2 * (h // 2) + 2)
                    ins = mm(bank[0][:, hcol(h)], Lk[:, h // 2, lcol(h, 0, d)], v[:, hcol(h)])
                ins.then_inc(sem("rhs_mm"), 1)
                pe.wait_ge(sem("Nt_ready"), 4 * n + 4)
                b16 = bank[4].bitcast(f16)
                for h in range(NH):
                    ins = nc.tensor.transpose(b16[:, h * P:(h + 1) * P], inv[:, h, 0:P], ident16)
                ins.then_inc(sem("N_mm"), 1)
                if n + 1 < STEPS:
                    decay_sums(n + 1)
                pe.wait_ge(sem("N_ready"), n + 1)
                for l in range(LEVELS):
                    for h in range(NH):
                        if h >= 4:
                            wait_level(pe, n, l, h - 4)
                        if l:
                            wait_level(pe, n, l - 1, h)
                            if h < 4:
                                wait_level(pe, n, l - 1, h + 4)
                        b = bank[4 + h % 4]
                        nt, x, m = inv[:, h, 0:P], inv[:, h, P:2 * P], inv[:, h, 2 * P:3 * P]
                        if l == 0:
                            mm(b[:, 0:P], m, nt, True)
                            mm(b[:, P:2 * P], m, ident16)
                            mm(b[:, P:2 * P], ident16, ident16)
                            ins = mm(b[:, 2 * P:3 * P], nt, m)
                        elif l < LEVELS - 1:
                            mm(b[:, 0:2 * P], m, inv[:, h, 0:2 * P], True)
                            mm(b[:, P:2 * P], ident16, x)
                            ins = mm(b[:, 2 * P:3 * P], nt, m)
                        else:
                            mm(b[:, P:2 * P], m, x, True)
                            ins = mm(b[:, P:2 * P], ident16, x)
                        ins.then_inc(sem("inv_mm"), 1)
                    if l == 0 and n:
                        pe.wait_ge(sem("y_ready"), n)
                    for h in (range(4 * l, 4 * l + 4) if l < 2 else ()):
                        mm(bank[2][:, hcol(h)], head_of(IR, h), stp[n % 2][:, h // 2, (h % 2) * HD:(h % 2 + 1) * HD], h == 0)
                    for h in (range(2 * l - 4, 2 * l - 2) if 2 <= l < 6 else ()):
                        mm(bank[2][:, hcol(h)], Lk[:, h // 2, lcol(h, 1, d)], v[:, hcol(h)])
            n = len(steps) - 1
            first_solution(n)
            times_n(n)
            correction(n)
            advance(n)
            pe.wait_ge(sem("rec_tok"), 1)
            for t in range(NT):
                if t >= 2:
                    pe.wait_ge(sem("rec_ready"), t - 1)
                for j in range(NPAIR):
                    ins = nc.tensor.transpose(bank[t % 2][:, j * P:(j + 1) * P], gate[:, t, j * P:(j + 1) * P], ident)
                ins.then_inc(sem("rec_tr"), 1)

        top[0] = base5
        x2 = take(NT * D).rearrange("p (t d) -> p t d", t=NT)
        g2_row = take(2 * D).rearrange("p (g d) -> p g d", g=2)
        wts = take(NT * 2).rearrange("p (t k) -> p t k", k=2)
        pos_i = take(NT * 2).bitcast(i32).rearrange("p (t k) -> p t k", k=2)
        base6 = top[0]
        NSLOT = 3
        WEXP = 2 * KD * HID + KH * D
        w1_s, w3_s, w2_s = [], [], []
        for at in (ARENA - WEXP, ARENA - 2 * WEXP, P + 2):
            top[0] = at
            w2_s.append(take(KH * D).rearrange("p (k n) -> p k n", k=KH))
            w1_s.append(take(KD * HID).rearrange("p (k n) -> p k n", k=KD))
            w3_s.append(take(KD * HID).rearrange("p (k n) -> p k n", k=KD))
        assert top[0] == base5
        w1_v = A["exp_w1"][0].rearrange("e (k p) n -> e p k n", p=P)
        w3_v = A["exp_w3"][0].rearrange("e (k p) n -> e p k n", p=P)
        w2_v = A["exp_w2"][0].rearrange("e (k p) n -> e p k n", p=P)

        def one(ap, e):
            return ap[bass.ds(e, 1)].rearrange("o p k n -> p (o k) n")

        top[0] = ARENA - 2 * WEXP + KH * D
        wout = take(KD * D).rearrange("p (k n) -> p k n", k=KD)
        assert top[0] <= ARENA - WEXP
        h2T = [take(D).rearrange("p (k c) -> p k c", k=KD) for _ in range(2)]
        sq5 = take(D)
        zero = take(512)
        before, ones = take(P), take(P)
        assert top[0] <= ARENA - WEXP + KH * D
        top[0] = base6
        g1_row = take(2 * D).rearrange("p (g d) -> p g d", g=2)
        ss_row = take(4 * D).rearrange("p (g m d) -> p g m d", g=2, m=2)
        n2_row = take(D)
        h2 = [take(D) for _ in range(2)]
        sel5 = take(3 * P).rearrange("p (g c) -> p g c", g=3)
        rw = take(KD * 36).rearrange("p (k e) -> p k e", k=KD)
        rb = take(36)
        stat5 = take(NT * 4).rearrange("p (t m) -> p t m", t=NT)
        logit = take(NT * 36).rearrange("p (t e) -> p t e", t=NT)
        expert_row, first_row, fall_row, place = take(NE), take(NE), take(8), take(1)
        token_i = take(NT).bitcast(i32)
        gm, gsum, m1, m2, pk = (take(NT) for _ in range(5))
        og, tg = (take(NT * NG).rearrange("p (t g) -> p t g", g=NG) for _ in range(2))
        s8, t8, o1, o2 = (take(NT * 8).rearrange("p (t e) -> p t e", e=8) for _ in range(4))
        e1, e2, both, slot_f, lsel = (take(NT * NE).rearrange("p (t e) -> p t e", e=NE) for _ in range(5))
        tilebase = take((NT + 1) * NE).rearrange("p (t e) -> p t e", e=NE)
        over, incl, incl2, o32, excl = (take(NE) for _ in range(5))
        lst = take(2)
        lst_i = take(2).bitcast(i32)
        assert top[0] <= ARENA - 2 * WEXP + KH * D, top[0]

        def sp_phase5(sp):
            sp.wait_ge(sem("zero5"), 1)
            sp.dma_start(slot_dram.rearrange("(p n) o -> p (n o)", p=P), zero.bitcast(i32)[:, 0:NBLK * BLK // P]).then_inc(sem("slots_zero"), 16)
            unused = y_dram[NE * BLK:, :].rearrange("(p s) (j n) -> p (s j) n", p=P, n=512)
            sp.dma_start(unused, zero.unsqueeze(1).to_broadcast([P, MAX_OVER * BLK // P * 2, 512])).then_inc(sem("unused_zero"), 16)
            for dst, src in ((sel5, A["c_sel"]), (n2_row, A["norm2_g"][0].partition_broadcast(P)), (before, A["c_before"]),
                             (ones, A["c_ones"]), (rw, A["router_w"]), (rb, A["router_b"].partition_broadcast(P)),
                             (expert_row, A["c_expert"]), (first_row, A["c_first"]), (fall_row, A["c_fall8"]),
                             (place, A["c_place"]), (token_i, A["c_token"])):
                sp.dma_start(dst, src).then_inc(sem("consts5_in"), 16)
            sp.dma_start(wout, A["w_out"][0].rearrange("(k p) n -> p k n", p=P)).then_inc(sem("wout_in"), 16)
            for t in range(NT):
                sp.dma_start(x2[:, t, :], x_tile[t]).then_inc(sem("x5_in"), 16)
            for slot, view in ((w1_s, w1_v), (w3_s, w3_v)):
                sp.dma_start(slot[0], view[0]).then_inc(sem("weights_in"), 16)
            for t in range(NT):
                sp.wait_ge(sem("h2_ready"), t + 1)
                sp.dma_start(h2_dram[t * P:(t + 1) * P, :], h2[t % 2]).then_inc(sem(f"h2_out{t % 2}"), 16)
            sp.wait_ge(sem("o5_mm"), 2 * NT)
            sp.wait_ge(sem("row5_mm"), 16)
            for k in (1, 2):
                for slot, view in ((w1_s, w1_v), (w3_s, w3_v)):
                    sp.dma_start(slot[k], view[k]).then_inc(sem("weights_in"), 16)
            sp.dma_start(w2_s[2], w2_v[2]).then_inc(sem("weights_in"), 16)
            sp.wait_ge(sem("list_ready"), 1)
            sp.dma_start(over_dram, lst_i[0:MAX_OVER, :]).then_inc(sem("list_out"), 16)
            sp.wait_ge(sem("weights_in"), 16 * 7)
            sp.wait_ge(sem("list_out"), 16)
            sp.wait_ge(sem("unused_zero"), 16)
            sp.wait_ge(sem("h2_out0"), 48)
            sp.wait_ge(sem("h2_out1"), 48)

        def pool_phase5(pool):
            nc.gpsimd.memset(zero, 0.0).then_inc(sem("zero5"), 1)
            pool.wait_ge(sem("slots_zero"), 16)
            pool.wait_ge(sem("consts5_in"), 16 * 11)
            pool.wait_ge(sem("pos_ready"), 1)
            for t in range(NT):
                for k in range(2):
                    nc.gpsimd.indirect_dma_start(slot_dram, bass.IndirectOffsetOnAxis(ap=pos_i.bitcast(u32)[:, t, k:k + 1], axis=0),
                                                 token_i[:, t:t + 1], None).then_inc(sem("slot_out"), 16)
            pool.wait_ge(sem("slot_out"), 16 * 2 * NT)

        def act_phase5(act):
            own = Own(act, sem("act_own5"))
            for t in range(NT):
                act.wait_ge(sem("x2_ready"), t + 1)
                if t:
                    own.wait(own.n)
                own.link(nc.scalar.activation(sq5, x2[:, t, :], ACT.Square, scale=1.0 / 32.0, accum_out=stat5[:, t, 0:1]))
                own.done(nc.scalar.activation(stat5[:, t, 1:2], stat5[:, t, 0:1], ACT.Sqrt, bias=eps[:, 0:1]))
                if t:
                    h2T_evac(act, t - 1)
            h2T_evac(act, NT - 1)
            act.wait_ge(sem("g_centred"), 1)
            nc.scalar.activation(tg, tg, ACT.Exp).then_inc(sem("g_exp"), 1)
            act.wait_ge(sem("m_diff"), 1)
            nc.scalar.activation(m2, m2, ACT.Exp).then_inc(sem("m_exp"), 1)

        def h2T_evac(act, t):
            for hf in range(2):
                act.wait_ge(sem("h2T_mm"), 2 * t + hf + 1)
                if t >= 2:
                    act.wait_ge(sem("router_mm"), t - 1)
                nc.scalar.copy(h2T[t % 2][:, 4 * hf:4 * hf + 4, :], bank[6 + hf].rearrange("p (k c) -> p k c", k=4)).then_inc(sem("h2T_ready"), 1)

        MODS = [(2, g1_row, None), (3, ss_row, 0), (4, ss_row, 1), (5, g2_row, None)]

        def dve_phase5(dve):
            own = Own(dve, sem("dve_own5"))
            dve.wait_ge(sem("consts5_in"), 16 * 11)
            n = 0
            for m, to, which in MODS:
                for g in range(2):
                    for hf in range(2):
                        dve.wait_ge(sem("row5_mm"), n + 1)
                        cols = slice(hf * 512, hf * 512 + 512)
                        dst = to[:, g, cols] if which is None else to[:, g, which, cols]
                        if which == 1:
                            ins = nc.vector.scalar_tensor_tensor(dst, bank[n % 2], 1.0, n2_row[:, cols], ALU.add, ALU.mult)
                        else:
                            ins = nc.vector.tensor_copy(dst, bank[n % 2])
                        ins.then_inc(sem("row5_ready"), 1)
                        n += 1
            dve.wait_ge(sem("row5_ready"), 16)
            dve.wait_ge(sem("x5_in"), 16 * NT)

            def residual(t):
                tmp = h2[t % 2]
                if t >= 2:
                    dve.wait_ge(sem(f"h2_out{t % 2}"), 16 * (t // 2))
                    dve.wait_ge(sem("h2T_mm"), 2 * (t - 1))
                for hf in range(2):
                    cols = slice(hf * 512, hf * 512 + 512)
                    dve.wait_ge(sem("o5_mm"), 2 * t + hf + 1)
                    k = own.done(nc.vector.tensor_tensor(tmp[:, cols], bank[2 + 2 * (t % 2) + hf], g1_row[:, group(t), cols], ALU.mult))
                own.wait(k)
                nc.vector.tensor_tensor(x2[:, t, :], x2[:, t, :], tmp, ALU.add).then_inc(sem("x2_ready"), 1)

            def norm(t):
                dve.wait_ge(sem("act_own5"), 2 * t + 2)
                own.link(nc.vector.reciprocal(stat5[:, t, 2:3], stat5[:, t, 1:2]))
                own.link(nc.vector.scalar_tensor_tensor(h2[t % 2], x2[:, t, :], stat5[:, t, 2:3], ss_row[:, group(t), 1, :], ALU.mult, ALU.mult))
                nc.vector.tensor_tensor(h2[t % 2], h2[t % 2], ss_row[:, group(t), 0, :], ALU.add).then_inc(sem("h2_ready"), 1)

            def scores(t):
                dve.wait_ge(sem("router_mm"), t + 1)
                nc.vector.tensor_tensor(logit[:, t, :], bank[t % 2][:, 0:36], rb, ALU.add).then_inc(sem("logit_ready"), 1)

            residual(0)
            for t in range(NT):
                if t + 1 < NT:
                    residual(t + 1)
                norm(t)
                if t:
                    scores(t - 1)
            scores(NT - 1)
            dve.wait_ge(sem("logit_ready"), NT)

            def b(ap, shape):
                return ap.unsqueeze(len(ap.shape)).to_broadcast(shape)

            def first_max(one_hot, top_v, values, tmp, width):
                shape = [P, NT, width]
                own.link(nc.vector.tensor_reduce(top_v, values, AX, ALU.max))
                own.link(nc.vector.tensor_tensor(tmp, values, b(top_v, shape), ALU.is_equal))
                own.link(nc.vector.tensor_tensor(tmp, tmp, fall_row[:, 0:width].unsqueeze(1).to_broadcast(shape), ALU.mult))
                own.link(nc.vector.tensor_reduce(pk, tmp, AX, ALU.max))
                own.link(nc.vector.tensor_tensor(one_hot, tmp, b(pk, shape), ALU.is_equal))

            pg = logit[:, :, 0:NG]
            first_max(og, gm, pg, tg, NG)
            nc.vector.tensor_tensor(tg, pg, b(gm, [P, NT, NG]), ALU.subtract).then_inc(sem("g_centred"), 1)
            le = logit[:, :, NG:].rearrange("p t (g e) -> p t g e", g=NG)
            own.link(nc.vector.tensor_tensor(lsel.rearrange("p t (g e) -> p t g e", g=NG), le, b(og, [P, NT, NG, EPG]), ALU.mult))
            own.link(nc.vector.tensor_reduce(s8, lsel.rearrange("p t (g e) -> p t e g", g=NG), AX, ALU.add))
            first_max(o1, m1, s8, t8, EPG)
            own.link(nc.vector.scalar_tensor_tensor(s8, o1, -1e30, s8, ALU.mult, ALU.add))
            first_max(o2, m2, s8, t8, EPG)
            own.link(nc.vector.tensor_tensor(m2, m2, m1, ALU.subtract))
            dve.wait_ge(sem("g_exp"), 1)
            nc.vector.tensor_reduce(gsum, tg, AX, ALU.add).then_inc(sem("m_diff"), 1)
            dve.wait_ge(sem("m_exp"), 1)
            own.link(nc.vector.tensor_scalar(m1, m2, 1.0, None, ALU.add))
            own.link(nc.vector.tensor_tensor(m1, m1, gsum, ALU.mult))
            own.link(nc.vector.reciprocal(wts[:, :, 0], m1))
            own.link(nc.vector.tensor_tensor(wts[:, :, 1], wts[:, :, 0], m2, ALU.mult))
            for one, o8 in ((e1, o1), (e2, o2)):
                own.link(nc.vector.tensor_tensor(one.rearrange("p t (g e) -> p t g e", g=NG), b(og, [P, NT, NG, EPG]),
                                                 o8.unsqueeze(2).to_broadcast([P, NT, NG, EPG]), ALU.mult))
            nc.vector.tensor_tensor(both, e1, e2, ALU.add).then_inc(sem("hits_ready"), 1)
            own.link(nc.vector.memset(tilebase[:, 0, :], 0.0))
            dve.wait_ge(sem("rank_mm"), 2)
            tot = bank[3][:, 0:NT * NE].rearrange("p (t e) -> p t e", e=NE)
            for t in range(NT):
                own.link(nc.vector.tensor_tensor(tilebase[:, t + 1, :], tot[:, t, :], tilebase[:, t, :], ALU.add))
            cnt = tilebase[:, NT, :]
            own.link(nc.vector.tensor_scalar(over, cnt, float(BLK), None, ALU.is_gt))
            for k in range(2, TOK // BLK):
                own.link(nc.vector.scalar_tensor_tensor(over, cnt, float(BLK * k), over, ALU.is_gt, ALU.add))
            own.link(nc.vector.tensor_copy(incl, over))
            a, c = incl, incl2
            for s in (1, 2, 4, 8, 16):
                own.done(nc.vector.tensor_copy(c[:, 0:s], a[:, 0:s]))
                own.link(nc.vector.tensor_tensor(c[:, s:NE], a[:, s:NE], a[:, 0:NE - s], ALU.add))
                a, c = c, a
            own.link(nc.vector.tensor_tensor(excl, a, over, ALU.subtract))
            own.link(nc.vector.tensor_scalar(over, excl, float(NE - 1), float(BLK), ALU.add, ALU.mult))
            own.link(nc.vector.tensor_tensor(over, over, first_row, ALU.subtract))
            own.link(nc.vector.tensor_tensor(slot_f, bank[2][:, 0:NT * NE].rearrange("p (t e) -> p t e", e=NE), tilebase[:, 0:NT, :], ALU.add))
            own.link(nc.vector.scalar_tensor_tensor(lsel, slot_f, float(BLK), over.unsqueeze(1).to_broadcast([P, NT, NE]), ALU.is_ge, ALU.mult))
            own.link(nc.vector.tensor_tensor(slot_f, slot_f, lsel, ALU.add))
            own.link(nc.vector.tensor_tensor(slot_f, slot_f, first_row.unsqueeze(1).to_broadcast([P, NT, NE]), ALU.add))
            for k, one in enumerate((e1, e2)):
                own.link(nc.vector.tensor_tensor(one, one, slot_f, ALU.mult))
                own.link(nc.vector.tensor_reduce(pk, one, AX, ALU.add))
                ins = nc.vector.tensor_copy(pos_i[:, :, k], pk)
                if k == 0:
                    own.link(ins)
            ins.then_inc(sem("pos_ready"), 1)
            own.link(nc.vector.tensor_scalar(o32, a, place, None, ALU.is_gt))
            own.link(nc.vector.scalar_tensor_tensor(o32, excl, place, o32, ALU.is_le, ALU.mult))
            own.link(nc.vector.tensor_tensor(o32, o32, expert_row, ALU.mult))
            own.link(nc.vector.tensor_reduce(lst[:, 0:1], o32, AX, ALU.add))
            own.link(nc.vector.tensor_copy(lst[:, 1:2], a[:, NE - 1:NE]))
            nc.vector.tensor_copy(lst_i, lst).then_inc(sem("list_ready"), 1)

        def pe_phase5(pe):
            pe.wait_ge(sem("consts5_in"), 16 * 11)
            n = 0
            for m, _, _ in MODS:
                for g in range(2):
                    for hf in range(2):
                        if n >= 2:
                            pe.wait_ge(sem("row5_ready"), n - 1)
                        nc.tensor.matmul(bank[n % 2], sel5[:, g, :], modp[:, (2 * m + hf) * 512:(2 * m + hf + 1) * 512],
                                         start=True, stop=True).then_inc(sem("row5_mm"), 1)
                        n += 1
            pe.wait_ge(sem("wout_in"), 16)
            for t in range(NT + 2):
                if t < NT:
                    if t >= 2:
                        pe.wait_ge(sem("x2_ready"), t - 1)
                    for hf in range(2):
                        for k in range(KD):
                            ins = nc.tensor.matmul(bank[2 + 2 * (t % 2) + hf], catT[:, k, t * P:(t + 1) * P], wout[:, k, hf * 512:hf * 512 + 512],
                                                   start=(k == 0), stop=(k == KD - 1))
                        ins.then_inc(sem("o5_mm"), 1)
                if t >= 2:
                    j = t - 2
                    pe.wait_ge(sem("h2_ready"), j + 1)
                    for hf in range(2):
                        if j:
                            pe.wait_ge(sem("h2T_ready"), 2 * (j - 1) + hf + 1)
                        for k in range(4):
                            kk = 4 * hf + k
                            ins = nc.tensor.transpose(bank[6 + hf][:, k * P:(k + 1) * P], h2[j % 2][:, kk * P:(kk + 1) * P], ident)
                        ins.then_inc(sem("h2T_mm"), 1)
                    pe.wait_ge(sem("h2T_ready"), 2 * j + 2)
                    if j >= 2:
                        pe.wait_ge(sem("logit_ready"), j - 1)
                    for k in range(KD):
                        ins = nc.tensor.matmul(bank[j % 2][:, 0:36], h2T[j % 2][:, k, :], rw[:, k, :], start=(k == 0), stop=(k == KD - 1))
                    ins.then_inc(sem("router_mm"), 1)
            pe.wait_ge(sem("hits_ready"), 1)
            hits = both.rearrange("p t e -> p (t e)")
            nc.tensor.matmul(bank[2][:, 0:NT * NE], before, hits, start=True, stop=True).then_inc(sem("rank_mm"), 1)
            nc.tensor.matmul(bank[3][:, 0:NT * NE], ones, hits, start=True, stop=True).then_inc(sem("rank_mm"), 1)

        top[0] = base6
        HALF = HID // 2
        idx_o = take(1).bitcast(i32)
        idx_c = [take(1).bitcast(i32) for _ in range(2)]
        xg = [take(D) for _ in range(2)]
        xT = [take(KD * BLK).rearrange("p (k c) -> p k c", k=KD) for _ in range(2)]
        sil, hid = take(HALF), take(HALF)
        hidT = take(HALF).rearrange("p (c n t) -> p c n t", c=2, n=2)
        yb = [take(HID) for _ in range(2)]
        top6 = top[0]
        assert top6 <= ARENA - 2 * WEXP
        y_v = y_dram.rearrange("s (j n) -> s j n", j=2)

        CREDIT = 3
        LOOP = 2 * NSLOT

        class Main:
            over = ""
            credit = CREDIT

            def __init__(self, e, u, n, wn, sn):
                self.e, self.n, self.w, self.wn, self.s, self.sn = e, n, u % NSLOT, wn, u % 2, sn
                self.first_slot = e * BLK

            def sem(self, name):
                return sem(name)

        class Over:
            over = "over_"
            credit = 0

            def __init__(self, m, e=None):
                self.e, self.n, self.w, self.wn, self.s, self.sn = e, m, 0, m, 0, m
                self.first_slot = m * BLK + NE * BLK

            def sem(self, name):
                return sem("over_" + name)

        def turns(eng, body, last=0):
            whole = (NE - last) // LOOP
            with eng.Fori(0, whole) as i:
                for u in range(LOOP):
                    body(Main(i * LOOP + u, u, i * LOOP + u, i * (LOOP // NSLOT) + u // NSLOT, i * (LOOP // 2) + u // 2))
            for e in range(whole * LOOP, NE):
                body(Main(e, e, e, e // NSLOT, e // 2))

        def overflow(eng, body, with_expert=False):
            count = eng.value_load(over_dram[0:1, 1:2], min_val=0, max_val=MAX_OVER)
            with eng.If(count > 0):
                with eng.Fori(0, count) as m:
                    e = eng.value_load(over_dram[bass.ds(m, 1), 0:1], min_val=0, max_val=NE - 1) if with_expert else None
                    body(Over(m, e))
            with eng.Else():
                pass

        WEIGHTS = (("h1_mm", w1_s, w1_v), ("h3_mm", w3_s, w3_v), ("y_mm6", w2_s, w2_v))

        def sp_phase6(sp):
            for k in range(NSLOT):
                for name in ("h1_mm", "h3_mm") + (("y_mm6",) if k == 2 else ()):
                    sp.sem_inc(sem(f"{name}_w{k}"), 16)
            for k in range(2):
                sp.dma_start(idx_c[k][0:BLK, :], slot_dram[k * BLK:(k + 1) * BLK, :]).then_inc(sem(f"idx_in{k}"), 16)
                sp.dma_start(w2_s[k], w2_v[k]).then_inc(sem(f"y_mm6_w{k}"), 16)

            def ahead(c):
                static = isinstance(c.n, int)
                if not static or c.n + 2 < NE:
                    sp.wait_ge(sem("xg_in%d" % c.s), 16 * c.sn + 16)
                    sp.dma_start(idx_c[c.s][0:BLK, :], slot_dram[bass.ds(c.first_slot + 2 * BLK, BLK), :]).then_inc(sem(f"idx_in{c.s}"), 16)
                if not static or c.n + NSLOT < NE:
                    for name, slot, view in WEIGHTS:
                        sp.wait_ge(sem(name), CREDIT + c.n + 1)
                        sp.dma_start(slot[c.w], one(view, c.e + NSLOT)).then_inc(sem(f"{name}_w{c.w}"), 16)

            turns(sp, ahead, last=NSLOT)

            def over(c):
                sp.wait_ge(sem("over_y_out0"), 32 * c.n + 16)
                sp.dma_start(idx_o[0:BLK, :], slot_dram[bass.ds(c.first_slot, BLK), :]).then_inc(c.sem("idx_in0"), 16)
                for name, slot, view in WEIGHTS:
                    sp.dma_start(slot[0], one(view, c.e)).then_inc(c.sem(f"{name}_w0"), 16)

            sp.wait_ge(sem("y_mm6"), CREDIT + NE)
            overflow(sp, over, with_expert=True)

        def pool_phase6(pool):
            def gather(c):
                pool.wait_ge(c.sem(f"idx_in{c.s}"), 16 * c.sn + 16)
                if not c.over:
                    pool.wait_ge(sem("xT_mm"), CREDIT + c.n - 1)
                pool.sem_inc(sem("pool_turn"), 1)
                idx = idx_o if c.over else idx_c[c.s]
                nc.gpsimd.indirect_dma_start(xg[c.s][0:BLK, :], None, h2_dram,
                                             bass.IndirectOffsetOnAxis(ap=idx.bitcast(u32)[0:BLK, :], axis=0)).then_inc(c.sem(f"xg_in{c.s}"), 16)

            turns(pool, gather)
            overflow(pool, gather)

        def act_phase6(act):
            for name in ("y_out0", "y_out1", "over_y_out0"):
                act.sem_inc(sem(name), 16)
            for name in ("xT_ready", "sil_ready", "hidT_ready"):
                act.sem_inc(sem(name), CREDIT)

            def body(c):
                k = c.credit + c.n + 1
                act.wait_ge(c.sem("xT_mm"), k)
                if not c.over:
                    act.wait_ge(sem("h3_mm"), k - 2)
                nc.scalar.copy(xT[c.s], bank[0].rearrange("p (k c) -> p k c", k=KD)).then_inc(c.sem("xT_ready"), 1)
                act.wait_ge(c.sem("h1_mm"), k)
                if not c.over:
                    act.wait_ge(sem("hid_ready"), k - 1)
                nc.scalar.activation(sil, bank[1 + 2 * c.s][:, 0:HALF], ACT.Silu).then_inc(c.sem("sil_ready"), 1)
                act.wait_ge(c.sem("hidT_mm"), k)
                if not c.over:
                    act.wait_ge(sem("y_mm6"), k - 1)
                nc.scalar.copy(hidT, bank[5][:, 0:HALF].rearrange("p (c n t) -> p c n t", c=2, n=2)).then_inc(c.sem("hidT_ready"), 1)
                act.wait_ge(c.sem("y_ready6"), k)
                for j in range(2):
                    act.dma_start(y_v[bass.ds(c.first_slot, BLK), j, :], yb[c.s][j * BLK:(j + 1) * BLK, :]).then_inc(c.sem(f"y_out{c.s}"), 16)

            turns(act, body)
            act.wait_ge(sem("y_out0"), 16 + 32 * NE // 2)
            act.wait_ge(sem("y_out1"), 16 + 32 * NE // 2)

            def over(c):
                body(c)
                act.wait_ge(sem("over_y_out0"), 32 * c.n + 48)

            overflow(act, over)

        def dve_phase6(dve):
            for name in ("hid_ready", "y_ready6"):
                dve.sem_inc(sem(name), CREDIT)

            def body(c):
                k = c.credit + c.n + 1
                dve.wait_ge(c.sem("sil_ready"), k)
                dve.wait_ge(c.sem("h3_mm"), k)
                if not c.over:
                    dve.wait_ge(sem("hidT_mm"), k - 1)
                nc.vector.tensor_tensor(hid, bank[2 + 2 * c.s][:, 0:HALF], sil, ALU.mult).then_inc(c.sem("hid_ready"), 1)
                dve.wait_ge(c.sem("y_mm6"), k)
                if not c.over:
                    dve.wait_ge(sem(f"y_out{c.s}"), 32 * c.sn + 16)
                nc.vector.tensor_copy(yb[c.s], bank[6 + c.s]).then_inc(c.sem("y_ready6"), 1)

            turns(dve, body)
            overflow(dve, body)

        def pe_phase6(pe):
            for name in ("xT_mm", "h1_mm", "h3_mm", "hidT_mm", "y_mm6"):
                pe.sem_inc(sem(name), CREDIT)

            def body(c):
                k = c.credit + c.n + 1
                pe.wait_ge(c.sem(f"xg_in{c.s}"), 16 * c.sn + 16)
                if not c.over:
                    pe.wait_ge(sem("xT_ready"), k - 1)
                pe.sem_inc(sem("pe_turn"), 1)
                for j in range(KD):
                    ins = nc.tensor.transpose(bank[0][:, j * BLK:(j + 1) * BLK], xg[c.s][0:BLK, j * P:(j + 1) * P], ident[0:BLK, 0:BLK])
                ins.then_inc(c.sem("xT_mm"), 1)
                pe.wait_ge(c.sem("xT_ready"), k)
                for name, slot, b, free in (("h1_mm", w1_s, 1, "sil_ready"), ("h3_mm", w3_s, 2, "hid_ready")):
                    pe.wait_ge(c.sem(f"{name}_w{c.w}"), 16 * c.wn + 16)
                    if not c.over:
                        pe.wait_ge(sem(free), k - 2)
                    for j in range(KD):
                        for n in range(2):
                            ins = nc.tensor.matmul(bank[b + 2 * c.s][BLK * n:BLK * n + BLK, 0:HALF], xT[c.s][:, j, :],
                                                   slot[c.w][:, j, n * HALF:(n + 1) * HALF], start=(j == 0), stop=(j == KD - 1))
                    ins.then_inc(c.sem(name), 1)
                pe.wait_ge(c.sem("hid_ready"), k)
                if not c.over:
                    pe.wait_ge(sem("hidT_ready"), k - 1)
                for j in range(2):
                    ins = nc.tensor.transpose(bank[5][:, j * P:(j + 1) * P], hid[:, j * P:(j + 1) * P], ident)
                ins.then_inc(c.sem("hidT_mm"), 1)
                pe.wait_ge(c.sem("hidT_ready"), k)
                pe.wait_ge(c.sem(f"y_mm6_w{c.w}"), 16 * c.wn + 16)
                if not c.over:
                    pe.wait_ge(sem("y_ready6"), k - 2)
                for j in range(KH):
                    for n in range(2):
                        ins = nc.tensor.matmul(bank[6 + c.s][BLK * n:BLK * n + BLK, :], hidT[:, j % 2, j // 2, :],
                                               w2_s[c.w][:, j, n * 512:(n + 1) * 512], start=(j == 0), stop=(j == KH - 1))
                ins.then_inc(c.sem("y_mm6"), 1)

            turns(pe, body)
            overflow(pe, body)

        top[0] = base6
        ya = [[take(D) for _ in range(2)] for _ in range(2)]
        sq7 = take(D)
        yo = [take(D) for _ in range(2)]
        f_row = take(D)
        stat7 = take(NT * 4).rearrange("p (t m) -> p t m", t=NT)
        y_out_v = [O[1][0, t * P:(t + 1) * P, :] for t in range(NT_S)] + [O[0][0, t * P:(t + 1) * P, :] for t in range(NT_P)]

        def sp_phase7(sp):
            sp.dma_start(f_row, A["final_row"].partition_broadcast(P)).then_inc(sem("final_in"), 16)
            for t in range(NT):
                sp.wait_ge(sem("final_ready"), t + 1)
                sp.dma_start(y_out_v[t], yo[t % 2]).then_inc(sem(f"final_out{t % 2}"), 16)
            sp.wait_ge(sem("final_out0"), 16 * NT // 2)
            sp.wait_ge(sem("final_out1"), 16 * NT // 2)

        def pool_phase7(pool):
            for t in range(NT):
                if t >= 2:
                    pool.wait_ge(sem("joined"), t - 1)
                for k in range(2):
                    nc.gpsimd.indirect_dma_start(ya[t % 2][k], None, y_dram,
                                                 bass.IndirectOffsetOnAxis(ap=pos_i.bitcast(u32)[:, t, k:k + 1], axis=0)).then_inc(sem(f"rows_in{t % 2}"), 16)

        def act_phase7(act):
            own = Own(act, sem("act_own7"))
            for t in range(NT):
                act.wait_ge(sem("joined"), t + 1)
                if t:
                    own.wait(own.n)
                own.link(nc.scalar.activation(sq7, x2[:, t, :], ACT.Square, scale=1.0 / 32.0, accum_out=stat7[:, t, 0:1]))
                own.done(nc.scalar.activation(stat7[:, t, 1:2], stat7[:, t, 0:1], ACT.Sqrt, bias=eps[:, 0:1]))

        def dve_phase7(dve):
            own = Own(dve, sem("dve_own7"))
            dve.wait_ge(sem("final_in"), 16)

            def join(t):
                a, b = ya[t % 2]
                dve.wait_ge(sem(f"rows_in{t % 2}"), 32 * (t // 2 + 1))
                own.link(nc.vector.tensor_scalar(a, a, wts[:, t, 0:1], None, ALU.mult))
                own.link(nc.vector.scalar_tensor_tensor(a, b, wts[:, t, 1:2], a, ALU.mult, ALU.add))
                nc.vector.tensor_tensor(a, a, g2_row[:, group(t), :], ALU.mult).then_inc(sem("joined0"), 1)
                dve.wait_ge(sem("joined0"), t + 1)
                nc.vector.tensor_tensor(x2[:, t, :], x2[:, t, :], a, ALU.add).then_inc(sem("joined"), 1)

            def norm(t):
                dve.wait_ge(sem("act_own7"), 2 * t + 2)
                if t >= 2:
                    dve.wait_ge(sem(f"final_out{t % 2}"), 16 * (t // 2))
                own.link(nc.vector.reciprocal(stat7[:, t, 2:3], stat7[:, t, 1:2]))
                nc.vector.scalar_tensor_tensor(yo[t % 2], x2[:, t, :], stat7[:, t, 2:3], f_row, ALU.mult, ALU.mult).then_inc(sem("final_ready"), 1)

            for t in range(NT):
                join(t)
                if t:
                    norm(t - 1)
            norm(NT - 1)

        def run_phase(sp=None, pool=None, act=None, dve=None, pe=None):
            with nc.Block() as block:
                for engine, own_program in ((block.sync, sp), (block.gpsimd, pool), (block.scalar, act), (block.vector, dve), (block.tensor, pe)):
                    if own_program is not None:
                        engine(own_program)
            nc.clear_and_free_semaphores(list(sems.values()))
            sems.clear()
            nc.all_engine_barrier()

        for programs in ((sp_phase1, pool_phase1, act_phase1, dve_phase1, pe_phase1),
                         (sp_phase2, pool_phase2, act_phase2, dve_phase2, pe_phase2),
                         (sp_phase3, pool_phase3, act_phase3, dve_phase3, pe_phase3),
                         (sp_phase4, pool_phase4, act_phase4, dve_phase4, pe_phase4),
                         (sp_phase5, pool_phase5, act_phase5, dve_phase5, pe_phase5),
                         (sp_phase6, pool_phase6, act_phase6, dve_phase6, pe_phase6),
                         (sp_phase7, pool_phase7, act_phase7, dve_phase7, None))[:upto]:
            run_phase(*programs)


def layout(inputs):
    a = {k: np.ascontiguousarray(np.asarray(v)) for k, v in inputs.items()}
    a["c_cols"] = np.ascontiguousarray(np.stack([a.pop("c_sample")[0], a.pop("c_prompt")[0]], -1)
                                       .reshape(KD, P, 2).transpose(1, 0, 2))
    a["mu"] = np.ascontiguousarray(a.pop("rwkv_mu")[0].reshape(2, NZ, P).transpose(2, 1, 0))
    rpb = a.pop("na_rpb")[0]
    pad = np.pad(rpb, ((0, 0), (0, 0), (16, 16)))
    i, m = np.arange(8)[:, None, None, None], np.arange(8)[None, None, :, None]
    qc, kc = np.arange(QB)[None, :, None, None], np.arange(KB)[None, None, None, :]
    bias = np.stack([pad[:, m - i + 7, kc + off - qc + 15 + 16] for off in (0, -8, -16)])
    a["bias"] = np.ascontiguousarray(bias.reshape(3, NH, P, 8 * KB).transpose(0, 2, 1, 3))
    a["router_w"] = np.ascontiguousarray(np.concatenate([a.pop("router_g_w")[0], a.pop("router_e_w")[0]], 1)
                                         .reshape(KD, P, NG + NE).transpose(1, 0, 2))
    a["router_b"] = np.concatenate([a.pop("router_g_b")[0], a.pop("router_e_b")[0]])
    a["final_row"] = a.pop("final_g")
    a.update(constants())
    return a


def program(nc, inputs, upto=7):
    arrays = {f"in_{k}": v for k, v in layout(inputs).items()}
    A = {k[3:]: nc.dram_tensor(k, v.shape, mybir.dt.from_np(v.dtype), kind="ExternalInput").ap() for k, v in arrays.items()}
    O = [nc.dram_tensor("y_prompt", (1, T_P, D), f32, kind="ExternalOutput").ap(),
         nc.dram_tensor("y_sample", (1, T_S, D), f32, kind="ExternalOutput").ap()]
    build(nc, A, O, upto)
    return arrays


def kernel(**inputs):
    import concourse.bacc as bacc
    from concourse.bass_utils import run_bass_kernel_spmd

    nc = bacc.Bacc("TRN2", target_bir_lowering=False, num_devices=1)
    arrays = program(nc, inputs)
    r = run_bass_kernel_spmd(nc, [arrays], core_ids=[0])
    return r.results[0]["y_prompt"], r.results[0]["y_sample"]
```

```python
from contextlib import ExitStack

import numpy as np

import concourse.bass as bass
import concourse.mybir as mybir

f32 = mybir.dt.float32
f16 = mybir.dt.float16
i32 = mybir.dt.int32
u32 = mybir.dt.uint32
ALU = mybir.AluOpType
ACT = mybir.ActivationFunctionType
AX = mybir.AxisListType.X

P = 128
D = 1024
KD = D // P
T_S, T_P = 512, 256
NT_S, NT_P = T_S // P, T_P // P
NT = NT_S + NT_P
TOK = NT * P
W = 512
HD = 64
NH = W // HD
NPAIR = NH // 2
GW = 64
QB, KB = 16, 32
NQB = GW // QB
NZ = 15
ZLORA = 12
NE, EPG, NG = 32, 8, 4
HID = 512
KH = HID // P
BLK = 64
MAX_OVER = 2 * TOK // BLK
NBLK = NE + MAX_OVER
EPS = 1e-6
LNX_EPS = 64e-5
DECAY = float(np.exp(-0.5))
BIG = 3.0e38
U_SCALE = 2048.0
LEVELS = 7


class Own:

    def __init__(self, eng, sem):
        self.eng, self.sem, self.n = eng, sem, 0

    def done(self, ins):
        self.n += 1
        ins.then_inc(self.sem, 1)
        return self.n

    def wait(self, value):
        self.eng.wait_ge(self.sem, value)

    def link(self, ins):
        self.wait(self.done(ins))


def constants():
    j, t = np.arange(P)[:, None], np.arange(P)[None, :]
    half = (np.arange(P) < P // 2).astype(np.float32)
    c = {}
    c["c_ident"] = np.eye(P, dtype=np.float32)
    c["c_ident16"] = np.eye(P, dtype=np.float16)
    c["c_tri"] = np.stack([(j <= t) - half[:, None], (j >= t) - (1 - half)[:, None]]).astype(np.float32).transpose(1, 0, 2)
    c["c_mid"] = np.stack([np.stack([half, 1 - half], 1), np.stack([1 - half, half], 1)]).astype(np.float32).transpose(1, 0, 2)
    seen = [np.concatenate([j < t, j <= t], 1), np.concatenate([j >= t, j > t], 1)]
    c["c_seen"] = np.stack([np.concatenate([m, m], 1) for m in seen]).astype(np.float32).transpose(1, 0, 2)
    c["c_pair"] = np.kron(np.eye(2), np.ones((HD, HD))).astype(np.float32)
    sel = np.zeros((P, 3, P), np.float32)
    for g in range(2):
        sel[g::32, g] = 1
    sel[0, 2, 0:2] = 1
    c["c_sel"] = sel
    before = np.zeros((P, P), np.float32)
    before[j < t] = 1
    c["c_before"] = before
    c["c_eps"] = np.tile(np.array([EPS, LNX_EPS], np.float32), (P, 1))
    c["c_ones"] = np.ones((P, P), np.float32)
    qc = np.arange(QB)
    mask = np.zeros((3, P, KB), np.float32)
    for kind, n in enumerate((0, 1, 3)):
        cols = n * QB + qc
        start = np.clip(n * QB - QB // 2, 0, GW - KB)
        win = np.clip(cols - 8, 0, GW - 16)
        kc = start + np.arange(KB)
        ok = (kc >= win[:, None]) & (kc < win[:, None] + 16)
        mask[kind] = np.tile(np.where(ok, 0.0, -1e30), (8, 1))
    c["c_window"] = np.ascontiguousarray(mask.transpose(1, 0, 2))
    e = np.arange(NE, dtype=np.float32)
    c["c_expert"] = np.tile(e, (P, 1))
    c["c_fall8"] = np.tile(8.0 - np.arange(8, dtype=np.float32), (P, 1))
    c["c_first"] = np.tile(e * BLK, (P, 1))
    c["c_place"] = np.arange(P, dtype=np.float32)[:, None].copy()
    c["c_token"] = (np.arange(NT)[None, :] * P + np.arange(P)[:, None]).astype(np.int32)
    return {k: np.ascontiguousarray(v) for k, v in c.items()}


def group(t):
    return 0 if t < NT_S else 1


def band(n):
    return min(max(n * QB - QB // 2, 0), GW - KB)


def build(nc, A, O, upto=7):
    ctx = ExitStack()
    with ctx:
        sems = {}

        def sem(name):
            if name not in sems:
                sems[name] = nc.alloc_semaphore(name=name)
            return sems[name]

        def dram(name, shape, dt=f32):
            return nc.dram_tensor(name, shape, dt, kind="Internal").ap()

        ARENA = 53200
        arena = ctx.enter_context(nc.sbuf_tensor("arena", [P, ARENA], f32))
        top = [0]

        def take(n):
            at = top[0]
            top[0] += n
            assert top[0] <= ARENA, top[0]
            return arena[:, at:at + n]

        bank = [ctx.enter_context(nc.psum_tensor(f"bank{i}", [P, 512], f32))[:, :] for i in range(8)]

        v_dram = dram("v_scratch", [TOK, W])
        dir_dram = dram("direction_scratch", [2, 3, NT, P, W])
        h2_dram = dram("h2_scratch", [TOK, D])
        slot_dram = dram("slot_token", [NBLK * BLK, 1], i32)
        y_dram = dram("slot_out", [NBLK * BLK, D])
        over_dram = dram("overflow_list", [MAX_OVER, 2], i32)

        ident = take(P)
        eps = take(2)
        modp = take(6 * D)
        catT = take(KD * TOK).rearrange("p (c t) -> p c t", c=KD)
        hT = catT
        base5 = top[0]
        ident16 = take(P // 2).bitcast(f16)
        kk_row, ka_row, rk_row, lg_row, lb_row = (take(W) for _ in range(5))
        rkv = take(3 * NT * W).rearrange("p (q t c) -> p q t c", q=3, t=NT)
        kkn = take(NT * W).rearrange("p (t c) -> p t c", t=NT)
        gate = take(NT * W).rearrange("p (t c) -> p t c", t=NT)
        bonus = take(NT * NH).rearrange("p (t h) -> p t h", t=NT)
        base4 = top[0]
        qT = take(NPAIR * TOK).rearrange("p (c t) -> p c t", c=NPAIR)
        kT = take(NPAIR * TOK).rearrange("p (c t) -> p c t", c=NPAIR)
        base3 = top[0]

        top[0] = base3
        adaw = [take(KD * 512).rearrange("p (k n) -> p k n", k=KD) for _ in range(2)]
        NWIN = 3
        winb = [take(KD * P).rearrange("p (k n) -> p k n", k=KD) for _ in range(NWIN)]
        lz = take(3 * TOK).rearrange("p (c t) -> p c t", c=3)
        sel = take(3 * P).rearrange("p (g c) -> p g c", g=3)
        mu = take(NZ * 3).rearrange("p (c m) -> p c m", m=3)
        cT = take(KD * 2).rearrange("p (k g) -> p k g", g=2)
        siluT = take(KD * 32).rearrange("p (k m) -> p k m", k=KD)
        stat = take(NT * 4).rearrange("p (t m) -> p t m", t=NT)
        at_rkv = top[0]
        top[0] = base5 + P // 2 + 5 * W
        xb = [take(D) for _ in range(2)]
        hb = [take(D) for _ in range(2)]
        rows = take(4 * D).rearrange("p (g m d) -> p g m d", g=2, m=2)
        n1_row = take(D)
        sq1 = take(D)
        adab = [take(512) for _ in range(2)]
        zs = [take(TOK) for _ in range(2)]
        top[0] = at_rkv

        x_tile = [A["x_sample"][0, t * P:(t + 1) * P, :] for t in range(NT_S)] + \
                 [A["x_prompt"][0, t * P:(t + 1) * P, :] for t in range(NT_P)]
        ada_v = A["ada_w"][0].rearrange("(k p) n -> p k n", p=P)
        win_v = A["w_in"][0].rearrange("(k p) n -> p k n", p=P)
        ZCOL = 3 * W
        order = [("z", ZLORA + i, ZCOL + (ZLORA + i) * P) for i in range(3)]
        order += [("z", i, ZCOL + i * P) for i in range(ZLORA)]
        order += [("q", i, i * P) for i in range(NPAIR)] + [("k", i, W + i * P) for i in range(NPAIR)]
        NCHUNK = 6 * D // 512
        ring = [("ada", c) for c in range(NCHUNK)] + [("wv", 0)]
        TMOD = len(order) - (NCHUNK - 4)

        def sp_phase1(sp):
            late = [(kk_row, A["rwkv_kk"][0].partition_broadcast(P)), (ka_row, A["rwkv_ka"][0].partition_broadcast(P)),
                    (rk_row, A["rwkv_rk"][0].partition_broadcast(P)), (lg_row, A["rwkv_lnx_g"][0].partition_broadcast(P)),
                    (lb_row, A["rwkv_lnx_b"][0].partition_broadcast(P)), (ident16, A["c_ident16"])]
            early = [(sel, A["c_sel"]), (ident, A["c_ident"]), (eps, A["c_eps"]), (mu[:, :, 0:2], A["mu"]),
                     (n1_row, A["norm1_g"][0].partition_broadcast(P))]
            sp.dma_start(cT, A["c_cols"]).then_inc(sem("consts_in"), 16)

            def wide(i):
                kind, c = ring[i]
                if i >= 2:
                    sp.wait_ge(sem("mod_mm"), i - 1)
                s = sem(f"wide_in{i % 2}")
                if kind == "ada":
                    sp.dma_start(adaw[i % 2], ada_v[:, :, c * 512:(c + 1) * 512]).then_inc(s, 16)
                    sp.dma_start(adab[i % 2][0:1, :], A["ada_b"][0:1, c * 512:(c + 1) * 512]).then_inc(s, 16)
                else:
                    sp.dma_start(adaw[i % 2], win_v[:, :, 2 * W:3 * W]).then_inc(s, 32)

            def win(i):
                if i >= NWIN:
                    sp.wait_ge(sem("proj_mm"), i - NWIN + 1)
                c = order[i][2]
                sp.dma_start(winb[i % NWIN], win_v[:, :, c:c + P]).then_inc(sem(f"win_in{i % NWIN}"), 16)

            def x(t):
                if t >= 2:
                    sp.wait_ge(sem("x_used"), t - 1)
                sp.dma_start(xb[t % 2], x_tile[t]).then_inc(sem(f"x_in{t % 2}"), 16)

            wide(0)
            for dst, src in early:
                sp.dma_start(dst, src).then_inc(sem("consts_in"), 16)
            x(0)
            x(1)
            for i in range(1, 4):
                wide(i)
            for i in range(NWIN):
                win(i)
            for t in range(2, NT):
                x(t)
            wide(4)
            wide(5)
            for dst, src in late:
                sp.dma_start(dst, src).then_inc(sem("late_in"), 16)
            for i in range(NWIN, len(order)):
                win(i)
                if i >= TMOD + NWIN:
                    wide(6 + i - TMOD - NWIN)
            for i in range(6 + len(order) - TMOD - NWIN, len(ring)):
                wide(i)
            sp.wait_ge(sem("late_in"), 16 * len(late))

        def pool_phase1(pool):
            nc.gpsimd.memset(siluT, 0.0).then_inc(sem("silu_zero"), 1)

        def act_phase1(act):
            own = Own(act, sem("act_own"))
            act.wait_ge(sem("consts_in"), 16 * 6)
            act.wait_ge(sem("silu_zero"), 1)
            nc.scalar.activation(siluT[:, :, 0:2], cT, ACT.Silu).then_inc(sem("silu_ready"), 1)

            def mod(i, at):
                act.wait_ge(sem("mod_mm"), i + 1)
                nc.scalar.copy(modp[:, at * 512:(at + 1) * 512], bank[i % 2]).then_inc(sem("mod_ready"), 1)

            for i in range(4):
                mod(i, i)

            def rms(t):
                act.wait_ge(sem(f"x_in{t % 2}"), 16 * (t // 2 + 1))
                if t:
                    own.wait(own.n)
                own.link(nc.scalar.activation(sq1, xb[t % 2], ACT.Square, scale=1.0 / 32.0, accum_out=stat[:, t, 0:1]))
                own.done(nc.scalar.activation(stat[:, t, 1:2], stat[:, t, 0:1], ACT.Sqrt, bias=eps[:, 0:1]))

            rms(0)
            rms(1)
            for t in range(NT):
                act.wait_ge(sem("hT_mm"), 2 * t + 1)
                nc.scalar.copy(hT[:, 0:4, t * P:(t + 1) * P], bank[2].rearrange("p (k c) -> p k c", k=4)).then_inc(sem("hT_act"), 1)
                if t + 2 < NT:
                    rms(t + 2)
            for i, (kind, c, _) in enumerate(order):
                b0, b1 = bank[4 + i % 2], bank[6 + i % 2]
                act.wait_ge(sem("proj_mm"), i + 1)
                if kind in "qk":
                    dst = qT if kind == "q" else kT
                    s = float(HD) ** -0.5 if kind == "q" else 1.0
                    for lo, hi, src in ((0, T_S, b0), (T_S, TOK, b1[:, 0:T_P])):
                        to = dst[:, c, lo:hi]
                        if kind == "q":
                            to = to.rearrange("p (n r c) -> p r n c", n=NQB, c=QB)
                            src = src.rearrange("p (r n c) -> p r n c", n=NQB, c=QB)
                        nc.scalar.mul(to, src, s).then_inc(sem("proj_act"), 1)
                else:
                    if i == 0:
                        act.wait_ge(sem("mu_ready"), 1)
                    dst = lz[:, c - ZLORA, :] if c >= ZLORA else zs[i % 2]
                    if c < ZLORA and i >= 5:
                        act.wait_ge(sem("z_tr"), i - 4)
                    nc.scalar.mul(dst[:, 0:T_S], b0, mu[:, c, 2:3]).then_inc(sem("proj_act"), 1)
                    nc.scalar.mul(dst[:, T_S:TOK], b1[:, 0:T_P], mu[:, c, 2:3]).then_inc(sem("proj_act"), 1)
                    if c < ZLORA and i >= 4:
                        act_z_evac(act, i - 1)
                if i == 15:
                    act_z_evac(act, 14)
                if i >= TMOD:
                    mod(i - TMOD + 4, i - TMOD + 4)
            for i, t in enumerate(range(NT)):
                act.wait_ge(sem("v_mm"), i + 1)
                if i >= 2:
                    act.wait_ge(sem(f"v_out{i % 2}"), 16 * (i // 2))
                nc.scalar.copy(zs[i % 2][:, 0:W], bank[2 + i % 2]).then_inc(sem("v_ready"), 1)
                act.wait_ge(sem("v_ready"), i + 1)
                act.dma_start(v_dram[t * P:(t + 1) * P, :], zs[i % 2][:, 0:W]).then_inc(sem(f"v_out{i % 2}"), 16)
            act.wait_ge(sem("v_out0"), 48)
            act.wait_ge(sem("v_out1"), 48)

        def act_z_evac(act, i):
            c = order[i][1]
            act.wait_ge(sem("z_tr"), i - 2)
            nc.scalar.copy(rkv[:, c // 4, 0:NT_S, (c % 4) * P:(c % 4 + 1) * P],
                           bank[i % 2].rearrange("p (t c) -> p t c", t=4)).then_inc(sem("z_act"), 1)

        def dve_z_evac(dve, i):
            c = order[i][1]
            dve.wait_ge(sem("z_tr"), i - 2)
            nc.vector.tensor_copy(rkv[:, c // 4, NT_S:NT, (c % 4) * P:(c % 4 + 1) * P],
                                  bank[2 + i % 2][:, 0:256].rearrange("p (t c) -> p t c", t=2)).then_inc(sem("z_dve"), 1)

        def dve_phase1(dve):
            own = Own(dve, sem("dve_own"))
            dve.wait_ge(sem("consts_in"), 16 * 6)
            own.link(nc.vector.tensor_tensor(mu[:, :, 2], mu[:, :, 0], mu[:, :, 1], ALU.add))
            nc.vector.tensor_scalar(mu[:, :, 2], mu[:, :, 2], -1.0, 1.0, ALU.mult, ALU.add).then_inc(sem("mu_ready"), 1)
            n = 0
            for m in range(2):
                for g in range(2):
                    for hf in range(2):
                        dve.wait_ge(sem("row_mm"), n + 1)
                        dst = rows[:, g, m, hf * 512:(hf + 1) * 512]
                        if m == 0:
                            ins = nc.vector.tensor_copy(dst, bank[n % 2])
                        else:
                            ins = nc.vector.scalar_tensor_tensor(dst, bank[n % 2], 1.0, n1_row[:, hf * 512:(hf + 1) * 512],
                                                                 ALU.add, ALU.mult)
                        ins.then_inc(sem("row_ready"), 1)
                        n += 1
            dve.wait_ge(sem("row_ready"), 8)

            def hT_evac(t):
                dve.wait_ge(sem("hT_mm"), 2 * t + 2)
                nc.vector.tensor_copy(hT[:, 4:8, t * P:(t + 1) * P], bank[3].rearrange("p (k c) -> p k c", k=4)).then_inc(sem("hT_dve"), 1)

            for t in range(NT):
                if t >= 2:
                    dve.wait_ge(sem("hT_mm"), 2 * t - 2)
                dve.wait_ge(sem("act_own"), 2 * t + 2)
                own.link(nc.vector.reciprocal(stat[:, t, 2:3], stat[:, t, 1:2]))
                ins = nc.vector.scalar_tensor_tensor(hb[t % 2], xb[t % 2], stat[:, t, 2:3], rows[:, group(t), 1, :], ALU.mult, ALU.mult)
                ins.then_inc(sem("x_used"), 1)
                dve.wait_ge(sem("x_used"), t + 1)
                nc.vector.tensor_tensor(hb[t % 2], hb[t % 2], rows[:, group(t), 0, :], ALU.add).then_inc(sem("h_ready"), 1)
                if t:
                    hT_evac(t - 1)
            hT_evac(NT - 1)
            for i, (kind, c, _) in enumerate(order):
                if kind != "z":
                    if i == 15:
                        dve_z_evac(dve, 14)
                    continue
                b0, b1 = bank[4 + i % 2], bank[6 + i % 2]
                dst = lz[:, c - ZLORA, :] if c >= ZLORA else zs[i % 2]
                dve.wait_ge(sem("proj_act"), 2 * i + 2)
                own.done(nc.vector.scalar_tensor_tensor(dst[:, 1:T_S], b0[:, 0:T_S - 1], mu[:, c, 0:1], dst[:, 1:T_S], ALU.mult, ALU.add))
                k = own.done(nc.vector.scalar_tensor_tensor(dst[:, T_S + 1:TOK], b1[:, 0:T_P - 1], mu[:, c, 0:1], dst[:, T_S + 1:TOK], ALU.mult, ALU.add))
                own.wait(k)
                nc.vector.scalar_tensor_tensor(dst[:, 0:T_S - 1], b0[:, 1:T_S], mu[:, c, 1:2], dst[:, 0:T_S - 1], ALU.mult, ALU.add).then_inc(sem("z_ready"), 1)
                nc.vector.scalar_tensor_tensor(dst[:, T_S:TOK - 1], b1[:, 1:T_P], mu[:, c, 1:2], dst[:, T_S:TOK - 1], ALU.mult, ALU.add).then_inc(sem("z_ready"), 1)
                if c < ZLORA and i >= 4:
                    dve_z_evac(dve, i - 1)

        def pe_phase1(pe):
            def mod(i, r):
                pe.wait_ge(sem(f"wide_in{r % 2}"), 32 * (r // 2 + 1))
                if i >= 2:
                    pe.wait_ge(sem("mod_ready"), i - 1)
                for k in range(2):
                    for q in range(4):
                        nc.tensor.matmul(bank[i % 2][32 * q:32 * q + 32, :], siluT[:, 2 * q + k, :], adaw[r % 2][:, 2 * q + k, :],
                                         start=(k == 0), stop=(k == 1 and q > 0), tile_position=(0, 32 * q))
                nc.tensor.matmul(bank[i % 2][0:32, :], sel[0:1, 2, 0:32], adab[r % 2][0:1, :],
                                 start=False, stop=True).then_inc(sem("mod_mm"), 1)

            pe.wait_ge(sem("silu_ready"), 1)
            pe.wait_ge(sem("consts_in"), 16 * 6)
            for i in range(4):
                mod(i, i)
            pe.wait_ge(sem("mod_ready"), 4)
            n = 0
            for m in range(2):
                for g in range(2):
                    for hf in range(2):
                        if n >= 2:
                            pe.wait_ge(sem("row_ready"), n - 1)
                        c = m * 2 + hf
                        nc.tensor.matmul(bank[n % 2], sel[:, g, :], modp[:, c * 512:(c + 1) * 512], start=True, stop=True).then_inc(sem("row_mm"), 1)
                        n += 1
            for t in range(NT):
                pe.wait_ge(sem("h_ready"), t + 1)
                for hf in range(2):
                    if t:
                        pe.wait_ge(sem("hT_act" if hf == 0 else "hT_dve"), t)
                    for k in range(4):
                        ins = nc.tensor.transpose(bank[2 + hf][:, k * P:(k + 1) * P], hb[t % 2][:, (hf * 4 + k) * P:(hf * 4 + k + 1) * P], ident)
                    ins.then_inc(sem("hT_mm"), 1)
            pe.wait_ge(sem("hT_act"), NT)
            pe.wait_ge(sem("hT_dve"), NT)

            def z_transposes(i):
                pe.wait_ge(sem("z_ready"), 2 * i + 2)
                if i >= 5:
                    pe.wait_ge(sem("z_act"), i - 4)
                    pe.wait_ge(sem("z_dve"), i - 4)
                for t in range(NT):
                    dst = bank[i % 2][:, t * P:(t + 1) * P] if t < NT_S else bank[2 + i % 2][:, (t - NT_S) * P:(t - NT_S + 1) * P]
                    ins = nc.tensor.transpose(dst, zs[i % 2][:, t * P:(t + 1) * P], ident)
                ins.then_inc(sem("z_tr"), 1)

            for i, (kind, c, _) in enumerate(order):
                pe.wait_ge(sem(f"win_in{i % NWIN}"), 16 * (i // NWIN + 1))
                if i >= 2:
                    pe.wait_ge(sem("proj_act"), 2 * (i - 1))
                    if order[i - 2][0] == "z":
                        pe.wait_ge(sem("z_ready"), 2 * (i - 1))
                for k in range(KD):
                    nc.tensor.matmul(bank[4 + i % 2], winb[i % NWIN][:, k, :], hT[:, k, 0:T_S], start=(k == 0), stop=(k == KD - 1))
                    ins = nc.tensor.matmul(bank[6 + i % 2][:, 0:T_P], winb[i % NWIN][:, k, :], hT[:, k, T_S:TOK], start=(k == 0), stop=(k == KD - 1))
                ins.then_inc(sem("proj_mm"), 1)
                if 4 <= i <= 15:
                    z_transposes(i - 1)
                if i >= TMOD:
                    if i == TMOD:
                        pe.wait_ge(sem("z_act"), 12)
                        pe.wait_ge(sem("z_dve"), 12)
                    mod(i - TMOD + 4, i - TMOD + 4)
            pe.wait_ge(sem("wide_in0"), 32 * (NCHUNK // 2 + 1))
            pe.wait_ge(sem("mod_ready"), NCHUNK)
            pe.wait_ge(sem("z_act"), 12)
            pe.wait_ge(sem("z_dve"), 12)
            for t in range(NT):
                if t >= 2:
                    pe.wait_ge(sem("v_ready"), t - 1)
                for k in range(KD):
                    ins = nc.tensor.matmul(bank[2 + t % 2], hT[:, k, t * P:(t + 1) * P], adaw[0][:, k, :], start=(k == 0), stop=(k == KD - 1))
                ins.then_inc(sem("v_mm"), 1)

        GR = [T_S // GW, T_P // GW]
        TOFF = [0, T_S]
        top[0] = base3
        w_lora = take(5 * W).rearrange("p (j c) -> p j c", j=5)
        lrow = take(4 * W).rearrange("p (j c) -> p j c", j=4)
        nrm = take(NT * NH)
        bias = take(3 * NH * 8 * KB).rearrange("p (k h c) -> p k h c", k=3, h=NH)
        window = take(3 * KB).rearrange("p (k c) -> p k c", k=3)
        at_lz = base3 + 2 * KD * 512 + NWIN * KD * P
        assert top[0] <= at_lz
        top[0] = at_lz + 3 * TOK
        sq2 = take(W)
        bon = take(W)
        at_band = top[0]
        sg = catT.rearrange("p c t -> p (c t)").rearrange("p (b d q c) -> p b d q c", b=2, d=2, q=3)
        top[0] = at_band
        vb = [take(W) for _ in range(2)]
        top[0] = base3
        vb += [take(W) for _ in range(NQB * 3 - 3)]
        assert top[0] <= base3 + 9 * W
        top[0] = at_lz + 3 * TOK
        vb.append(take(W))

        def band_load(sp, g, n):
            for m in range(GR[g]):
                r0 = TOFF[g] + m * GW + band(n)
                s = m // 4 if g == 0 else 2
                sp.dma_start(vband(n, s)[32 * (m % 4):32 * (m % 4) + 32, :], v_dram[r0:r0 + KB, :]).then_inc(sem(f"band_in{g}{n}"), 16)

        def vband(n, s):
            return vb[2 * n + s] if s < 2 else vb[2 * NQB + n]

        def sp_phase2(sp):
            sp.dma_start(w_lora[:, 4, :], A["rwkv_g2"][0]).then_inc(sem("lora_in"), 16)
            for d in range(2):
                sp.dma_start(lrow[:, 2 * d, :], A["rwkv_w0"][0, d].partition_broadcast(P)).then_inc(sem("lora_in"), 16)
                sp.dma_start(lrow[:, 2 * d + 1, :], A["rwkv_a0"][0, d].partition_broadcast(P)).then_inc(sem("lora_in"), 16)
            for d in range(2):
                half = slice(d * 64, d * 64 + 64)
                sp.dma_start(w_lora[half, 2 * d, :], A["rwkv_w2"][0, d]).then_inc(sem("lora_in"), 16)
                sp.dma_start(w_lora[half, 2 * d + 1, :], A["rwkv_a2"][0, d]).then_inc(sem("lora_in"), 16)
            sp.dma_start(window, A["c_window"]).then_inc(sem("bias_in"), 16)
            for k in range(3):
                sp.dma_start(bias[:, k], A["bias"][k]).then_inc(sem("bias_in"), 16)
            band_load(sp, 0, 0)
            for t in range(NT):
                sp.wait_ge(sem("key_ready"), t + 1)
                sp.dma_start(dir_dram[:, :, t].rearrange("d q p c -> p (d q) c"), sg[:, t % 2].rearrange("p d q c -> p (d q) c")).then_inc(sem(f"sig_out{t % 2}"), 16)
            sp.wait_ge(sem("sig_out0"), 16 * NT // 2)
            sp.wait_ge(sem("sig_out1"), 16 * NT // 2)
            sp.wait_ge(sem("band_in00"), 16 * GR[0])

        def pool_phase2(pool):
            for d in range(2):
                other = slice(64 - d * 64, 128 - d * 64)
                nc.gpsimd.memset(w_lora[other, 2 * d:2 * d + 2, :], 0.0).then_inc(sem("lora_zero"), 1)
            pool.wait_ge(sem("lora_zero"), 2)
            own = Own(pool, sem("pool_own2"))
            for t in range(NT):
                nc.gpsimd.tensor_tensor(kkn[:, t, :], rkv[:, 1, t, :], kk_row, ALU.mult).then_inc(sem("kk_raw"), 1)
                pool.wait_ge(sem("kk_raw"), t + 1)
                if t:
                    pool.wait_ge(sem("kk_sum"), t)
                nc.gpsimd.tensor_tensor(sq2, kkn[:, t, :], kkn[:, t, :], ALU.mult).then_inc(sem("kk_sq"), 1)
                if t:
                    bonus_terms(pool, own, t - 1)
            bonus_terms(pool, own, NT - 1)

        def bonus_terms(pool, own, t):
            pool.wait_ge(sem("key_ready"), t + 1)
            if t:
                pool.wait_ge(sem("bonus_read"), t)
            nc.gpsimd.tensor_tensor(bon, sg[:, t % 2, 0, 2, :], sg[:, t % 2, 1, 2, :], ALU.add).then_inc(sem("keys_added"), 1)
            pool.wait_ge(sem("keys_added"), t + 1)
            own.link(nc.gpsimd.tensor_tensor(bon, bon, rkv[:, 0, t, :], ALU.mult))
            nc.gpsimd.tensor_tensor(bon, bon, rk_row, ALU.mult).then_inc(sem("bonus_ready"), 1)

        def act_phase2(act):
            nc.scalar.activation(lz[:, 0, :], lz[:, 0, :], ACT.Tanh).then_inc(sem("lz_act"), 1)
            nc.scalar.activation(lz[:, 2, :], lz[:, 2, :], ACT.Sigmoid).then_inc(sem("lz_act"), 1)
            for t in range(NT):
                act.wait_ge(sem("pre_ready"), 4 * t + 4)
                nc.scalar.activation(sg[:, t % 2, :, 0:2, :], sg[:, t % 2, :, 0:2, :], ACT.Sigmoid).then_inc(sem("sig_ready"), 1)
                act.wait_ge(sem("lora_mm"), 5 * t + 5)
                nc.scalar.copy(gate[:, t, :], bank[4]).then_inc(sem("gate_ready"), 1)
            act.wait_ge(sem("kk_sum"), NT)
            nc.scalar.activation(nrm, nrm, ACT.Sqrt).then_inc(sem("kk_root"), 1)

        def pe_phase2(pe):
            pe.wait_ge(sem("lora_in"), 16 * 9)
            pe.wait_ge(sem("lora_zero"), 2)
            pe.wait_ge(sem("lz_act"), 2)
            for t in range(NT):
                for j in range(5):
                    if t:
                        if j < 4:
                            pe.wait_ge(sem("pre_ready"), 4 * (t - 1) + j + 1)
                        else:
                            pe.wait_ge(sem("gate_ready"), t)
                    c = 2 if j == 4 else j % 2
                    nc.tensor.matmul(bank[j], lz[:, c, t * P:(t + 1) * P], w_lora[:, j, :], start=True, stop=True).then_inc(sem("lora_mm"), 1)

        def dve_phase2(dve):
            own = Own(dve, sem("dve_own2"))
            dve.wait_ge(sem("lora_in"), 16 * 9)

            def key_sum(t):
                dve.wait_ge(sem("kk_sq"), t + 1)
                nc.vector.reduce_sum(nrm[:, t * NH:(t + 1) * NH], sq2.rearrange("p (h c) -> p h c", h=NH), AX).then_inc(sem("kk_sum"), 1)

            def before_sigmoid(t):
                if t >= 2:
                    dve.wait_ge(sem(f"sig_out{t % 2}"), 16 * (t // 2))
                    dve.wait_ge(sem("keys_added"), t - 1)
                for j in range(4):
                    dve.wait_ge(sem("lora_mm"), 5 * t + j + 1)
                    nc.vector.tensor_tensor(sg[:, t % 2, j // 2, j % 2, :], bank[j], lrow[:, j, :], ALU.add).then_inc(sem("pre_ready"), 1)

            def bonus_sum(t):
                dve.wait_ge(sem("bonus_ready"), t + 1)
                nc.vector.reduce_sum(bonus[:, t, :], bon.rearrange("p (h c) -> p h c", h=NH), AX).then_inc(sem("bonus_read"), 1)

            before_sigmoid(0)
            for t in range(NT):
                if t == 0:
                    before_sigmoid(1)
                key_sum(t)
                dve.wait_ge(sem("sig_ready"), t + 1)
                keys = [sg[:, t % 2, d, 2, :] for d in range(2)]
                for d in range(2):
                    own.done(nc.vector.scalar_tensor_tensor(keys[d], sg[:, t % 2, d, 1, :], -1.0, ka_row, ALU.add, ALU.mult))
                own.wait(own.n - 1)
                own.done(nc.vector.scalar_tensor_tensor(keys[0], keys[0], 1.0, rkv[:, 1, t, :], ALU.add, ALU.mult))
                own.wait(own.n)
                nc.vector.scalar_tensor_tensor(keys[1], keys[1], 1.0, rkv[:, 1, t, :], ALU.add, ALU.mult).then_inc(sem("key_ready"), 1)
                if 1 <= t < NT - 1:
                    before_sigmoid(t + 1)
                if t:
                    bonus_sum(t - 1)
            bonus_sum(NT - 1)
            dve.wait_ge(sem("kk_root"), 1)
            own.link(nc.vector.tensor_scalar(nrm, nrm, 1e-12, None, ALU.max))
            own.link(nc.vector.reciprocal(nrm, nrm))
            for t in range(NT):
                k3 = kkn[:, t, :].rearrange("p (h c) -> p h c", h=NH)
                s3 = nrm[:, t * NH:(t + 1) * NH].unsqueeze(2).to_broadcast([P, NH, HD])
                nc.vector.tensor_tensor(k3, k3, s3, ALU.mult)
            dve.wait_ge(sem("bias_in"), 16 * 4)
            mask_bias(0)

        def mask_bias(k):
            b3 = bias[:, k].rearrange("p h (m c) -> p (h m) c", c=KB)
            return nc.vector.tensor_tensor(b3, b3, window[:, k, :].unsqueeze(1).to_broadcast([P, NH * 8, KB]), ALU.add)

        top[0] = at_lz
        NSC = 6
        AT, AO = 4, 6
        sc = [take(8 * KB) for _ in range(NSC)]
        pT = [take(8 * KB) for _ in range(2)]
        items = [(g, n, h) for g in range(2) for n in range(NQB) for h in range(NH)]
        NI = len(items)
        nmax, psum_row, pinv = (take(NI) for _ in range(3))
        assert top[0] <= at_lz + 3 * TOK
        KIND = [0, 1, 1, 2]

        def grid(ap, g, col, cols):
            return ap[:, TOFF[g]:TOFF[g] + GR[g] * GW].rearrange("p (r c) -> p r c", c=GW)[:, :, col:col + cols]

        def sp_phase3(sp):
            for g in range(2):
                for n in range(NQB):
                    if (g, n) != (0, 0):
                        band_load(sp, g, n)

        def pool_phase3(pool):
            for i, (g, n, h) in enumerate(items):
                nq, nk = GR[g] * QB, GR[g] * KB
                pool.wait_ge(sem("p_inv"), i + 1)
                nc.gpsimd.tensor_scalar(sc[i % NSC][0:nq, 0:nk], sc[i % NSC][0:nq, 0:nk], pinv[0:nq, i:i + 1], None, ALU.mult).then_inc(sem("p_ready"), 1)

        def act_phase3(act):
            for i in range(NI + AO):
                if i < NI:
                    g, n, h = items[i]
                    nq, nk = GR[g] * QB, GR[g] * KB
                    act.wait_ge(sem("s_max"), i + 1)
                    nc.scalar.activation(sc[i % NSC][0:nq, 0:nk], sc[i % NSC][0:nq, 0:nk], ACT.Exp, bias=nmax[0:nq, i:i + 1],
                                         accum_out=psum_row[0:nq, i:i + 1]).then_inc(sem("p_exp"), 1)
                if AT <= i < NI + AT:
                    j = i - AT
                    n_t = 256 if items[j][0] == 0 else 64
                    act.wait_ge(sem("pT_mm"), j + 1)
                    if j >= 2:
                        act.wait_ge(sem("o_mm"), j - 1)
                    nc.scalar.copy(pT[j % 2][:, 0:n_t], bank[3 + j % 2][:, 0:n_t]).then_inc(sem("pT_ready"), 1)
                if i >= AO and (i - AO) % 2 == 1:
                    j = i - AO
                    g, n, h = items[j]
                    act.wait_ge(sem("o_mm"), j + 1)
                    nc.scalar.copy(grid(catT[:, h // 2, :], g, n * QB, QB),
                                   bank[5 + (j // 2) % 2][:, 0:GR[g] * QB].rearrange("p (r c) -> p r c", c=QB)).then_inc(sem("o_ready"), 1)

        def dve_phase3(dve):
            own = Own(dve, sem("dve_own3"))

            def inverse(i):
                nq = GR[items[i][0]] * QB
                dve.wait_ge(sem("p_exp"), i + 1)
                nc.vector.reciprocal(pinv[0:nq, i:i + 1], psum_row[0:nq, i:i + 1]).then_inc(sem("p_inv"), 1)

            for i, (g, n, h) in enumerate(items):
                nq, nk = GR[g] * QB, GR[g] * KB
                dve.wait_ge(sem("s_mm"), i + 1)
                if i >= NSC:
                    dve.wait_ge(sem("pT_mm"), i - NSC + 1)
                own.link(nc.vector.tensor_tensor(sc[i % NSC][0:nq, 0:nk], bank[i % 3][0:nq, 0:nk], bias[0:nq, KIND[n], h, 0:nk], ALU.add))
                nc.vector.tensor_reduce(nmax[0:nq, i:i + 1], sc[i % NSC][0:nq, 0:nk], AX, ALU.max, negate=True).then_inc(sem("s_max"), 1)
                if i:
                    inverse(i - 1)
                if i in (4, 10):
                    own.link(mask_bias(1 if i == 4 else 2))
            inverse(NI - 1)

        def pe_phase3(pe):
            for i in range(NI + AO):
                if i < NI:
                    g, n, h = items[i]
                    nq, nk = GR[g] * QB, GR[g] * KB
                    hp = slice(64 * (h % 2), 64 * (h % 2) + 64)
                    if i >= 3:
                        pe.wait_ge(sem("s_max"), i - 2)
                    nc.tensor.matmul(bank[i % 3][0:nq, 0:nk], qT[hp, h // 2, TOFF[g] + n * nq:TOFF[g] + (n + 1) * nq], grid(kT[hp, h // 2, :], g, band(n), KB),
                                     start=True, stop=True).then_inc(sem("s_mm"), 1)
                if AT <= i < NI + AT:
                    j = i - AT
                    g = items[j][0]
                    nq = GR[g] * QB
                    pe.wait_ge(sem("p_ready"), j + 1)
                    if j >= 2:
                        pe.wait_ge(sem("pT_ready"), j - 1)
                    for s in range(2 - g):
                        ins = nc.tensor.transpose(bank[3 + j % 2][:, s * P:s * P + nq], sc[j % NSC][0:nq, s * P:(s + 1) * P], ident[0:nq, 0:nq])
                    ins.then_inc(sem("pT_mm"), 1)
                if i >= AO:
                    j = i - AO
                    g, n, h = items[j]
                    nq = GR[g] * QB
                    hp = slice(64 * (h % 2), 64 * (h % 2) + 64)
                    pe.wait_ge(sem("pT_ready"), j + 1)
                    if h == 0 and (g, n) != (0, 0):
                        pe.wait_ge(sem(f"band_in{g}{n}"), 16 * GR[g])
                    if j >= 4 and h % 2 == 0:
                        pe.wait_ge(sem("o_ready"), j // 2 - 1)
                    for s in range(2 - g):
                        ins = nc.tensor.matmul(bank[5 + (j // 2) % 2][hp, 0:nq], vband(n, 2 if g else s)[:, h * HD:(h + 1) * HD],
                                               pT[j % 2][:, s * P:s * P + nq], start=(s == 0), stop=(s == 1 - g))
                    ins.then_inc(sem("o_mm"), 1)

        top[0] = base4
        tri = take(2 * P).rearrange("p (d c) -> p d c", d=2)
        midc = take(4).rearrange("p (d c) -> p d c", d=2)
        seen = take(2 * 512).rearrange("p (d c) -> p d c", d=2)
        pairm = take(P)
        sgw = [take(3 * W).rearrange("p (q c) -> p q c", q=3) for _ in range(2)]
        cin, cinv = take(W), take(W)
        tok_ar = take(2 * W).rearrange("p (q c) -> p q c", q=2)
        tok_bk = [take(2 * W).rearrange("p (q c) -> p q c", q=2) for _ in range(2)]
        bkT = take(2 * W).rearrange("p (q j c) -> p q j c", q=2, j=NPAIR)
        arT = take(2 * W).rearrange("p (q j c) -> p q j c", q=2, j=NPAIR)
        ar4 = take(NPAIR * 512).rearrange("p (j c) -> p j c", j=NPAIR)
        Lb = take(NH * 3 * P).rearrange("p (h r c) -> p h r c", h=NH, r=3)
        Lk = take(NPAIR * 512).rearrange("p (j c) -> p j c", j=NPAIR)
        inv = take(NH * 192).bitcast(f16).rearrange("p (h c) -> p h c", h=NH)
        cme = take(8).rearrange("p (j m) -> p j m", m=2)
        cend = take(W).rearrange("p (j c) -> p j c", j=NPAIR)
        state = [take(W) for _ in range(2)]
        stp = [take(W).rearrange("p (j c) -> p j c", j=NPAIR) for _ in range(2)]
        rhs, u0, res = kk_row, ka_row, rk_row
        u1 = res
        rhs16, res16 = take(W // 2).bitcast(f16), take(W // 2).bitcast(f16)
        yacc = catT[:, 4:8, :].rearrange("p c t -> p (c t)").rearrange("p (t c) -> p t c", t=NT)
        IA, IR, IB, IK = range(4)
        steps = [(d, t) for i in range(NT_S) for d, t in ((0, i), (1, NT_S - 1 - i))] + \
                [(d, t) for i in range(NT_P) for d, t in ((0, NT_S + i), (1, NT - 1 - i))]
        fresh = (0, 1, 2 * NT_S, 2 * NT_S + 1)

        def tok(n, q):
            return tok_ar[:, q, :] if q in (IA, IR) else tok_bk[n % 2][:, q - IB, :]

        def hcol(h):
            return slice(h * HD, (h + 1) * HD)

        def lcol(h, r, d):
            at = (h % 2) * 256 + (r ^ d) * P
            return slice(at, at + P)

        ACT_HEADS, DVE_HEADS = (0, 2, 3, 5, 7), (1, 4, 6)

        def wait_level(eng, n, l, h):
            name, heads = ("inv_act", ACT_HEADS) if h in ACT_HEADS else ("inv_dve", DVE_HEADS)
            eng.wait_ge(sem(name), (LEVELS * n + l) * len(heads) + heads.index(h) + 1)

        def levels_out(eng, n):
            wait_level(eng, n, LEVELS - 1, ACT_HEADS[-1])
            wait_level(eng, n, LEVELS - 1, DVE_HEADS[-1])

        STEPS = len(steps)

        def sp_phase4(sp):
            for dst, src in ((tri, A["c_tri"]), (midc, A["c_mid"]), (seen, A["c_seen"]), (pairm, A["c_pair"])):
                sp.dma_start(dst, src).then_inc(sem("consts4_in"), 16)
            for n, (d, t) in enumerate(steps):
                if n >= 2:
                    sp.wait_ge(sem("mid_mm"), n - 1)
                    sp.wait_ge(sem("atok_ready"), n - 1)
                    sp.wait_ge(sem("ktok_ready"), n - 1)
                sp.dma_start(sgw[n % 2], dir_dram[d, :, t].rearrange("q p c -> p q c")).then_inc(sem(f"sig_in{n % 2}"), 16)
            sp.wait_ge(sem("y_ready"), STEPS)
            for dst, src in ((sel5, A["c_sel"]), (n2_row, A["norm2_g"][0].partition_broadcast(P))):
                sp.dma_start(dst, src).then_inc(sem("sel5_in"), 16)
            sp.dma_start(wout, A["w_out"][0].rearrange("(k p) n -> p k n", p=P)).then_inc(sem("wout_in"), 16)
            sp.wait_ge(sem("wout_in"), 16)

        def pool_phase4(pool):
            own = Own(pool, sem("pool_own4"))
            nc.gpsimd.memset(ar4, 0.0).then_inc(sem("zero4"), 1)
            nc.gpsimd.memset(yacc, 0.0).then_inc(sem("zero4"), 1)
            pool.wait_ge(sem("consts4_in"), 64)

            def rows(n):
                t = steps[n][1]
                pool.wait_ge(sem(f"sig_in{n % 2}"), 16 * (n // 2 + 1))
                if n >= 2:
                    pool.wait_ge(sem("st_mm"), n - 1)
                last = own.done(nc.gpsimd.tensor_tensor(tok(n, IB), kkn[:, t, :], sgw[n % 2][:, 1, :], ALU.mult))
                if n:
                    pool.wait_ge(sem("tr_mm"), 4 * n)
                pool.wait_ge(sem("exps"), 3 * n + 2)
                own.wait(last)
                nc.gpsimd.tensor_tensor(tok(n, IB), tok(n, IB), cinv, ALU.mult).then_inc(sem("btok_ready"), 1)
                nc.gpsimd.tensor_tensor(tok(n, IR), rkv[:, 0, t, :], cin, ALU.mult).then_inc(sem("rtok_ready"), 1)
                nc.gpsimd.tensor_tensor(tok(n, IK), sgw[n % 2][:, 2, :], cinv, ALU.mult).then_inc(sem("ktok_ready"), 1)

            def together(n, q):
                for hh in range(2):
                    hp = slice(64 * hh, 64 * hh + 64)
                    nc.gpsimd.tensor_copy(arT[hp, q], ar4[hp, :, lcol(hh, int(q == IR), steps[n][0])]).then_inc(sem("arT_ready"), 1)
                    pool.wait_ge(sem("arT_ready"), 4 * n + 2 * (q == IR) + hh + 1)

            rows(0)
            for n in range(STEPS):
                pool.wait_ge(sem("chT_act"), 3 * n + 3)
                pool.wait_ge(sem("chT_dve"), 3 * n + 3)
                together(n, IA)
                together(n, IR)
                pool.wait_ge(sem("cme_ready"), n + 1)
                if n:
                    pool.wait_ge(sem("st_ready"), n)
                nc.gpsimd.tensor_tensor(cend, pairm.unsqueeze(1).to_broadcast([P, NPAIR, P]),
                                        cme[:, :, 1:2].to_broadcast([P, NPAIR, P]), ALU.mult).then_inc(sem("cend_ready"), 1)
                if n + 1 < STEPS:
                    rows(n + 1)
                if n == N0 + 1:
                    pool.wait_ge(sem("y_mean"), 1)
                    centre(nc.gpsimd, y_of(0), nrm4[:, 0:NT_S * NH]).then_inc(sem("y_centred"), 1)
                    v4, bon = v_of(0)
                    own.done(nc.gpsimd.tensor_tensor(v4, v4, bon, ALU.mult))
                if n == N0 + 3:
                    pool.wait_ge(sem("y_rstd"), 1)
                    scale_shift(nc.gpsimd, own, 0)
            pool.wait_ge(sem("y_ready"), STEPS)
            v4, bon = v_of(1)
            nc.gpsimd.tensor_tensor(v4, v4, bon, ALU.mult).then_inc(sem("v_bonus"), 1)
            pool.wait_ge(sem("row5_ready"), 12)
            pool.wait_ge(sem("sel5_in"), 32)
            for g in range(2):
                nc.gpsimd.tensor_tensor(ss_row[:, g, 1, :], ss_row[:, g, 1, :], n2_row, ALU.mult)

        def tiles_of(g):
            return slice(0, NT_S) if g == 0 else slice(NT_S, NT)

        def y_of(g):
            return yacc[:, tiles_of(g), :].rearrange("p t (h c) -> p (t h) c", c=HD)

        def v_of(g):
            b = bonus[:, tiles_of(g), :].rearrange("p t h -> p (t h)")
            return (rkv[:, 2, tiles_of(g), :].rearrange("p t (h c) -> p (t h) c", c=HD),
                    b.unsqueeze(2).to_broadcast([P, b.shape[1], HD]))

        def nrm_of(g):
            return nrm4[:, 0:NT_S * NH] if g == 0 else nrm4[:, NT_S * NH:NT * NH]

        def centre(eng, y4, nrm):
            return eng.tensor_tensor(y4, y4, nrm.unsqueeze(2).to_broadcast(list(y4.shape)), ALU.subtract)

        def scale_shift(eng, own, g):
            ts, y4 = tiles_of(g), y_of(g)
            nt = ts.stop - ts.start
            own.link(eng.tensor_tensor(y4, y4, nrm_of(g).unsqueeze(2).to_broadcast(list(y4.shape)), ALU.mult))
            own.link(eng.tensor_tensor(yacc[:, ts], yacc[:, ts], lg_row.unsqueeze(1).to_broadcast([P, nt, W]), ALU.mult))
            own.link(eng.tensor_tensor(yacc[:, ts], yacc[:, ts], lb_row.unsqueeze(1).to_broadcast([P, nt, W]), ALU.add))
            own.link(eng.tensor_tensor(yacc[:, ts], yacc[:, ts], rkv[:, 2, ts], ALU.add))
            eng.tensor_tensor(gate[:, ts], gate[:, ts], yacc[:, ts], ALU.mult).then_inc(sem("rec_tok"), 1)

        def act_phase4(act):
            def u0_out(n):
                act.wait_ge(sem("u0_mm"), n + 1)
                nc.scalar.copy(u0, bank[1]).then_inc(sem("u0_ready"), 1)

            def decays(n, part):
                if part == 0:
                    act.wait_ge(sem("cum_mm"), n + 1)
                    if n:
                        for name in ("rtok_ready", "btok_ready", "ktok_ready", "cend_ready", "stp_ready"):
                            act.wait_ge(sem(name), n)
                    nc.scalar.activation(cinv, bank[1], ACT.Exp, scale=DECAY).then_inc(sem("exps"), 1)
                elif part == 1:
                    nc.scalar.activation(cin, bank[1], ACT.Exp, scale=-DECAY).then_inc(sem("exps"), 1)
                elif part == 2:
                    act.wait_ge(sem("cex_ready"), n + 1)
                    nc.scalar.activation(sgw[n % 2][:, 0, :], sgw[n % 2][:, 0, :], ACT.Exp, scale=-DECAY).then_inc(sem("exps"), 1)
                elif part == 3:
                    act.wait_ge(sem("mid_mm"), n + 1)
                    nc.scalar.activation(cme, bank[3][:, 0:8].rearrange("p (j m) -> p j m", m=2), ACT.Exp, scale=-DECAY).then_inc(sem("cme_ready"), 1)

            for part in range(4):
                decays(0, part)
            for n, (d, t) in enumerate(steps):
                act.wait_ge(sem("tr_mm"), 4 * n + 1)
                nc.scalar.copy(bkT[:, 0], bank[4 + IB].rearrange("p (j c) -> p j c", j=NPAIR)).then_inc(sem("chT_act"), 1)
                if n:
                    u0_out(n - 1)
                else:
                    act.wait_ge(sem("zero4"), 1)
                for q, j in ((IR, 2), (IA, 4)):
                    act.wait_ge(sem("tr_mm"), 4 * n + j)
                    nc.scalar.copy(ar4[0:64, :, lcol(0, int(q == IR), d)],
                                   bank[4 + q][0:64, :].rearrange("p (j c) -> p j c", j=NPAIR)).then_inc(sem("chT_act"), 1)
                for j in range(NPAIR):
                    act.wait_ge(sem("L_ready"), 8 * n + 2 * j + 1)
                    nc.scalar.copy(inv[:, 2 * j:2 * j + 2, 0:P], Lb[:, 2 * j:2 * j + 2, 1, :]).then_inc(sem("Nt_ready"), 1)
                act.wait_ge(sem("rhs_mm"), n + 1)
                nc.scalar.copy(rhs, bank[0]).then_inc(sem("rhs_ready"), 1)
                for l in range(LEVELS):
                    if n + 1 < STEPS and l < 4:
                        decays(n + 1, l)
                    for h in ACT_HEADS:
                        act.wait_ge(sem("inv_mm"), NH * (LEVELS * n + l) + h + 1)
                        if l < LEVELS - 1:
                            ins = nc.scalar.copy(inv[:, h, :], bank[4 + h % 4][:, 0:3 * P])
                        else:
                            ins = nc.scalar.copy(inv[:, h, P:2 * P], bank[4 + h % 4][:, P:2 * P])
                        ins.then_inc(sem("inv_act"), 1)
                    if n == N0 + 2 and l < NT_S:
                        act.wait_ge(sem("y_centred"), 1)
                        nc.scalar.activation(rkv[:, 0, l], yacc[:, l], ACT.Square).then_inc(sem("y_squared"), 1)
                    if n == N0 + 3 and l == 4:
                        act.wait_ge(sem("y_var"), NT_S)
                        nc.scalar.activation(nrm_of(0), nrm_of(0), ACT.Sqrt, scale=1.0 / HD, bias=eps[:, 1:2]).then_inc(sem("y_root"), 1)
            u0_out(STEPS - 1)
            n = 0
            for m, to, which in MODS[:3]:
                for g in range(2):
                    for hf in range(2):
                        if n == 4:
                            act.wait_ge(sem("y_centred"), 2)
                            nc.scalar.activation(rkv[:, 0, NT_S:], yacc[:, NT_S:], ACT.Square).then_inc(sem("y_squared"), 1)
                        if n == 8:
                            act.wait_ge(sem("y_var"), NT_S + 1)
                            nc.scalar.activation(nrm_of(1), nrm_of(1), ACT.Sqrt, scale=1.0 / HD, bias=eps[:, 1:2]).then_inc(sem("y_root"), 1)
                        act.wait_ge(sem("row5_mm"), n + 1)
                        cols = slice(hf * 512, hf * 512 + 512)
                        nc.scalar.activation(to[:, g, cols] if which is None else to[:, g, which, cols], bank[6 + n % 2], ACT.Copy,
                                             bias=1.0 if which == 1 else 0.0).then_inc(sem("row5_ready"), 1)
                        n += 1
            for t in range(0, NT, 2):
                act.wait_ge(sem("rec_tok"), 2)
                act.wait_ge(sem("rec_tr"), t + 1)
                nc.scalar.copy(catT[:, 4:8, t * P:(t + 1) * P], bank[t].rearrange("p (j c) -> p j c", j=NPAIR))

        def dve_phase4(dve):
            own = Own(dve, sem("dve_own4"))
            dve.wait_ge(sem("zero4"), 2)
            dve.wait_ge(sem("consts4_in"), 64)

            def residual(n):
                dve.wait_ge(sem("u0_ready"), n + 1)
                own.link(nc.vector.tensor_tensor(res, rhs, u0, ALU.subtract))
                own.done(nc.vector.tensor_scalar(res, res, U_SCALE, None, ALU.mult))

            def residual16(n):
                own.wait(own.n)
                dve.wait_ge(sem("nu_mm"), n + 1)
                nc.vector.scalar_tensor_tensor(res16, bank[0], U_SCALE, res, ALU.mult, ALU.add).then_inc(sem("res16_ready"), 1)

            def solution(n):
                dve.wait_ge(sem("du_mm"), n + 1)
                nc.vector.scalar_tensor_tensor(u1, bank[1], 1.0 / U_SCALE, u0, ALU.mult, ALU.add).then_inc(sem("u1_ready"), 1)

            def advance(n):
                d, t = steps[n]
                dve.wait_ge(sem("st_mm"), n + 1)
                own.link(nc.vector.tensor_tensor(state[d], bank[3], stp[n % 2].rearrange("p j c -> p (j c)"), ALU.add))
                dve.wait_ge(sem("cend_ready"), n + 1)
                s3 = state[d].rearrange("p (j c) -> p j c", j=NPAIR)
                nc.vector.tensor_tensor(s3, s3, cend, ALU.mult).then_inc(sem("st_ready"), 1)
                dve.wait_ge(sem("y_mm"), n + 1)
                nc.vector.tensor_tensor(yacc[:, t, :], bank[2], yacc[:, t, :], ALU.add).then_inc(sem("y_ready"), 1)

            def without(n):
                dve.wait_ge(sem(f"sig_in{n % 2}"), 16 * (n // 2 + 1))
                dve.wait_ge(sem("mid_mm"), n + 1)
                dve.wait_ge(sem("exps"), 3 * n + 2)
                nc.vector.tensor_tensor(sgw[n % 2][:, 0, :], bank[1], sgw[n % 2][:, 0, :], ALU.subtract).then_inc(sem("cex_ready"), 1)

            def a_row(n):
                dve.wait_ge(sem("exps"), 3 * n + 3)
                if n:
                    dve.wait_ge(sem("tr_mm"), 4 * n)
                nc.vector.scalar_tensor_tensor(tok(n, IA), kkn[:, steps[n][1], :], -1.0, sgw[n % 2][:, 0, :], ALU.mult, ALU.mult).then_inc(sem("atok_ready"), 1)

            without(0)
            a_row(0)
            for n, (d, t) in enumerate(steps):
                if n in fresh:
                    own.wait(own.done(nc.vector.memset(state[d], 0.0)))
                dve.wait_ge(sem("cme_ready"), n + 1)
                s3 = state[d].rearrange("p (j c) -> p j c", j=NPAIR)
                nc.vector.tensor_tensor(stp[n % 2], s3, cme[:, :, 0:1].to_broadcast([P, NPAIR, P]), ALU.mult).then_inc(sem("stp_ready"), 1)
                for q, j in ((IR, 2), (IK, 3), (IA, 4)):
                    dve.wait_ge(sem("tr_mm"), 4 * n + j)
                    src = bank[4 + q].rearrange("p (j c) -> p j c", j=NPAIR)
                    if q == IK:
                        ins = nc.vector.tensor_copy(bkT[:, 1], src)
                    else:
                        ins = nc.vector.tensor_copy(ar4[64:128, :, lcol(1, int(q == IR), d)], src[64:128])
                    ins.then_inc(sem("chT_dve"), 1)
                    if n and q == IK:
                        residual(n - 1)
                if n:
                    residual16(n - 1)
                for j in range(NPAIR):
                    for k, L in ((0, Lb[:, 2 * j:2 * j + 2, 1 - d:3 - d, :].rearrange("p h r c -> p h (r c)")),
                                 (1, Lk[:, j, :].rearrange("p (h c) -> p h c", h=2))):
                        dve.wait_ge(sem("L_mm"), 8 * n + 2 * j + k + 1)
                        nc.vector.scalar_tensor_tensor(L, bank[4 + 2 * (j % 2) + k].rearrange("p (h c) -> p h c", h=2), BIG,
                                                       seen[:, d, :].rearrange("p (h c) -> p h c", h=2), ALU.min, ALU.mult).then_inc(sem("L_ready"), 1)
                    if n and j == 0:
                        solution(n - 1)
                    if n and j == 2:
                        advance(n - 1)
                dve.wait_ge(sem("N_mm"), n + 1)
                nc.vector.tensor_copy(inv[:, :, 2 * P:3 * P], bank[4].bitcast(f16).rearrange("p (h c) -> p h c", h=NH)).then_inc(sem("N_ready"), 1)
                for l in range(LEVELS):
                    if n + 1 < STEPS and l == 2:
                        without(n + 1)
                    if n + 1 < STEPS and l == 4:
                        a_row(n + 1)
                    if l == 6:
                        dve.wait_ge(sem("rhs_ready"), n + 1)
                        nc.vector.tensor_copy(rhs16, rhs).then_inc(sem("rhs16_ready"), 1)
                    for h in DVE_HEADS:
                        dve.wait_ge(sem("inv_mm"), NH * (LEVELS * n + l) + h + 1)
                        if l < LEVELS - 1:
                            ins = nc.vector.tensor_copy(inv[:, h, :], bank[4 + h % 4][:, 0:3 * P])
                        else:
                            ins = nc.vector.tensor_copy(inv[:, h, P:2 * P], bank[4 + h % 4][:, P:2 * P])
                        ins.then_inc(sem("inv_dve"), 1)
                    if n == N0 + 1 and l < NT_S:
                        own.done(nc.vector.reduce_sum(nrm4[:, l * NH:(l + 1) * NH], yacc[:, l].rearrange("p (h c) -> p h c", c=HD), AX))
                    if n == N0 + 1 and l == NT_S:
                        own.wait(own.n)
                        nc.vector.tensor_scalar(nrm_of(0), nrm_of(0), 1.0 / HD, None, ALU.mult).then_inc(sem("y_mean"), 1)
                    if n == N0 + 3 and l < NT_S:
                        dve.wait_ge(sem("y_squared"), l + 1)
                        nc.vector.reduce_sum(nrm4[:, l * NH:(l + 1) * NH], rkv[:, 0, l].rearrange("p (h c) -> p h c", c=HD), AX).then_inc(sem("y_var"), 1)
                    if n == N0 + 3 and l == LEVELS - 1:
                        dve.wait_ge(sem("y_root"), 1)
                        nc.vector.reciprocal(nrm_of(0), nrm_of(0)).then_inc(sem("y_rstd"), 1)
            n = len(steps) - 1
            residual(n)
            residual16(n)
            solution(n)
            advance(n)
            dve.wait_ge(sem("y_ready"), STEPS)
            own.link(nc.vector.reduce_sum(nrm_of(1), y_of(1), AX))
            own.link(nc.vector.tensor_scalar(nrm_of(1), nrm_of(1), 1.0 / HD, None, ALU.mult))
            centre(nc.vector, y_of(1), nrm_of(1)).then_inc(sem("y_centred"), 1)
            dve.wait_ge(sem("y_squared"), NT_S + 1)
            nc.vector.reduce_sum(nrm_of(1), rkv[:, 0, NT_S:].rearrange("p t (h c) -> p (t h) c", c=HD), AX).then_inc(sem("y_var"), 1)
            dve.wait_ge(sem("y_root"), 2)
            own.link(nc.vector.reciprocal(nrm_of(1), nrm_of(1)))
            dve.wait_ge(sem("v_bonus"), 1)
            scale_shift(nc.vector, own, 1)
            for t in range(1, NT, 2):
                dve.wait_ge(sem("rec_tok"), 2)
                dve.wait_ge(sem("rec_tr"), t + 1)
                nc.vector.tensor_copy(catT[:, 4:8, t * P:(t + 1) * P], bank[t].rearrange("p (j c) -> p j c", j=NPAIR))

        nrm4 = take(NT * NH)
        N0 = 2 * NT_S

        def pe_phase4(pe):
            pe.wait_ge(sem("consts4_in"), 64)

            def mm(out, lhsT, r, start=False):
                return nc.tensor.matmul(out, lhsT, r, start=start, stop=True, skip_group_check=True)

            def first_solution(n):
                pe.wait_ge(sem("rhs16_ready"), n + 1)
                levels_out(pe, n)
                if n + 1 < STEPS:
                    pe.wait_ge(sem("cex_ready"), n + 2)
                    pe.wait_ge(sem("exps"), 3 * n + 5)
                for h in range(NH):
                    ins = mm(bank[1][:, hcol(h)], inv[:, h, P:2 * P], rhs16[:, hcol(h)], h == 0)
                ins.then_inc(sem("u0_mm"), 1)

            def times_n(n):
                pe.wait_ge(sem("u0_ready"), n + 1)
                for h in range(NH):
                    ins = mm(bank[0][:, hcol(h)], Lb[:, h, 1, :], u0[:, hcol(h)], h == 0)
                ins.then_inc(sem("nu_mm"), 1)

            def correction(n):
                pe.wait_ge(sem("res16_ready"), n + 1)
                for h in range(NH):
                    ins = mm(bank[1][:, hcol(h)], inv[:, h, P:2 * P], res16[:, hcol(h)], h == 0)
                ins.then_inc(sem("du_mm"), 1)

            def advance(n):
                v = rkv[:, 2, steps[n][1], :]
                pe.wait_ge(sem("u1_ready"), n + 1)
                if n + 1 < STEPS:
                    pe.wait_ge(sem("cme_ready"), n + 2)
                if n:
                    pe.wait_ge(sem("st_ready"), n)
                for j in range(NPAIR):
                    mm(bank[3][:, j * P:(j + 1) * P], tok(n, IB)[:, j * P:(j + 1) * P], u1[:, j * P:(j + 1) * P], j == 0)
                    ins = mm(bank[3][:, j * P:(j + 1) * P], tok(n, IK)[:, j * P:(j + 1) * P], v[:, j * P:(j + 1) * P])
                ins.then_inc(sem("st_mm"), 1)
                for h in range(NH):
                    ins = mm(bank[2][:, hcol(h)], Lb[:, h, 2 - 2 * steps[n][0], :], u1[:, hcol(h)])
                ins.then_inc(sem("y_mm"), 1)

            def decay_sums(n):
                d = steps[n][0]
                pe.wait_ge(sem(f"sig_in{n % 2}"), 16 * (n // 2 + 1))
                if n >= 2:
                    pe.wait_ge(sem("u1_ready"), n - 1)
                    pe.wait_ge(sem("st_ready"), n - 1)
                mm(bank[1], tri[:, d, :], sgw[n % 2][:, 0, :], True).then_inc(sem("cum_mm"), 1)
                for j in range(NPAIR):
                    ins = mm(bank[3][:, 2 * j:2 * j + 2], sgw[n % 2][:, 0, j * P:(j + 1) * P], midc[:, d, :], True)
                ins.then_inc(sem("mid_mm"), 1)

            decay_sums(0)
            for n, (d, t) in enumerate(steps):
                v = rkv[:, 2, t, :]
                if n:
                    levels_out(pe, n - 1)
                for q, s in ((IB, "btok_ready"), (IR, "rtok_ready"), (IK, "ktok_ready"), (IA, "atok_ready")):
                    pe.wait_ge(sem(s), n + 1)
                    for j in range(NPAIR):
                        ins = nc.tensor.transpose(bank[4 + q][:, j * P:(j + 1) * P], tok(n, q)[:, j * P:(j + 1) * P], ident)
                    ins.then_inc(sem("tr_mm"), 1)
                    if n and q == IB:
                        first_solution(n - 1)
                if n:
                    times_n(n - 1)
                pe.wait_ge(sem("chT_act"), 3 * n + 3)
                pe.wait_ge(sem("chT_dve"), 3 * n + 3)
                for j in range(NPAIR):
                    for k in range(2):
                        if j >= 2:
                            pe.wait_ge(sem("L_ready"), 8 * n + 2 * (j - 2) + k + 1)
                        mm(bank[4 + 2 * (j % 2) + k], bkT[:, k, j, :], ar4[:, j, :], True).then_inc(sem("L_mm"), 1)
                    if n and j == 0:
                        correction(n - 1)
                    if n and j == 1:
                        advance(n - 1)
                pe.wait_ge(sem("stp_ready"), n + 1)
                pe.wait_ge(sem("arT_ready"), 4 * n + 2)
                for j in range(NPAIR):
                    mm(bank[0][:, j * P:(j + 1) * P], arT[:, IA, j, :], stp[n % 2][:, j, :], j == 0)
                for h in range(NH):
                    pe.wait_ge(sem("L_ready"), 8 * n + 2 * (h // 2) + 2)
                    ins = mm(bank[0][:, hcol(h)], Lk[:, h // 2, lcol(h, 0, d)], v[:, hcol(h)])
                ins.then_inc(sem("rhs_mm"), 1)
                pe.wait_ge(sem("Nt_ready"), 4 * n + 4)
                b16 = bank[4].bitcast(f16)
                for h in range(NH):
                    ins = nc.tensor.transpose(b16[:, h * P:(h + 1) * P], inv[:, h, 0:P], ident16)
                ins.then_inc(sem("N_mm"), 1)
                if n + 1 < STEPS:
                    decay_sums(n + 1)
                pe.wait_ge(sem("N_ready"), n + 1)
                for l in range(LEVELS):
                    for h in range(NH):
                        if h >= 4:
                            wait_level(pe, n, l, h - 4)
                        if l:
                            wait_level(pe, n, l - 1, h)
                            if h < 4:
                                wait_level(pe, n, l - 1, h + 4)
                        b = bank[4 + h % 4]
                        nt, x, m = inv[:, h, 0:P], inv[:, h, P:2 * P], inv[:, h, 2 * P:3 * P]
                        if l == 0:
                            mm(b[:, 0:P], m, nt, True)
                            mm(b[:, P:2 * P], m, ident16)
                            mm(b[:, P:2 * P], ident16, ident16)
                            ins = mm(b[:, 2 * P:3 * P], nt, m)
                        elif l < LEVELS - 1:
                            mm(b[:, 0:2 * P], m, inv[:, h, 0:2 * P], True)
                            mm(b[:, P:2 * P], ident16, x)
                            ins = mm(b[:, 2 * P:3 * P], nt, m)
                        else:
                            mm(b[:, P:2 * P], m, x, True)
                            ins = mm(b[:, P:2 * P], ident16, x)
                        ins.then_inc(sem("inv_mm"), 1)
                    if l == 0:
                        pe.wait_ge(sem("arT_ready"), 4 * n + 4)
                    if l == 0 and n:
                        pe.wait_ge(sem("y_ready"), n)
                    for j in (range(2 * l, 2 * l + 2) if l < 2 else ()):
                        mm(bank[2][:, j * P:(j + 1) * P], arT[:, IR, j, :], stp[n % 2][:, j, :], j == 0)
                    for h in (range(2 * l - 4, 2 * l - 2) if 2 <= l < 6 else ()):
                        mm(bank[2][:, hcol(h)], Lk[:, h // 2, lcol(h, 1, d)], v[:, hcol(h)])
            n = len(steps) - 1
            first_solution(n)
            times_n(n)
            correction(n)
            advance(n)
            pe.wait_ge(sem("sel5_in"), 32)
            n = 0
            for m, _, _ in MODS[:3]:
                for g in range(2):
                    for hf in range(2):
                        if n >= 2:
                            pe.wait_ge(sem("row5_ready"), n - 1)
                        mm(bank[6 + n % 2], sel5[:, g, :], modp[:, (2 * m + hf) * 512:(2 * m + hf + 1) * 512], True).then_inc(sem("row5_mm"), 1)
                        n += 1
            pe.wait_ge(sem("y_ready"), STEPS)
            for t in range(NT):
                pe.wait_ge(sem("rec_tok"), 1 if t < NT_S else 2)
                for j in range(NPAIR):
                    ins = nc.tensor.transpose(bank[t][:, j * P:(j + 1) * P], gate[:, t, j * P:(j + 1) * P], ident)
                ins.then_inc(sem("rec_tr"), 1)

        top[0] = base5
        x2 = take(NT * D).rearrange("p (t d) -> p t d", t=NT)
        g2_row = take(2 * D).rearrange("p (g d) -> p g d", g=2)
        wts = take(NT * 2).rearrange("p (t k) -> p t k", k=2)
        pos_i = take(NT * 2).bitcast(i32).rearrange("p (t k) -> p t k", k=2)
        base6 = top[0]
        NSLOT = 3
        WEXP = 2 * KD * HID + KH * D
        w1_s, w3_s, w2_s = [], [], []
        for at in (ARENA - WEXP, ARENA - 2 * WEXP, P + 2):
            top[0] = at
            w2_s.append(take(KH * D).rearrange("p (k n) -> p k n", k=KH))
            w1_s.append(take(KD * HID).rearrange("p (k n) -> p k n", k=KD))
            w3_s.append(take(KD * HID).rearrange("p (k n) -> p k n", k=KD))
        assert top[0] == base5
        w1_v = A["exp_w1"][0].rearrange("e (k p) n -> e p k n", p=P)
        w3_v = A["exp_w3"][0].rearrange("e (k p) n -> e p k n", p=P)
        w2_v = A["exp_w2"][0].rearrange("e (k p) n -> e p k n", p=P)

        def one(ap, e):
            return ap[bass.ds(e, 1)].rearrange("o p k n -> p (o k) n")

        top[0] = ARENA - 2 * WEXP + KH * D
        wout = take(KD * D).rearrange("p (k n) -> p k n", k=KD)
        assert top[0] <= ARENA - WEXP
        top[0] = ARENA - 2 * WEXP + KH * D - 2 * D
        assert top[0] >= base4
        g1_row = take(2 * D).rearrange("p (g d) -> p g d", g=2)
        top[0] = ARENA - WEXP
        ss_row = take(4 * D).rearrange("p (g m d) -> p g m d", g=2, m=2)
        assert top[0] <= ARENA - WEXP + KH * D
        n2_row = take(D)
        sel5 = take(3 * P).rearrange("p (g c) -> p g c", g=3)
        top[0] = base6
        h2T = [take(D).rearrange("p (k c) -> p k c", k=KD) for _ in range(2)]
        sq5 = take(D)
        zero = take(512)
        before, ones = take(P), take(P)
        sel5g = take(2 * P).rearrange("p (g c) -> p g c", g=2)
        h2 = [take(D) for _ in range(2)]
        rw = take(KD * 36).rearrange("p (k e) -> p k e", k=KD)
        rb = take(36)
        stat5 = take(NT * 4).rearrange("p (t m) -> p t m", t=NT)
        logit = take(NT * 36).rearrange("p (t e) -> p t e", t=NT)
        expert_row, first_row, fall_row, place = take(NE), take(NE), take(8), take(1)
        token_i = take(NT).bitcast(i32)
        gm, gsum, m1, m2, pk = (take(NT) for _ in range(5))
        og, tg = (take(NT * NG).rearrange("p (t g) -> p t g", g=NG) for _ in range(2))
        s8, t8, o1, o2 = (take(NT * 8).rearrange("p (t e) -> p t e", e=8) for _ in range(4))
        e1, e2, both, slot_f, lsel = (take(NT * NE).rearrange("p (t e) -> p t e", e=NE) for _ in range(5))
        tilebase = take((NT + 1) * NE).rearrange("p (t e) -> p t e", e=NE)
        over, incl, incl2, o32, excl = (take(NE) for _ in range(5))
        lst = take(2)
        lst_i = take(2).bitcast(i32)
        assert top[0] <= ARENA - 2 * WEXP + KH * D - 2 * D, top[0]

        def sp_phase5(sp):
            sp.wait_ge(sem("zero5"), 1)
            sp.dma_start(slot_dram.rearrange("(p n) o -> p (n o)", p=P), zero.bitcast(i32)[:, 0:NBLK * BLK // P]).then_inc(sem("slots_zero"), 16)
            for dst, src in ((sel5g, A["c_sel"][:, 0:2, :]), (before, A["c_before"]),
                             (ones, A["c_ones"]), (rw, A["router_w"]), (rb, A["router_b"].partition_broadcast(P)),
                             (expert_row, A["c_expert"]), (first_row, A["c_first"]), (fall_row, A["c_fall8"]),
                             (place, A["c_place"]), (token_i, A["c_token"])):
                sp.dma_start(dst, src).then_inc(sem("consts5_in"), 16)
            for t in range(NT):
                sp.dma_start(x2[:, t, :], x_tile[t]).then_inc(sem("x5_in"), 16)
            unused = y_dram[NE * BLK:, :].rearrange("(p s) (j n) -> p (s j) n", p=P, n=512)
            sp.dma_start(unused, zero.unsqueeze(1).to_broadcast([P, MAX_OVER * BLK // P * 2, 512])).then_inc(sem("unused_zero"), 16)
            for slot, view in ((w1_s, w1_v), (w3_s, w3_v)):
                sp.dma_start(slot[0], view[0]).then_inc(sem("weights_in"), 16)
            for t in range(NT):
                sp.wait_ge(sem("h2_ready"), t + 1)
                sp.dma_start(h2_dram[t * P:(t + 1) * P, :], h2[t % 2]).then_inc(sem(f"h2_out{t % 2}"), 16)
            sp.wait_ge(sem("o5_mm"), 2 * NT)
            sp.wait_ge(sem("g2_mm"), 4)
            for k in (1, 2):
                for slot, view in ((w1_s, w1_v), (w3_s, w3_v)):
                    sp.dma_start(slot[k], view[k]).then_inc(sem("weights_in"), 16)
            sp.dma_start(w2_s[2], w2_v[2]).then_inc(sem("weights_in"), 16)
            sp.wait_ge(sem("list_ready"), 1)
            sp.dma_start(over_dram, lst_i[0:MAX_OVER, :]).then_inc(sem("list_out"), 16)
            sp.wait_ge(sem("weights_in"), 16 * 7)
            sp.wait_ge(sem("list_out"), 16)
            sp.wait_ge(sem("unused_zero"), 16)
            sp.wait_ge(sem("h2_out0"), 48)
            sp.wait_ge(sem("h2_out1"), 48)

        def pool_phase5(pool):
            nc.gpsimd.memset(zero, 0.0).then_inc(sem("zero5"), 1)
            pool.wait_ge(sem("slots_zero"), 16)
            pool.wait_ge(sem("consts5_in"), 16 * 10)
            pool.wait_ge(sem("pos_ready"), 1)
            for t in range(NT):
                for k in range(2):
                    nc.gpsimd.indirect_dma_start(slot_dram, bass.IndirectOffsetOnAxis(ap=pos_i.bitcast(u32)[:, t, k:k + 1], axis=0),
                                                 token_i[:, t:t + 1], None).then_inc(sem("slot_out"), 16)
            pool.wait_ge(sem("slot_out"), 16 * 2 * NT)

        def act_phase5(act):
            own = Own(act, sem("act_own5"))
            for t in range(NT):
                act.wait_ge(sem("x2_ready"), t + 1)
                if t:
                    own.wait(own.n)
                own.link(nc.scalar.activation(sq5, x2[:, t, :], ACT.Square, scale=1.0 / 32.0, accum_out=stat5[:, t, 0:1]))
                own.done(nc.scalar.activation(stat5[:, t, 1:2], stat5[:, t, 0:1], ACT.Sqrt, bias=eps[:, 0:1]))
                if t:
                    h2T_evac(act, t - 1)
            h2T_evac(act, NT - 1)
            act.wait_ge(sem("g_centred"), 1)
            nc.scalar.activation(tg, tg, ACT.Exp).then_inc(sem("g_exp"), 1)
            act.wait_ge(sem("m_diff"), 1)
            nc.scalar.activation(m2, m2, ACT.Exp).then_inc(sem("m_exp"), 1)

        def h2T_evac(act, t):
            for hf in range(2):
                act.wait_ge(sem("h2T_mm"), 2 * t + hf + 1)
                if t >= 2:
                    act.wait_ge(sem("router_mm"), t - 1)
                nc.scalar.copy(h2T[t % 2][:, 4 * hf:4 * hf + 4, :], bank[6 + hf].rearrange("p (k c) -> p k c", k=4)).then_inc(sem("h2T_ready"), 1)

        MODS = [(2, g1_row, None), (3, ss_row, 0), (4, ss_row, 1), (5, g2_row, None)]

        def dve_phase5(dve):
            own = Own(dve, sem("dve_own5"))
            dve.wait_ge(sem("consts5_in"), 16 * 10)
            dve.wait_ge(sem("x5_in"), 16 * NT)

            def residual(t):
                tmp = h2[t % 2]
                if t >= 2:
                    dve.wait_ge(sem(f"h2_out{t % 2}"), 16 * (t // 2))
                    dve.wait_ge(sem("h2T_mm"), 2 * (t - 1))
                for hf in range(2):
                    cols = slice(hf * 512, hf * 512 + 512)
                    dve.wait_ge(sem("o5_mm"), 2 * t + hf + 1)
                    k = own.done(nc.vector.tensor_tensor(tmp[:, cols], bank[2 + 2 * (t % 2) + hf], g1_row[:, group(t), cols], ALU.mult))
                own.wait(k)
                nc.vector.tensor_tensor(x2[:, t, :], x2[:, t, :], tmp, ALU.add).then_inc(sem("x2_ready"), 1)

            def norm(t):
                dve.wait_ge(sem("act_own5"), 2 * t + 2)
                own.link(nc.vector.reciprocal(stat5[:, t, 2:3], stat5[:, t, 1:2]))
                own.link(nc.vector.scalar_tensor_tensor(h2[t % 2], x2[:, t, :], stat5[:, t, 2:3], ss_row[:, group(t), 1, :], ALU.mult, ALU.mult))
                nc.vector.tensor_tensor(h2[t % 2], h2[t % 2], ss_row[:, group(t), 0, :], ALU.add).then_inc(sem("h2_ready"), 1)

            def scores(t):
                dve.wait_ge(sem("router_mm"), t + 1)
                nc.vector.tensor_tensor(logit[:, t, :], bank[t % 2][:, 0:36], rb, ALU.add).then_inc(sem("logit_ready"), 1)

            residual(0)
            for t in range(NT):
                if t + 1 < NT:
                    residual(t + 1)
                norm(t)
                if t:
                    scores(t - 1)
            scores(NT - 1)
            for n in range(4):
                dve.wait_ge(sem("g2_mm"), n + 1)
                nc.vector.tensor_copy(g2_row[:, n // 2, (n % 2) * 512:(n % 2) * 512 + 512], bank[4 + n])
            dve.wait_ge(sem("logit_ready"), NT)

            def b(ap, shape):
                return ap.unsqueeze(len(ap.shape)).to_broadcast(shape)

            def first_max(one_hot, top_v, values, tmp, width):
                shape = [P, NT, width]
                own.link(nc.vector.tensor_reduce(top_v, values, AX, ALU.max))
                own.link(nc.vector.tensor_tensor(tmp, values, b(top_v, shape), ALU.is_equal))
                own.link(nc.vector.tensor_tensor(tmp, tmp, fall_row[:, 0:width].unsqueeze(1).to_broadcast(shape), ALU.mult))
                own.link(nc.vector.tensor_reduce(pk, tmp, AX, ALU.max))
                own.link(nc.vector.tensor_tensor(one_hot, tmp, b(pk, shape), ALU.is_equal))

            pg = logit[:, :, 0:NG]
            first_max(og, gm, pg, tg, NG)
            nc.vector.tensor_tensor(tg, pg, b(gm, [P, NT, NG]), ALU.subtract).then_inc(sem("g_centred"), 1)
            le = logit[:, :, NG:].rearrange("p t (g e) -> p t g e", g=NG)
            own.link(nc.vector.tensor_tensor(lsel.rearrange("p t (g e) -> p t g e", g=NG), le, b(og, [P, NT, NG, EPG]), ALU.mult))
            own.link(nc.vector.tensor_reduce(s8, lsel.rearrange("p t (g e) -> p t e g", g=NG), AX, ALU.add))
            first_max(o1, m1, s8, t8, EPG)
            own.link(nc.vector.scalar_tensor_tensor(s8, o1, -1e30, s8, ALU.mult, ALU.add))
            first_max(o2, m2, s8, t8, EPG)
            own.link(nc.vector.tensor_tensor(m2, m2, m1, ALU.subtract))
            dve.wait_ge(sem("g_exp"), 1)
            nc.vector.tensor_reduce(gsum, tg, AX, ALU.add).then_inc(sem("m_diff"), 1)
            dve.wait_ge(sem("m_exp"), 1)
            own.link(nc.vector.tensor_scalar(m1, m2, 1.0, None, ALU.add))
            own.link(nc.vector.tensor_tensor(m1, m1, gsum, ALU.mult))
            own.link(nc.vector.reciprocal(wts[:, :, 0], m1))
            own.link(nc.vector.tensor_tensor(wts[:, :, 1], wts[:, :, 0], m2, ALU.mult))
            for one, o8 in ((e1, o1), (e2, o2)):
                own.link(nc.vector.tensor_tensor(one.rearrange("p t (g e) -> p t g e", g=NG), b(og, [P, NT, NG, EPG]),
                                                 o8.unsqueeze(2).to_broadcast([P, NT, NG, EPG]), ALU.mult))
            nc.vector.tensor_tensor(both, e1, e2, ALU.add).then_inc(sem("hits_ready"), 1)
            own.link(nc.vector.memset(tilebase[:, 0, :], 0.0))
            dve.wait_ge(sem("rank_mm"), 2)
            tot = bank[3][:, 0:NT * NE].rearrange("p (t e) -> p t e", e=NE)
            for t in range(NT):
                own.link(nc.vector.tensor_tensor(tilebase[:, t + 1, :], tot[:, t, :], tilebase[:, t, :], ALU.add))
            cnt = tilebase[:, NT, :]
            own.link(nc.vector.tensor_scalar(over, cnt, float(BLK), None, ALU.is_gt))
            for k in range(2, TOK // BLK):
                own.link(nc.vector.scalar_tensor_tensor(over, cnt, float(BLK * k), over, ALU.is_gt, ALU.add))
            own.link(nc.vector.tensor_copy(incl, over))
            a, c = incl, incl2
            for s in (1, 2, 4, 8, 16):
                own.done(nc.vector.tensor_copy(c[:, 0:s], a[:, 0:s]))
                own.link(nc.vector.tensor_tensor(c[:, s:NE], a[:, s:NE], a[:, 0:NE - s], ALU.add))
                a, c = c, a
            own.link(nc.vector.tensor_tensor(excl, a, over, ALU.subtract))
            own.link(nc.vector.tensor_scalar(over, excl, float(NE - 1), float(BLK), ALU.add, ALU.mult))
            own.link(nc.vector.tensor_tensor(over, over, first_row, ALU.subtract))
            own.link(nc.vector.tensor_tensor(slot_f, bank[2][:, 0:NT * NE].rearrange("p (t e) -> p t e", e=NE), tilebase[:, 0:NT, :], ALU.add))
            own.link(nc.vector.scalar_tensor_tensor(lsel, slot_f, float(BLK), over.unsqueeze(1).to_broadcast([P, NT, NE]), ALU.is_ge, ALU.mult))
            own.link(nc.vector.tensor_tensor(slot_f, slot_f, lsel, ALU.add))
            own.link(nc.vector.tensor_tensor(slot_f, slot_f, first_row.unsqueeze(1).to_broadcast([P, NT, NE]), ALU.add))
            for k, one in enumerate((e1, e2)):
                own.link(nc.vector.tensor_tensor(one, one, slot_f, ALU.mult))
                own.link(nc.vector.tensor_reduce(pk, one, AX, ALU.add))
                ins = nc.vector.tensor_copy(pos_i[:, :, k], pk)
                if k == 0:
                    own.link(ins)
            ins.then_inc(sem("pos_ready"), 1)
            own.link(nc.vector.tensor_scalar(o32, a, place, None, ALU.is_gt))
            own.link(nc.vector.scalar_tensor_tensor(o32, excl, place, o32, ALU.is_le, ALU.mult))
            own.link(nc.vector.tensor_tensor(o32, o32, expert_row, ALU.mult))
            own.link(nc.vector.tensor_reduce(lst[:, 0:1], o32, AX, ALU.add))
            own.link(nc.vector.tensor_copy(lst[:, 1:2], a[:, NE - 1:NE]))
            nc.vector.tensor_copy(lst_i, lst).then_inc(sem("list_ready"), 1)

        def pe_phase5(pe):
            for t in range(NT + 2):
                if t < NT:
                    if t >= 2:
                        pe.wait_ge(sem("x2_ready"), t - 1)
                    for hf in range(2):
                        for k in range(KD):
                            ins = nc.tensor.matmul(bank[2 + 2 * (t % 2) + hf], catT[:, k, t * P:(t + 1) * P], wout[:, k, hf * 512:hf * 512 + 512],
                                                   start=(k == 0), stop=(k == KD - 1))
                        ins.then_inc(sem("o5_mm"), 1)
                if t >= 2:
                    j = t - 2
                    if j == 0:
                        pe.wait_ge(sem("consts5_in"), 16 * 10)
                    pe.wait_ge(sem("h2_ready"), j + 1)
                    for hf in range(2):
                        if j:
                            pe.wait_ge(sem("h2T_ready"), 2 * (j - 1) + hf + 1)
                        for k in range(4):
                            kk = 4 * hf + k
                            ins = nc.tensor.transpose(bank[6 + hf][:, k * P:(k + 1) * P], h2[j % 2][:, kk * P:(kk + 1) * P], ident)
                        ins.then_inc(sem("h2T_mm"), 1)
                    pe.wait_ge(sem("h2T_ready"), 2 * j + 2)
                    if j >= 2:
                        pe.wait_ge(sem("logit_ready"), j - 1)
                    for k in range(KD):
                        ins = nc.tensor.matmul(bank[j % 2][:, 0:36], h2T[j % 2][:, k, :], rw[:, k, :], start=(k == 0), stop=(k == KD - 1))
                    ins.then_inc(sem("router_mm"), 1)
            pe.wait_ge(sem("x2_ready"), NT)
            pe.wait_ge(sem("h2T_ready"), 2 * NT)
            for n in range(4):
                nc.tensor.matmul(bank[4 + n], sel5g[:, n // 2, :], modp[:, (10 + n % 2) * 512:(11 + n % 2) * 512],
                                 start=True, stop=True).then_inc(sem("g2_mm"), 1)
            pe.wait_ge(sem("hits_ready"), 1)
            hits = both.rearrange("p t e -> p (t e)")
            nc.tensor.matmul(bank[2][:, 0:NT * NE], before, hits, start=True, stop=True).then_inc(sem("rank_mm"), 1)
            nc.tensor.matmul(bank[3][:, 0:NT * NE], ones, hits, start=True, stop=True).then_inc(sem("rank_mm"), 1)

        top[0] = base6
        HALF = HID // 2
        idx_o = take(1).bitcast(i32)
        LOOP = 2 * NSLOT
        idx_c = [take(1).bitcast(i32) for _ in range(LOOP)]
        xg = [take(D) for _ in range(2)]
        xT = [take(KD * BLK).rearrange("p (k c) -> p k c", k=KD) for _ in range(2)]
        sil, hid = take(HALF), take(HALF)
        hidT = take(HALF).rearrange("p (c n t) -> p c n t", c=2, n=2)
        yb = [take(HID) for _ in range(2)]
        top6 = top[0]
        assert top6 <= ARENA - 2 * WEXP
        y_v = y_dram.rearrange("s (j n) -> s j n", j=2)

        CREDIT = 3

        class Main:
            over = ""
            credit = CREDIT

            def __init__(self, e, u, n, wn, sn, qn):
                self.q, self.qn = u % LOOP, qn
                self.e, self.n, self.w, self.wn, self.s, self.sn = e, n, u % NSLOT, wn, u % 2, sn
                self.first_slot = e * BLK

            def sem(self, name):
                return sem(name)

        class Over:
            over = "over_"
            credit = 0

            def __init__(self, m, e=None):
                self.e, self.n, self.w, self.wn, self.s, self.sn = e, m, 0, m, 0, m
                self.q, self.qn = 0, m
                self.first_slot = m * BLK + NE * BLK

            def sem(self, name):
                return sem("over_" + name)

        def turns(eng, body, ahead=0, pairs=False):
            whole = (NE - ahead) // LOOP

            def block(i, u):
                return Main(i * LOOP + u, u, i * LOOP + u, i * (LOOP // NSLOT) + u // NSLOT, i * (LOOP // 2) + u // 2, i + u // LOOP)

            with eng.Fori(0, whole) as i:
                for u in range(LOOP):
                    body(block(i, u), *([block(i, u + 1)] if pairs else []))
            for u in range(NE - whole * LOOP):
                last = whole * LOOP + u == NE - 1
                body(block(whole, u), *([None if last else block(whole, u + 1)] if pairs else []))

        def overflow(eng, body, with_expert=False):
            count = eng.value_load(over_dram[0:1, 1:2], min_val=0, max_val=MAX_OVER)
            with eng.If(count > 0):
                with eng.Fori(0, count) as m:
                    e = eng.value_load(over_dram[bass.ds(m, 1), 0:1], min_val=0, max_val=NE - 1) if with_expert else None
                    body(Over(m, e))
            with eng.Else():
                pass

        WEIGHTS = (("h1_mm", w1_s, w1_v), ("h3_mm", w3_s, w3_v), ("y_mm6", w2_s, w2_v))

        def sp_phase6(sp):
            for k in range(NSLOT):
                for name in ("h1_mm", "h3_mm") + (("y_mm6",) if k == 2 else ()):
                    sp.sem_inc(sem(f"{name}_w{k}"), 16)
            for k in range(LOOP):
                sp.dma_start(idx_c[k][0:BLK, :], slot_dram[k * BLK:(k + 1) * BLK, :]).then_inc(sem(f"idx_in{k}"), 16)
            for k in range(2):
                sp.dma_start(w2_s[k], w2_v[k]).then_inc(sem(f"y_mm6_w{k}"), 16)

            def ahead(c):
                static = isinstance(c.n, int)
                if not static or c.n + LOOP < NE:
                    sp.wait_ge(sem(f"xg_in{c.s}"), 16 * c.sn + 16)
                    sp.dma_start(idx_c[c.q][0:BLK, :], slot_dram[bass.ds(c.first_slot + LOOP * BLK, BLK), :]).then_inc(sem(f"idx_in{c.q}"), 16)
                if not static or c.n + NSLOT < NE:
                    for name, slot, view in WEIGHTS:
                        sp.wait_ge(sem(name), CREDIT + c.n + 1)
                        sp.dma_start(slot[c.w], one(view, c.e + NSLOT)).then_inc(sem(f"{name}_w{c.w}"), 16)

            turns(sp, ahead, ahead=NSLOT)

            def over(c):
                sp.wait_ge(sem("over_y_out0"), 32 * c.n + 16)
                sp.dma_start(idx_o[0:BLK, :], slot_dram[bass.ds(c.first_slot, BLK), :]).then_inc(c.sem("idx_in0"), 16)
                for name, slot, view in WEIGHTS:
                    sp.dma_start(slot[0], one(view, c.e)).then_inc(c.sem(f"{name}_w0"), 16)

            sp.wait_ge(sem("y_mm6"), CREDIT + NE)
            overflow(sp, over, with_expert=True)

        def pool_phase6(pool):
            def gather(c):
                pool.wait_ge(c.sem(f"idx_in{c.q}"), 16 * c.qn + 16)
                if not c.over:
                    pool.wait_ge(sem("xT_mm"), CREDIT + c.n - 1)
                pool.sem_inc(sem("pool_turn"), 1)
                idx = idx_o if c.over else idx_c[c.q]
                nc.gpsimd.indirect_dma_start(xg[c.s][0:BLK, :], None, h2_dram,
                                             bass.IndirectOffsetOnAxis(ap=idx.bitcast(u32)[0:BLK, :], axis=0)).then_inc(c.sem(f"xg_in{c.s}"), 16)

            turns(pool, gather)
            overflow(pool, gather)

        def act_phase6(act):
            for name in ("y_out0", "y_out1", "over_y_out0"):
                act.sem_inc(sem(name), 16)
            for name in ("xT_ready", "sil_ready", "hidT_ready"):
                act.sem_inc(sem(name), CREDIT)

            def rows(c):
                k = c.credit + c.n + 1
                act.wait_ge(c.sem("xT_mm"), k)
                if not c.over:
                    act.wait_ge(sem("h3_mm"), k - 2)
                nc.scalar.copy(xT[c.s], bank[0].rearrange("p (k c) -> p k c", k=KD)).then_inc(c.sem("xT_ready"), 1)

            def body(c, after=None):
                k = c.credit + c.n + 1
                act.wait_ge(c.sem("h1_mm"), k)
                if not c.over:
                    act.wait_ge(sem("hid_ready"), k - 1)
                nc.scalar.activation(sil, bank[1 + 2 * c.s][:, 0:HALF], ACT.Silu).then_inc(c.sem("sil_ready"), 1)
                if after:
                    rows(after)
                act.wait_ge(c.sem("hidT_mm"), k)
                if not c.over:
                    act.wait_ge(sem("y_mm6"), k - 1)
                nc.scalar.copy(hidT, bank[5][:, 0:HALF].rearrange("p (c n t) -> p c n t", c=2, n=2)).then_inc(c.sem("hidT_ready"), 1)
                act.wait_ge(c.sem("y_ready6"), k)
                for j in range(2):
                    act.dma_start(y_v[bass.ds(c.first_slot, BLK), j, :], yb[c.s][j * BLK:(j + 1) * BLK, :]).then_inc(c.sem(f"y_out{c.s}"), 16)

            rows(Main(0, 0, 0, 0, 0, 0))
            turns(act, body, ahead=1, pairs=True)
            act.wait_ge(sem("y_out0"), 16 + 32 * NE // 2)
            act.wait_ge(sem("y_out1"), 16 + 32 * NE // 2)

            def over(c):
                rows(c)
                body(c)
                act.wait_ge(sem("over_y_out0"), 32 * c.n + 48)

            overflow(act, over)

        def dve_phase6(dve):
            for name in ("hid_ready", "y_ready6"):
                dve.sem_inc(sem(name), CREDIT)

            def body(c):
                k = c.credit + c.n + 1
                dve.wait_ge(c.sem("sil_ready"), k)
                dve.wait_ge(c.sem("h3_mm"), k)
                if not c.over:
                    dve.wait_ge(sem("hidT_mm"), k - 1)
                nc.vector.tensor_tensor(hid, bank[2 + 2 * c.s][:, 0:HALF], sil, ALU.mult).then_inc(c.sem("hid_ready"), 1)
                dve.wait_ge(c.sem("y_mm6"), k)
                if not c.over:
                    dve.wait_ge(sem(f"y_out{c.s}"), 32 * c.sn + 16)
                nc.vector.tensor_copy(yb[c.s], bank[6 + c.s]).then_inc(c.sem("y_ready6"), 1)

            turns(dve, body)
            overflow(dve, body)

        def pe_phase6(pe):
            for name in ("xT_mm", "h1_mm", "h3_mm", "hidT_mm", "y_mm6"):
                pe.sem_inc(sem(name), CREDIT)

            def rows(c):
                k = c.credit + c.n + 1
                pe.wait_ge(c.sem(f"xg_in{c.s}"), 16 * c.sn + 16)
                if not c.over:
                    pe.wait_ge(sem("xT_ready"), k - 1)
                pe.sem_inc(sem("pe_turn"), 1)
                for j in range(KD):
                    ins = nc.tensor.transpose(bank[0][:, j * BLK:(j + 1) * BLK], xg[c.s][0:BLK, j * P:(j + 1) * P], ident[0:BLK, 0:BLK])
                ins.then_inc(c.sem("xT_mm"), 1)

            def body(c, after=None):
                k = c.credit + c.n + 1
                pe.wait_ge(c.sem("xT_ready"), k)
                for name, slot, b, free in (("h1_mm", w1_s, 1, "sil_ready"), ("h3_mm", w3_s, 2, "hid_ready")):
                    pe.wait_ge(c.sem(f"{name}_w{c.w}"), 16 * c.wn + 16)
                    if not c.over:
                        pe.wait_ge(sem(free), k - 2)
                    for j in range(KD):
                        for n in range(2):
                            ins = nc.tensor.matmul(bank[b + 2 * c.s][BLK * n:BLK * n + BLK, 0:HALF], xT[c.s][:, j, :],
                                                   slot[c.w][:, j, n * HALF:(n + 1) * HALF], start=(j == 0), stop=(j == KD - 1))
                    ins.then_inc(c.sem(name), 1)
                if after:
                    rows(after)
                pe.wait_ge(c.sem("hid_ready"), k)
                if not c.over:
                    pe.wait_ge(sem("hidT_ready"), k - 1)
                for j in range(2):
                    ins = nc.tensor.transpose(bank[5][:, j * P:(j + 1) * P], hid[:, j * P:(j + 1) * P], ident)
                ins.then_inc(c.sem("hidT_mm"), 1)
                pe.wait_ge(c.sem("hidT_ready"), k)
                pe.wait_ge(c.sem(f"y_mm6_w{c.w}"), 16 * c.wn + 16)
                if not c.over:
                    pe.wait_ge(sem("y_ready6"), k - 2)
                for j in range(KH):
                    for n in range(2):
                        ins = nc.tensor.matmul(bank[6 + c.s][BLK * n:BLK * n + BLK, :], hidT[:, j % 2, j // 2, :],
                                               w2_s[c.w][:, j, n * 512:(n + 1) * 512], start=(j == 0), stop=(j == KH - 1))
                ins.then_inc(c.sem("y_mm6"), 1)

            def over(c):
                rows(c)
                body(c)

            rows(Main(0, 0, 0, 0, 0, 0))
            turns(pe, body, ahead=1, pairs=True)
            overflow(pe, over)

        top[0] = base6
        ya = [[take(D) for _ in range(2)] for _ in range(2)]
        sq7 = take(D)
        yo = [take(D) for _ in range(2)]
        f_row = take(D)
        stat7 = take(NT * 4).rearrange("p (t m) -> p t m", t=NT)
        y_out_v = [O[1][0, t * P:(t + 1) * P, :] for t in range(NT_S)] + [O[0][0, t * P:(t + 1) * P, :] for t in range(NT_P)]

        def sp_phase7(sp):
            sp.dma_start(f_row, A["final_row"].partition_broadcast(P)).then_inc(sem("final_in"), 16)
            for t in range(NT):
                sp.wait_ge(sem("final_ready"), t + 1)
                sp.dma_start(y_out_v[t], yo[t % 2]).then_inc(sem(f"final_out{t % 2}"), 16)
            sp.wait_ge(sem("final_out0"), 16 * NT // 2)
            sp.wait_ge(sem("final_out1"), 16 * NT // 2)

        def pool_phase7(pool):
            for t in range(NT):
                if t >= 2:
                    pool.wait_ge(sem("joined"), t - 1)
                for k in range(2):
                    nc.gpsimd.indirect_dma_start(ya[t % 2][k], None, y_dram,
                                                 bass.IndirectOffsetOnAxis(ap=pos_i.bitcast(u32)[:, t, k:k + 1], axis=0)).then_inc(sem(f"rows_in{t % 2}"), 16)

        def act_phase7(act):
            own = Own(act, sem("act_own7"))

            def first_row(t):
                act.wait_ge(sem(f"rows_in{t % 2}"), 32 * (t // 2 + 1))
                a = ya[t % 2][0]
                nc.scalar.mul(a, a, wts[:, t, 0:1]).then_inc(sem("first_scaled"), 1)

            first_row(0)
            first_row(1)
            for t in range(NT):
                act.wait_ge(sem("joined"), t + 1)
                if t:
                    own.wait(own.n)
                own.link(nc.scalar.activation(sq7, x2[:, t, :], ACT.Square, scale=1.0 / 32.0, accum_out=stat7[:, t, 0:1]))
                own.done(nc.scalar.activation(stat7[:, t, 1:2], stat7[:, t, 0:1], ACT.Sqrt, bias=eps[:, 0:1]))
                if t + 2 < NT:
                    first_row(t + 2)

        def dve_phase7(dve):
            own = Own(dve, sem("dve_own7"))
            dve.wait_ge(sem("final_in"), 16)

            def join(t):
                a, b = ya[t % 2]
                dve.wait_ge(sem(f"rows_in{t % 2}"), 32 * (t // 2 + 1))
                dve.wait_ge(sem("first_scaled"), t + 1)
                own.link(nc.vector.scalar_tensor_tensor(a, b, wts[:, t, 1:2], a, ALU.mult, ALU.add))
                nc.vector.tensor_tensor(a, a, g2_row[:, group(t), :], ALU.mult).then_inc(sem("joined0"), 1)
                dve.wait_ge(sem("joined0"), t + 1)
                nc.vector.tensor_tensor(x2[:, t, :], x2[:, t, :], a, ALU.add).then_inc(sem("joined"), 1)

            def norm(t):
                dve.wait_ge(sem("act_own7"), 2 * t + 2)
                if t >= 2:
                    dve.wait_ge(sem(f"final_out{t % 2}"), 16 * (t // 2))
                own.link(nc.vector.reciprocal(stat7[:, t, 2:3], stat7[:, t, 1:2]))
                nc.vector.scalar_tensor_tensor(yo[t % 2], x2[:, t, :], stat7[:, t, 2:3], f_row, ALU.mult, ALU.mult).then_inc(sem("final_ready"), 1)

            for t in range(NT):
                join(t)
                if t:
                    norm(t - 1)
            norm(NT - 1)

        def run_phase(sp=None, pool=None, act=None, dve=None, pe=None):
            with nc.Block() as block:
                for engine, own_program in ((block.sync, sp), (block.gpsimd, pool), (block.scalar, act), (block.vector, dve), (block.tensor, pe)):
                    if own_program is not None:
                        engine(own_program)
            nc.clear_and_free_semaphores(list(sems.values()))
            sems.clear()
            nc.all_engine_barrier()

        for programs in ((sp_phase1, pool_phase1, act_phase1, dve_phase1, pe_phase1),
                         (sp_phase2, pool_phase2, act_phase2, dve_phase2, pe_phase2),
                         (sp_phase3, pool_phase3, act_phase3, dve_phase3, pe_phase3),
                         (sp_phase4, pool_phase4, act_phase4, dve_phase4, pe_phase4),
                         (sp_phase5, pool_phase5, act_phase5, dve_phase5, pe_phase5),
                         (sp_phase6, pool_phase6, act_phase6, dve_phase6, pe_phase6),
                         (sp_phase7, pool_phase7, act_phase7, dve_phase7, None))[:upto]:
            run_phase(*programs)


def layout(inputs):
    a = {k: np.ascontiguousarray(np.asarray(v)) for k, v in inputs.items()}
    a["c_cols"] = np.ascontiguousarray(np.stack([a.pop("c_sample")[0], a.pop("c_prompt")[0]], -1)
                                       .reshape(KD, P, 2).transpose(1, 0, 2))
    a["mu"] = np.ascontiguousarray(a.pop("rwkv_mu")[0].reshape(2, NZ, P).transpose(2, 1, 0))
    rpb = a.pop("na_rpb")[0]
    pad = np.pad(rpb, ((0, 0), (0, 0), (16, 16)))
    i, m = np.arange(8)[:, None, None, None], np.arange(8)[None, None, :, None]
    qc, kc = np.arange(QB)[None, :, None, None], np.arange(KB)[None, None, None, :]
    bias = np.stack([pad[:, m - i + 7, kc + off - qc + 15 + 16] for off in (0, -8, -16)])
    a["bias"] = np.ascontiguousarray(bias.reshape(3, NH, P, 8 * KB).transpose(0, 2, 1, 3))
    a["router_w"] = np.ascontiguousarray(np.concatenate([a.pop("router_g_w")[0], a.pop("router_e_w")[0]], 1)
                                         .reshape(KD, P, NG + NE).transpose(1, 0, 2))
    a["router_b"] = np.concatenate([a.pop("router_g_b")[0], a.pop("router_e_b")[0]])
    a["final_row"] = a.pop("final_g")
    a.update(constants())
    return a


def program(nc, inputs, upto=7):
    arrays = {f"in_{k}": v for k, v in layout(inputs).items()}
    A = {k[3:]: nc.dram_tensor(k, v.shape, mybir.dt.from_np(v.dtype), kind="ExternalInput").ap() for k, v in arrays.items()}
    O = [nc.dram_tensor("y_prompt", (1, T_P, D), f32, kind="ExternalOutput").ap(),
         nc.dram_tensor("y_sample", (1, T_S, D), f32, kind="ExternalOutput").ap()]
    build(nc, A, O, upto)
    return arrays


def kernel(**inputs):
    import concourse.bacc as bacc
    from concourse.bass_utils import run_bass_kernel_spmd

    nc = bacc.Bacc("TRN2", target_bir_lowering=False, num_devices=1)
    arrays = program(nc, inputs)
    r = run_bass_kernel_spmd(nc, [arrays], core_ids=[0])
    return r.results[0]["y_prompt"], r.results[0]["y_sample"]
```
